# Optimizing a Trainium2 kernel written in Bass

```python
import jax, jax.numpy as jnp
from jax import lax
import numpy as np
import math

D_MODEL = 1024
BATCH = 1
SEQ = 256
DEPTH = 2

D_MIX = D_MODEL
CONV_W = D_MIX // 4
CONV_K = 31
POOL_W = D_MIX // 4
POOL_WINDOWS = (2, 4, 8, 16)
POOL_G = 4
POOL_GW = POOL_W // POOL_G
HEAD_DIM = 64
ATTN_W = D_MIX // 2
N_HEADS = ATTN_W // HEAD_DIM
IDX_HEADS = 4
IDX_DIM = 64
TOPK_MAX = 256
Q_BLOCK = 128
ROPE_THETA = 10000.0
PLE_DIM = 256
EPS = 1e-6
SPLITS = (CONV_W, CONV_W, CONV_W,
          POOL_W, POOL_W,
          ATTN_W, ATTN_W, ATTN_W, ATTN_W,
          IDX_HEADS * IDX_DIM, IDX_DIM, IDX_HEADS)
D_IN = 3 * CONV_W + 2 * POOL_W + 4 * ATTN_W + IDX_HEADS * IDX_DIM + IDX_DIM + IDX_HEADS


def rmsnorm(x, g):
    xf = x.astype(jnp.float32)
    y = xf * lax.rsqrt(jnp.mean(xf * xf, axis=-1, keepdims=True) + EPS)
    return (y * g.astype(jnp.float32)).astype(x.dtype)

def layernorm(x, g, b):
    xf = x.astype(jnp.float32)
    mu = jnp.mean(xf, axis=-1, keepdims=True)
    xc = xf - mu
    y = xc * lax.rsqrt(jnp.mean(xc * xc, axis=-1, keepdims=True) + EPS)
    return (y * g.astype(jnp.float32) + b.astype(jnp.float32)).astype(x.dtype)

def rope(x, pos):
    half = x.shape[-1] // 2
    inv = ROPE_THETA ** (-jnp.arange(half, dtype=jnp.float32) / half)
    ang = pos.astype(jnp.float32)[:, None] * inv[None, :]
    cos = jnp.cos(ang)[None, :, None, :]
    sin = jnp.sin(ang)[None, :, None, :]
    xf = x.astype(jnp.float32)
    x1, x2 = xf[..., :half], xf[..., half:]
    return jnp.concatenate([x1 * cos - x2 * sin, x2 * cos + x1 * sin], axis=-1).astype(x.dtype)

def conv_module(val, glu, dw_w, dw_b, ln_g, ln_b, pw_w, pw_b):
    u = val * jax.nn.sigmoid(glu)
    u = lax.conv_general_dilated(u, dw_w[:, None, :], window_strides=(1,),
                                 padding=[(CONV_K - 1, 0)],
                                 dimension_numbers=('NWC', 'WIO', 'NWC'),
                                 feature_group_count=CONV_W) + dw_b
    u = jax.nn.silu(layernorm(u, ln_g, ln_b))
    return u @ pw_w + pw_b

def pool_mixer(u, w, b, scale):
    B, S, _ = u.shape
    ug = u.reshape(B, S, POOL_G, POOL_GW)
    t = jnp.arange(S)
    outs = []
    for g, win in enumerate(POOL_WINDOWS):
        xg = ug[:, :, g].astype(jnp.float32)
        cs = jnp.cumsum(xg, axis=1)
        lag = jnp.pad(cs, ((0, 0), (win, 0), (0, 0)))[:, :S]
        cnt = jnp.minimum(t + 1, win).astype(jnp.float32)[None, :, None]
        outs.append((cs - lag) / cnt - xg)
    d = jnp.stack(outs, axis=2).astype(u.dtype)
    y = jnp.einsum('bsgc,gcd->bsgd', d, w).reshape(B, S, POOL_W) + b
    return y * scale

def sparse_attention(q, k, v, qi, ki, wi):
    B, S, H, Dh = q.shape
    L = k.shape[1]
    topk = min(TOPK_MAX, L // 4)
    nb = S // Q_BLOCK
    key_pos = jnp.arange(L)
    kf = ki.astype(jnp.float32)

    def to_blocks(a):
        return a.reshape((B, nb, Q_BLOCK) + a.shape[2:]).swapaxes(0, 1)

    def gather(a, i):
        return a[i]

    def block(args):
        qb, qib, wib, start = args
        qpos = start + jnp.arange(Q_BLOCK)
        causal = key_pos[None, :] <= qpos[:, None]
        s = jnp.einsum('bqhd,bsd->bqhs', qib.astype(jnp.float32), kf) * (IDX_DIM ** -0.5)
        score = jnp.einsum('bqh,bqhs->bqs', wib.astype(jnp.float32), jax.nn.relu(s))
        score = jnp.where(causal[None], score, -jnp.inf)
        _, idx = lax.top_k(score, topk)
        kg = jax.vmap(gather)(k, idx)
        vg = jax.vmap(gather)(v, idx)
        logits = jnp.einsum('bqhd,bqkhd->bhqk', qb.astype(jnp.float32),
                            kg.astype(jnp.float32)) * (HEAD_DIM ** -0.5)
        valid = idx <= qpos[None, :, None]
        logits = jnp.where(valid[:, None], logits, -jnp.inf)
        pr = jax.nn.softmax(logits, axis=-1)
        o = jnp.einsum('bhqk,bqkhd->bqhd', pr, vg.astype(jnp.float32))
        return o.astype(q.dtype)

    starts = jnp.arange(nb) * Q_BLOCK
    o = lax.map(block, (to_blocks(q), to_blocks(qi), to_blocks(wi), starts))
    return o.swapaxes(0, 1).reshape(B, S, H * Dh)

def first_inputs(seed: int = 0) -> dict:
    key = jax.random.key(seed)
    ks = jax.random.split(key, 20)
    f32 = jnp.float32

    def nrm(k, shape, scale):
        return jax.random.normal(k, shape, f32) * scale

    return {
        'x': nrm(ks[0], (BATCH, SEQ, D_MODEL), 1.0),
        'p': nrm(ks[1], (DEPTH, BATCH, SEQ, PLE_DIM), 1.0),
        'norm_g': 1.0 + nrm(ks[2], (DEPTH, D_MODEL), 0.1),
        'w_in': nrm(ks[3], (DEPTH, D_MODEL, D_IN), D_MODEL ** -0.5),
        'b_in': nrm(ks[4], (DEPTH, D_IN), 0.02),
        'conv_dw_w': nrm(ks[5], (DEPTH, CONV_K, CONV_W), CONV_K ** -0.5),
        'conv_dw_b': nrm(ks[6], (DEPTH, CONV_W), 0.02),
        'conv_ln_g': 1.0 + nrm(ks[7], (DEPTH, CONV_W), 0.1),
        'conv_ln_b': nrm(ks[8], (DEPTH, CONV_W), 0.02),
        'conv_pw_w': nrm(ks[9], (DEPTH, CONV_W, CONV_W), CONV_W ** -0.5),
        'conv_pw_b': nrm(ks[10], (DEPTH, CONV_W), 0.02),
        'pool_w': nrm(ks[11], (DEPTH, POOL_G, POOL_GW, POOL_GW), POOL_GW ** -0.5),
        'pool_b': nrm(ks[12], (DEPTH, POOL_W), 0.02),
        'pool_scale': 1.0 + nrm(ks[13], (DEPTH, POOL_W), 0.1),
        'w_out': nrm(ks[14], (DEPTH, D_MIX, D_MODEL), D_MIX ** -0.5),
        'ple_w': nrm(ks[15], (DEPTH, PLE_DIM, D_MODEL), PLE_DIM ** -0.5),
        'ple_gate_w': nrm(ks[16], (DEPTH, D_MODEL, D_MODEL), D_MODEL ** -0.5),
        'final_norm_g': 1.0 + nrm(ks[17], (D_MODEL,), 0.1),
    }

def first_block(x, p, norm_g, w_in, b_in, conv_dw_w, conv_dw_b, conv_ln_g, conv_ln_b,
              conv_pw_w, conv_pw_b, pool_w, pool_b, pool_scale, w_out, ple_w,
              ple_gate_w, final_norm_g):
    B, S, _ = x.shape
    pos = jnp.arange(S)
    cut = [int(c) for c in np.cumsum(SPLITS)[:-1]]
    h = x
    for i in range(DEPTH):
        n = rmsnorm(h, norm_g[i])
        z = n @ w_in[i] + b_in[i]
        (c_val, c_glu, c_gate, p_in, p_gate, q, k, v, a_gate,
         qi, ki, wi) = jnp.split(z, cut, axis=-1)
        ya = conv_module(c_val, c_glu, conv_dw_w[i], conv_dw_b[i], conv_ln_g[i],
                         conv_ln_b[i], conv_pw_w[i], conv_pw_b[i]) * jax.nn.silu(c_gate)
        yb = pool_mixer(p_in, pool_w[i], pool_b[i], pool_scale[i]) * jax.nn.silu(p_gate)
        q = rope(q.reshape(B, S, N_HEADS, HEAD_DIM), pos)
        k = rope(k.reshape(B, S, N_HEADS, HEAD_DIM), pos)
        v = v.reshape(B, S, N_HEADS, HEAD_DIM)
        qi = rope(qi.reshape(B, S, IDX_HEADS, IDX_DIM), pos)
        ki = rope(ki[:, :, None, :], pos)[:, :, 0, :]
        yc = sparse_attention(q, k, v, qi, ki, wi) * jax.nn.silu(a_gate)
        h = h + jnp.concatenate([ya, yb, yc], axis=-1) @ w_out[i]
        h = h + (p[i] @ ple_w[i]) * jax.nn.sigmoid(h @ ple_gate_w[i])
    return rmsnorm(h, final_norm_g)


CTX_LEN = 256
GRID_W = 64
NEG_INF = -1e30

GLA_HEADS = 6
GLA_DK = 32
GLA_DV = 64
GLA_LOWRANK = 16
GLA_TAU = 16.0
GLA_CHUNK = 16
ROPE_BASE = 10000.0
SC_WIDTH = 256
SC_GROUPS = 4
NA_HEADS = 6
NA_DH = 64
NA_WIN_ROWS = 8
NA_WIN_COLS = 16
FFN_DIM = 2816

GLA_QK = GLA_HEADS * GLA_DK
GLA_V = GLA_HEADS * GLA_DV
NA_W = NA_HEADS * NA_DH
MIX_WIDTH = GLA_V + SC_WIDTH + NA_W
IN_SPLIT = (GLA_QK, GLA_QK, GLA_V, GLA_LOWRANK, GLA_LOWRANK, GLA_V,
            SC_WIDTH, SC_WIDTH, SC_WIDTH, NA_W, NA_W, NA_W)
IN_WIDTH = 2 * GLA_QK + 2 * GLA_V + 2 * GLA_LOWRANK + 3 * SC_WIDTH + 3 * NA_W


def rmsnorm_2(t, g):
    tf = t.astype(jnp.float32)
    y = tf * lax.rsqrt(jnp.mean(tf * tf, axis=-1, keepdims=True) + EPS)
    return (y * g.astype(jnp.float32)).astype(t.dtype)

def modulate(t, shift, scale):
    return t * (1 + scale) + shift

def split_cols(u):
    parts, start = [], 0
    for size in IN_SPLIT:
        parts.append(u[..., start:start + size])
        start += size
    return parts

def dwconv3(t, w, b):
    tp = jnp.pad(t, ((0, 0), (1, 1), (0, 0)))
    return tp[:, :-2] * w[0] + tp[:, 1:-1] * w[1] + tp[:, 2:] * w[2] + b

def axial_rope(n_tokens, dim):
    t = jnp.arange(n_tokens)
    n_freq = dim // 4
    inv_freq = ROPE_BASE ** (-jnp.arange(n_freq, dtype=jnp.float32) / n_freq)
    row = (t // GRID_W).astype(jnp.float32)[:, None] * inv_freq
    col = (t % GRID_W).astype(jnp.float32)[:, None] * inv_freq
    ang = jnp.concatenate([row, col], axis=-1)
    return jnp.cos(ang)[None, :, None, :], jnp.sin(ang)[None, :, None, :]

def apply_rope(t, cos, sin):
    t1, t2 = t[..., 0::2], t[..., 1::2]
    return jnp.stack([t1 * cos - t2 * sin, t1 * sin + t2 * cos], axis=-1).reshape(t.shape)

def gla_chunked(q, k, v, g, s0):
    bsz, n_tok, h, dk = q.shape
    dv = v.shape[-1]
    n_chunks = n_tok // GLA_CHUNK
    rs = lambda t: t.reshape(bsz, n_chunks, GLA_CHUNK, h, t.shape[-1])
    q, k, v, g = rs(q), rs(k), rs(v), rs(g)
    b = jnp.cumsum(g, axis=2)
    b_last = b[:, :, -1:]
    q_dec = q * jnp.exp(b)
    k_inv = k * jnp.exp(-b)
    k_end = k * jnp.exp(b_last - b)
    causal = jnp.tril(jnp.ones((GLA_CHUNK, GLA_CHUNK), dtype=bool))
    a = jnp.einsum('bnihk,bnjhk->bnhij', q_dec, k_inv)
    a = jnp.where(causal, a, 0.0)
    o_intra = jnp.einsum('bnhij,bnjhv->bnihv', a, v)

    def step(s, xs):
        qd, ke, vv, dec = xs
        o = jnp.einsum('bihk,bhkv->bihv', qd, s)
        s = s * dec[..., None] + jnp.einsum('bjhk,bjhv->bhkv', ke, vv)
        return s, o

    xs = (jnp.moveaxis(q_dec, 1, 0), jnp.moveaxis(k_end, 1, 0), jnp.moveaxis(v, 1, 0),
          jnp.moveaxis(jnp.exp(b_last[:, :, 0]), 1, 0))
    s_final, o_inter = lax.scan(step, s0, xs)
    o = o_intra + jnp.moveaxis(o_inter, 0, 1)
    return o.reshape(bsz, n_tok, h, dv), s_final

def gla_prep(q, k, v, glr_f, glr_b, wg2_fw, bg_fw, wg2_bw, bg_bw, rope):
    bsz, n_tok, _ = q.shape
    heads = lambda t, d: t.astype(jnp.float32).reshape(bsz, n_tok, GLA_HEADS, d)
    q = heads(q, GLA_DK) * (GLA_DK ** -0.5)
    k = heads(k, GLA_DK)
    v = heads(v, GLA_DV)
    if rope is not None:
        q = apply_rope(q, rope[0], rope[1])
        k = apply_rope(k, rope[0], rope[1])
    g_f = heads(jax.nn.log_sigmoid((glr_f @ wg2_fw + bg_fw).astype(jnp.float32)), GLA_DK) / GLA_TAU
    g_b = heads(jax.nn.log_sigmoid((glr_b @ wg2_bw + bg_bw).astype(jnp.float32)), GLA_DK) / GLA_TAU
    return q, k, v, g_f, g_b

def gla_output(o, r, norm_g):
    of = o * lax.rsqrt(jnp.mean(o * o, axis=-1, keepdims=True) + EPS) * norm_g.astype(jnp.float32)
    bsz, n_tok = o.shape[:2]
    return (of.reshape(bsz, n_tok, GLA_V) * jax.nn.silu(r.astype(jnp.float32))).astype(r.dtype)

def gla_mixer(lat, cpar, rope, wg2_fw, bg_fw, wg2_bw, bg_bw, norm_g, need_ctx_out):
    flip = lambda t: jnp.flip(t, axis=1)
    qc, kc, vc, gfc, gbc = gla_prep(*cpar[:5], wg2_fw, bg_fw, wg2_bw, bg_bw, None)
    ql, kl, vl, gfl, gbl = gla_prep(*lat[:5], wg2_fw, bg_fw, wg2_bw, bg_bw, rope)
    s0 = jnp.zeros((qc.shape[0], GLA_HEADS, GLA_DK, GLA_DV), jnp.float32)
    oc_f, sc_f = gla_chunked(qc, kc, vc, gfc, s0)
    oc_b, sc_b = gla_chunked(flip(qc), flip(kc), flip(vc), flip(gbc), s0)
    ol_f, _ = gla_chunked(ql, kl, vl, gfl, sc_f)
    ol_b, _ = gla_chunked(flip(ql), flip(kl), flip(vl), flip(gbl), sc_b)
    out_lat = gla_output(ol_f + flip(ol_b), lat[5], norm_g)
    out_ctx = gla_output(oc_f + flip(oc_b), cpar[5], norm_g) if need_ctx_out else None
    return out_lat, out_ctx

def short_conv(b_gate, c_gate, xh, w, bias):
    return b_gate * dwconv3(c_gate * xh, w, bias)

def neighbourhood_attention(q, k, v, k_ctx, v_ctx, rpb):
    bsz, n_tok, _ = q.shape
    rows = n_tok // GRID_W
    kh = min(NA_WIN_ROWS, rows)
    kw = NA_WIN_COLS
    grid = lambda t: t.reshape(bsz, rows, GRID_W, NA_HEADS, NA_DH)
    qg = grid(q.astype(jnp.float32) * (NA_DH ** -0.5))
    kg, vg = grid(k), grid(v)
    kc = k_ctx.reshape(bsz, -1, NA_HEADS, NA_DH).astype(jnp.float32)
    vc = v_ctx.reshape(bsz, -1, NA_HEADS, NA_DH).astype(jnp.float32)
    col = jnp.arange(GRID_W)
    col_start = jnp.clip(col - kw // 2, 0, GRID_W - kw)
    col_mask = (col[None, :] >= col_start[:, None]) & (col[None, :] < col_start[:, None] + kw)
    dc_idx = jnp.clip(col[None, :] - col[:, None] + NA_WIN_COLS - 1, 0, 2 * NA_WIN_COLS - 2)
    rpb_cols = jnp.take(rpb.astype(jnp.float32), dc_idx, axis=2)

    def row_block(r):
        rs = jnp.clip(r - kh // 2, 0, rows - kh)
        q_r = lax.dynamic_index_in_dim(qg, r, axis=1, keepdims=False)
        k_band = lax.dynamic_slice_in_dim(kg, rs, kh, axis=1).astype(jnp.float32)
        v_band = lax.dynamic_slice_in_dim(vg, rs, kh, axis=1).astype(jnp.float32)
        dr_idx = rs + jnp.arange(kh) - r + NA_WIN_ROWS - 1
        bias = jnp.take(rpb_cols, dr_idx, axis=1)
        s_loc = jnp.einsum('bqhd,bikhd->bhqik', q_r, k_band) + jnp.transpose(bias, (0, 2, 1, 3))[None]
        s_loc = jnp.where(col_mask[None, None, :, None, :], s_loc, NEG_INF)
        s_ctx = jnp.einsum('bqhd,bchd->bhqc', q_r, kc)
        s = jnp.concatenate([s_loc.reshape(bsz, NA_HEADS, GRID_W, kh * GRID_W), s_ctx], axis=-1)
        p = jax.nn.softmax(s, axis=-1)
        p_loc = p[..., :kh * GRID_W].reshape(bsz, NA_HEADS, GRID_W, kh, GRID_W)
        p_ctx = p[..., kh * GRID_W:]
        o = jnp.einsum('bhqik,bikhd->bqhd', p_loc, v_band) + jnp.einsum('bhqc,bchd->bqhd', p_ctx, vc)
        return o.astype(q.dtype)

    out = lax.map(row_block, jnp.arange(rows))
    return jnp.moveaxis(out, 0, 1).reshape(bsz, n_tok, NA_W)

def context_attention(q, k, v):
    bsz, n_tok, _ = q.shape
    hs = lambda t: t.astype(jnp.float32).reshape(bsz, n_tok, NA_HEADS, NA_DH)
    s = jnp.einsum('bqhd,bkhd->bhqk', hs(q) * (NA_DH ** -0.5), hs(k))
    o = jnp.einsum('bhqk,bkhd->bqhd', jax.nn.softmax(s, axis=-1), hs(v))
    return o.reshape(bsz, n_tok, NA_W).astype(q.dtype)

def conv_ffn(h, w_up, cw, cb, w_down):
    u = dwconv3(h @ w_up, cw, cb)
    a, b = jnp.split(u, 2, axis=-1)
    return (jax.nn.silu(a) * b) @ w_down

def second_inputs(seed: int = 0) -> dict:
    key = jax.random.key(seed)
    ks = jax.random.split(key, 24)
    nrm = lambda k, shape, s: jax.random.normal(k, shape, jnp.float32) * s
    return {
        "x": nrm(ks[0], (BATCH, SEQ, D_MODEL), 1.0),
        "c": nrm(ks[1], (BATCH, D_MODEL), 1.0),
        "ctx": nrm(ks[2], (BATCH, CTX_LEN, D_MODEL), 1.0),
        "c_ctx": nrm(ks[3], (D_MODEL,), 1.0),
        "w_ada": nrm(ks[4], (DEPTH, D_MODEL, 6 * D_MODEL), 0.5 * D_MODEL ** -0.5),
        "b_ada": nrm(ks[5], (DEPTH, 6 * D_MODEL), 0.02),
        "norm_mix_g": 1.0 + nrm(ks[6], (DEPTH, D_MODEL), 0.05),
        "norm_ffn_g": 1.0 + nrm(ks[7], (DEPTH, D_MODEL), 0.05),
        "w_in": nrm(ks[8], (DEPTH, D_MODEL, IN_WIDTH), D_MODEL ** -0.5),
        "gla_wg2_fw": nrm(ks[9], (DEPTH, GLA_LOWRANK, GLA_QK), GLA_LOWRANK ** -0.5),
        "gla_bg_fw": nrm(ks[10], (DEPTH, GLA_QK), 0.02),
        "gla_wg2_bw": nrm(ks[11], (DEPTH, GLA_LOWRANK, GLA_QK), GLA_LOWRANK ** -0.5),
        "gla_bg_bw": nrm(ks[12], (DEPTH, GLA_QK), 0.02),
        "gla_norm_g": 1.0 + nrm(ks[13], (DEPTH, GLA_DV), 0.05),
        "sc_conv_w": nrm(ks[14], (DEPTH, 3, SC_WIDTH), 3 ** -0.5),
        "sc_conv_b": nrm(ks[15], (DEPTH, SC_WIDTH), 0.02),
        "na_rpb": nrm(ks[16], (DEPTH, NA_HEADS, 2 * NA_WIN_ROWS - 1, 2 * NA_WIN_COLS - 1), 0.02),
        "w_out": nrm(ks[17], (DEPTH, MIX_WIDTH, D_MODEL), MIX_WIDTH ** -0.5),
        "ffn_w_up": nrm(ks[18], (DEPTH, D_MODEL, 2 * FFN_DIM), D_MODEL ** -0.5),
        "ffn_conv_w": nrm(ks[19], (DEPTH, 3, 2 * FFN_DIM), 3 ** -0.5),
        "ffn_conv_b": nrm(ks[20], (DEPTH, 2 * FFN_DIM), 0.02),
        "ffn_w_down": nrm(ks[21], (DEPTH, FFN_DIM, D_MODEL), FFN_DIM ** -0.5),
        "final_norm_g": 1.0 + nrm(ks[22], (D_MODEL,), 0.05),
    }

def second_block(x, c, ctx, c_ctx, w_ada, b_ada, norm_mix_g, norm_ffn_g, w_in, gla_wg2_fw, gla_bg_fw,
              gla_wg2_bw, gla_bg_bw, gla_norm_g, sc_conv_w, sc_conv_b, na_rpb, w_out, ffn_w_up,
              ffn_conv_w, ffn_conv_b, ffn_w_down, final_norm_g):
    n_lat = x.shape[1]
    rope = axial_rope(n_lat, GLA_DK)
    xc = ctx
    for layer in range(DEPTH):
        update_ctx = layer < DEPTH - 1
        mod = jax.nn.silu(c) @ w_ada[layer] + b_ada[layer]
        sh1, sc1, g1, sh2, sc2, g2 = jnp.split(mod[:, None, :], 6, axis=-1)
        modc = jax.nn.silu(c_ctx) @ w_ada[layer] + b_ada[layer]
        sh1c, sc1c, g1c, sh2c, sc2c, g2c = jnp.split(modc, 6, axis=-1)

        u = modulate(rmsnorm_2(x, norm_mix_g[layer]), sh1, sc1) @ w_in[layer]
        uc = modulate(rmsnorm_2(xc, norm_mix_g[layer]), sh1c, sc1c) @ w_in[layer]
        lat = split_cols(u)
        cpar = split_cols(uc)
        gla_lat, gla_ctx = gla_mixer(lat[:6], cpar[:6], rope, gla_wg2_fw[layer], gla_bg_fw[layer],
                                     gla_wg2_bw[layer], gla_bg_bw[layer], gla_norm_g[layer], update_ctx)
        sc_lat = short_conv(lat[6], lat[7], lat[8], sc_conv_w[layer], sc_conv_b[layer])
        na_lat = neighbourhood_attention(lat[9], lat[10], lat[11], cpar[10], cpar[11], na_rpb[layer])
        x = x + g1 * (jnp.concatenate([gla_lat, sc_lat, na_lat], axis=-1) @ w_out[layer])
        h = modulate(rmsnorm_2(x, norm_ffn_g[layer]), sh2, sc2)
        x = x + g2 * conv_ffn(h, ffn_w_up[layer], ffn_conv_w[layer], ffn_conv_b[layer], ffn_w_down[layer])

        if update_ctx:
            sc_ctx = short_conv(cpar[6], cpar[7], cpar[8], sc_conv_w[layer], sc_conv_b[layer])
            na_ctx = context_attention(cpar[9], cpar[10], cpar[11])
            xc = xc + g1c * (jnp.concatenate([gla_ctx, sc_ctx, na_ctx], axis=-1) @ w_out[layer])
            hc = modulate(rmsnorm_2(xc, norm_ffn_g[layer]), sh2c, sc2c)
            xc = xc + g2c * conv_ffn(hc, ffn_w_up[layer], ffn_conv_w[layer], ffn_conv_b[layer],
                                     ffn_w_down[layer])
    return rmsnorm_2(x, final_norm_g)


def setup_inputs(seed=0):
    out = dict(first_inputs(seed))
    for name, value in second_inputs(seed + 1).items():
        if name != "x":
            out[name + "_2"] = value
    return out


def reference(
    x, p, norm_g, w_in, b_in, conv_dw_w, conv_dw_b, conv_ln_g, conv_ln_b, conv_pw_w, conv_pw_b,
    pool_w, pool_b, pool_scale, w_out, ple_w, ple_gate_w, final_norm_g, c_2, ctx_2, c_ctx_2,
    w_ada_2, b_ada_2, norm_mix_g_2, norm_ffn_g_2, w_in_2, gla_wg2_fw_2, gla_bg_fw_2,
    gla_wg2_bw_2, gla_bg_bw_2, gla_norm_g_2, sc_conv_w_2, sc_conv_b_2, na_rpb_2, w_out_2,
    ffn_w_up_2, ffn_conv_w_2, ffn_conv_b_2, ffn_w_down_2, final_norm_g_2,
):
    x = first_block(
        x, p, norm_g, w_in, b_in, conv_dw_w, conv_dw_b, conv_ln_g, conv_ln_b, conv_pw_w,
        conv_pw_b, pool_w, pool_b, pool_scale, w_out, ple_w, ple_gate_w, final_norm_g,
    )
    return second_block(
        x, c_2, ctx_2, c_ctx_2, w_ada_2, b_ada_2, norm_mix_g_2, norm_ffn_g_2, w_in_2,
        gla_wg2_fw_2, gla_bg_fw_2, gla_wg2_bw_2, gla_bg_bw_2, gla_norm_g_2, sc_conv_w_2,
        sc_conv_b_2, na_rpb_2, w_out_2, ffn_w_up_2, ffn_conv_w_2, ffn_conv_b_2, ffn_w_down_2,
        final_norm_g_2,
    )


_drawn_inputs = setup_inputs


def setup_inputs(seed=0):
    import zlib

    import numpy as np

    out = dict(_drawn_inputs(seed))
    spreads = {}
    factors = {'conv_dw_b': 4.73,
     'conv_ln_b': 8.0,
     'conv_pw_b': 5.814,
     'pool_b': 6.271,
     'gla_wg2_fw_2': 2.916,
     'gla_bg_fw_2': 8.0,
     'gla_wg2_bw_2': 2.872,
     'gla_bg_bw_2': 8.0,
     'gla_norm_g_2': 6.386,
     'sc_conv_b_2': 8.0,
     'na_rpb_2': 64.0,
     'ffn_conv_b_2': 7.119,
     'norm_ffn_g_2': 2.962}
    for name, (base, spread) in spreads.items():
        noise = np.random.default_rng([zlib.crc32(name.encode()), seed]).standard_normal(out[name].shape)
        drawn = base * np.exp(spread * noise) if base else spread * noise
        out[name] = __import__('jax').numpy.asarray(drawn.astype(out[name].dtype))
    for name, factor in factors.items():
        out[name] = (out[name] * factor).astype(out[name].dtype)
    return out
```

```python
from contextlib import ExitStack

import numpy as np

import concourse.bass as bass
from concourse import mybir

F32 = mybir.dt.float32
F32R = mybir.dt.float32r
ALU = mybir.AluOpType
ACT = mybir.ActivationFunctionType
AX_X = mybir.AxisListType.X

P = 128
T = 256
TC = 512
TT = T // P
D = 1024
KS = D // P
DEPTH = 2
UNIT = 1024
EPS = 1e-6

CONV_W, CONV_K, POOL_W = 256, 31, 256
POOL_WINDOWS = (2, 4, 8, 16)
HD, NH1 = 64, 8
IDXH = 4
TOPK = T // 4
PLE = 256
TILES1 = ["q"] * 4 + ["k"] * 4 + ["qi"] * 2 + ["ki", "wi"] + ["val"] * 2 + ["glu"] * 2 + \
    ["cgate"] * 2 + ["pin"] * 2 + ["pgate"] * 2 + ["agate"] * 4
Z1 = {n: TILES1.index(n) for n in TILES1}
NZ1 = len(TILES1)

GH, GDK, GDV = 6, 32, 64
NAH = 6
FFN = 2816
FT = FFN // P
CH = 32
NCH = P // CH
CAP = 80.0
TILES2 = ["gqa", "gka", "gqk", "glr"] + ["nk"] * 3 + ["nq"] * 3 + ["r"] * 3 + ["scb"] * 2 + \
    ["scc"] * 2 + ["scx"] * 2
Z2 = {n: TILES2.index(n) for n in TILES2}
NZ2 = len(TILES2)
LAT_ONLY = ("nq", "r", "scb", "scc", "scx")
VW = 384

def param_columns():
    cols, at = {}, 0
    def add(name, n):
        nonlocal at
        cols[name] = at
        at += n
    for l in range(DEPTH):
        for name, n in (("norm", KS), ("bin", NZ1), ("dww", 2 * CONV_K), ("dwb", 2), ("lng", 2), ("lnb", 2),
                        ("pwb", 2), ("poolb", 2), ("pools", 2)):
            add(f"{name}{l}", n)
    add("fin1", KS)
    for l in range(DEPTH):
        for name, n in (("nmix", KS), ("nffn", KS), ("bada", 48), ("glag", 1), ("scw", 6), ("scbias", 2),
                        ("fw", 3 * 2 * FT), ("fb", 2 * FT)):
            add(f"{name}{l}", n)
    add("fin2", KS)
    add("cvec", 2 * KS)
    return cols, at


PC, NPC = param_columns()

def unit_widths():
    w = []
    for _ in range(DEPTH):
        w += [UNIT] * 48
    for _ in range(DEPTH):
        w += [UNIT] * 4 + [UNIT] * NZ1 + [UNIT] * KS + [UNIT] * 2 + [UNIT] * KS
    for _ in range(DEPTH):
        w += [2 * VW] * 8 + [UNIT] * NZ2 + [UNIT] * KS + [UNIT] * 2 * FT + [UNIT, UNIT, 6 * P] * KS
    return w


WIDTHS = unit_widths()
NU = len(WIDTHS)
RAW, SPL, AHEAD = 4, 3, 2

def layout(names):
    out, at = {}, 0
    for name, n in names:
        out[name] = (at, n)
        at += n
    return out, at


CC, NCC = layout([("ident", P), ("ones", P), ("ones256", P), ("blk", P), ("comb", 2), ("glrone", 1)])
C1, NC1 = layout([("perm", P), ("cos", T), ("sin", T), ("causal", 2 * T), ("icnt", 2 * T)])
C2, NC2 = layout([("perm", P), ("cos", T), ("sin", T), ("rep", P), ("uf", T), ("ub", T),
                  ("capkf", P), ("capkb", P), ("capq", P), ("mask", 4 * P)])


def build(nc, ws, prm, cc, c1, c2, xt, ptin, mat1, bv1, wgp, nab, out):
    with ExitStack() as ctx:
        sems = {}

        def S(name):
            if name not in sems:
                sems[name] = ctx.enter_context(nc.semaphore(name))
            return sems[name]

        def sb(stack, name, shape, dt=F32):
            return stack.enter_context(nc.sbuf_tensor(name, shape, dt))

        X = sb(ctx, "X", [P, KS, TC])
        NHI = sb(ctx, "NHI", [P, KS, TC], F32R)
        NLO = sb(ctx, "NLO", [P, KS, TC], F32R)
        RAWB = sb(ctx, "RAWB", [P, RAW, UNIT])
        WHI = sb(ctx, "WHI", [P, SPL, UNIT], F32R)
        WLO = sb(ctx, "WLO", [P, SPL, UNIT], F32R)
        CST = sb(ctx, "CST", [P, NCC])
        PRM = sb(ctx, "PRM", [P, NPC])
        MOD = sb(ctx, "MOD", [P, DEPTH, 48, 2])
        GM = sb(ctx, "GM", [P, KS, 2])

        def cst(name):
            a, n = CC[name]
            return CST[:, a:a + n]

        def prm_col(name, i=0, n=1):
            a = PC[name] + i
            return PRM[:, a:a + n]

        st = ExitStack()
        CHV = sb(st, "CHV", [P, KS, P], F32R)
        CS = sb(st, "CS", [P, KS, 2])
        ROWS = sb(st, "ROWS", [4, 2, 512])
        st.close()

        st = ExitStack()
        K1 = sb(st, "K1", [P, NC1])
        Z = sb(st, "Z", [P, NZ1, T])
        V1 = sb(st, "V1", [P, TT, 512])
        BV = sb(st, "BV", [P, 512])
        M1 = sb(st, "M1", [P, 768])
        PLEH = sb(st, "PLEH", [P, 2, 2, T], F32R)
        PIN = sb(st, "PIN", [P, 2, T])
        RT = sb(st, "RT", [P, 512])
        WI = sb(st, "WI", [P, TT, IDXH])
        RL = sb(st, "RL", [P, 2, T])
        SC = sb(st, "SC", [P, TT, T])
        MB = sb(st, "MB", [P, TT, T])
        M8 = sb(st, "M8", [P, 8])
        L1 = sb(st, "L1", [P, 3, T])
        P1 = sb(st, "P1", [P, 3, T])
        PT1 = sb(st, "PT1", [P, 2, T])
        ST1 = sb(st, "ST1", [P, 3, 4])
        OB = sb(st, "OB", [P, 4, T])
        UP = sb(st, "UP", [P, 2, CONV_K - 1 + T])
        CV = sb(st, "CV", [P, 2, T])
        CT = sb(st, "CT", [P, 2, T])
        PP = sb(st, "PP", [P, 2, 16 + T])
        PS = sb(st, "PS", [P, 4, 2, 16 + T])
        PB = sb(st, "PB", [P, 2])
        GT1 = sb(st, "GT1", [P, 8, T])
        SG = sb(st, "SG", [P, 2, T])
        Y1 = sb(st, "Y1", [P, KS, T])
        MS1 = sb(st, "MS1", [P, 4, T])
        st.close()

        mix = ExitStack()
        K2 = sb(mix, "K2", [P, NC2])
        ZB = sb(mix, "ZB", [P, NZ2, TC])
        V2 = sb(mix, "V2", [P, 4, 2 * VW])
        st = ExitStack()
        WG = sb(st, "WG", [64, 192])
        GT = sb(st, "GT", [P, 4, VW])
        GTA = sb(st, "GTA", [P, 4, VW])
        KQ = sb(st, "KQ", [P, 2, TC])
        BM = sb(st, "BM", [P, 2, 6])
        EX = sb(st, "EX", [P, 1280])
        EY = sb(st, "EY", [P, 2, 1280])
        E0 = sb(st, "E0", [64, TC])
        AM = sb(st, "AM", [P, TC])
        AF = sb(st, "AF", [P, 2, 2, T])
        A0 = sb(st, "A0", [P, 2, T])
        OG = sb(st, "OG", [P, TC])
        OM = sb(st, "OM", [P, 4, TC])
        st.close()
        st = ExitStack()
        NB = sb(st, "NB", [P, 2, TT, TC])
        L2 = sb(st, "L2", [P, 3, TC])
        P2 = sb(st, "P2", [P, 3, TC])
        PT2 = sb(st, "PT2", [P, 2, TC])
        ST2 = sb(st, "ST2", [P, 3, 4])
        OY = sb(st, "OY", [P, 3, TC])
        st.close()
        mix.close()
        st = ExitStack()
        SQ2 = sb(st, "SQ2", [P, KS, TC])
        TB2 = sb(st, "TB2", [P, KS, TC])
        MS2 = sb(st, "MS2", [P, 4, TC])
        st.close()
        st = ExitStack()
        HHI = sb(st, "HHI", [P, FT, TC], F32R)
        HLO = sb(st, "HLO", [P, FT, TC], F32R)
        CF = sb(st, "CF", [P, 2, 3, TC])
        st.close()

        bank = [ctx.enter_context(nc.psum_tensor(f"bank{i}", [P, 512], F32)) for i in range(8)]

        def c1v(name):
            a, n = C1[name]
            return K1[:, a:a + n]

        def c2v(name):
            a, n = C2[name]
            return K2[:, a:a + n]

        def bc(ap, n):
            return ap.unsqueeze(1).broadcast_to([ap.shape[0], n, ap.shape[1]])

        def bl(ap, n):
            return ap.unsqueeze(2).broadcast_to([ap.shape[0], ap.shape[1], n])

        def half(h):
            return slice(64 * (h % 2), 64 * (h % 2) + 64)

        def gates4(i):
            g = GTA[:].rearrange("p a b -> p (a b)")[:, (i % 3) * 512:(i % 3 + 1) * 512]
            return g.rearrange("p (i c k) -> p i c k", i=4, c=NCH)

        def gate_part(g, i):
            s, d = i // 2, i % 2
            return g[:, 2 * s:2 * s + 2, d * 192:(d + 1) * 192]

        class Side:

            def __init__(self, eng, name):
                self.eng, self.name, self.seen, self.u, self.tile = eng, name, {}, 0, 0

            def nth(self, name, k=1):
                self.seen[name] = self.seen.get(name, 0) + k
                return self.seen[name]

            def next_tile(self):
                self.tile += 1
                return (self.tile - 1) % 4

        ITEMS1 = [(h, qt, P * (qt + 1), False) for h in range(NH1) for qt in range(TT)]

        def items2(uc):
            return [(h, qt, T if own else TC, own) for h in range(NAH) for own in ((False, True) if uc else (False,))
                    for qt in range(TT)]

        def ends_pair(it, uc=False):
            return it[0] % 2 == 1 and it[1] == TT - 1 and it[3] == uc

        SH1, SC1, G1, SH2, SC2, G2 = (KS * i for i in range(6))

        block = ctx.enter_context(nc.Block())

        @block.sync
        def _(sp):
            for u in range(NU):
                if u >= RAW:
                    sp.wait_ge(S("lo_ready"), u - RAW + 1)
                w = WIDTHS[u]
                sp.dma_start(RAWB[:, u % RAW, 0:w], ws[u, :, 0:w]).then_inc(S(f"raw{u % RAW}"), 16)
            sp.wait_ge(S("x_new"), KS * (DEPTH + 2))
            sp.dma_start(out, X[:, :, 0:T]).then_inc(S("stored"), 16)
            sp.wait_ge(S("stored"), 16)

        @block.gpsimd
        def _(pool):
            me = Side(pool, "pool")

            pool.dma_start(PRM[:], prm).then_inc(S("ld_prm"), 16)
            pool.dma_start(CST[:], cc).then_inc(S("ld_cst"), 16)
            nc.gpsimd.memset(CHV[:].bitcast(F32), 0.0).then_inc(S("ch_zero"), 1)
            pool.dma_start(X[:], xt).then_inc(S("ld_x"), 16)
            pool.wait_ge(S("mod_done"), me.nth("mod_done", DEPTH))
            pool.dma_start(K1[:], c1).then_inc(S("ld_c1"), 16)
            for l in range(DEPTH):
                if l > 0:
                    pool.wait_ge(S("x_new"), me.nth("x_new", KS))
                pool.dma_start(BV[:], bv1[l:l + 1, :].broadcast_to([P, 512])).then_inc(S("ld_p1"), 16)
                pool.dma_start(M1[:], mat1[l]).then_inc(S("ld_p1"), 16)
                pool.dma_start(PIN[:], ptin[l]).then_inc(S("ld_p1"), 16)
            pool.wait_ge(S("x_split"), me.nth("x_split", KS * DEPTH))
            pool.wait_ge(S("s_freed"), me.nth("s_freed", len(ITEMS1) * DEPTH))
            pool.wait_ge(S("y_split"), me.nth("y_split", KS * DEPTH))
            for l in range(DEPTH):
                pool.wait_ge(S("x_split"), me.nth("x_split", KS))
                pool.dma_start(K2[:], c2).then_inc(S("ld_c2"), 16)
                pool.dma_start(WG[:], wgp[l]).then_inc(S("ld_c2"), 16)
                pool.wait_ge(S("g_ready"), me.nth("g_ready", 4))
                for i in range(2 * GH):
                    h, d = i // 2, i % 2
                    if i >= 3:
                        pool.wait_ge(S("b_ready"), me.nth("b_ready"))
                    g = GT[:, :, d * 192 + h * GDK:d * 192 + (h + 1) * GDK]
                    nc.gpsimd.tensor_copy(gates4(i), g.unsqueeze(2).broadcast_to([P, 4, NCH, GDK])).then_inc(S("g4_ready"), 1)
                pool.wait_ge(S("b_ready"), me.nth("b_ready", 3))
                pool.wait_ge(S("y_split"), me.nth("y_split", 5))
                per_head = TT * (2 if l < DEPTH - 1 else 1)
                for h in range(NAH):
                    if h >= 2:
                        pool.wait_ge(S("s_freed"), me.nth("s_freed", per_head))
                    pool.dma_start(NB[:, h % 2, :, 0:T], nab[l, h]).then_inc(S(f"ld_nb{h % 2}"), 16)
                pool.wait_ge(S("s_freed"), me.nth("s_freed", 2 * per_head))
                pool.wait_ge(S("y_split"), me.nth("y_split", 3))
                pool.wait_ge(S("x_split"), me.nth("x_split", KS))

        @block.tensor
        def _(pe):
            me = Side(pe, "pe")
            held, made = {}, {}

            def read_by(b, freed):
                made[freed] = made.get(freed, 0) + 1
                held[b] = (S(freed), made[freed])

            def unit():
                u = me.u
                me.u += 1
                pe.wait_ge(S("lo_ready"), u + 1)
                return WHI[:, u % SPL, :], WLO[:, u % SPL, :]

            def fm(slabs, n, rhs, freed):
                b = me.next_tile()
                if b in held:
                    pe.wait_ge(*held[b])
                o = bank[b][:, 0:n]
                for s in range(slabs):
                    if s % 8 == 0:
                        hi, lo = unit()
                    w = slice((s % 8) * P, (s % 8 + 1) * P)
                    xh, xl = rhs(s)
                    nc.tensor.matmul(o, hi[:, w], xh, start=(s == 0), stop=False)
                    nc.tensor.matmul(o, hi[:, w], xl, start=False, stop=False)
                    ins = nc.tensor.matmul(o, lo[:, w], xh, start=False, stop=(s == slabs - 1))
                    if s % 8 == 7 and s != slabs - 1:
                        ins.then_inc(S("unit_done"), 1)
                ins.then_inc(S("unit_done"), 1)
                read_by(b, freed)

            def tm(tts, w):
                for b in range(tts):
                    if b in held:
                        pe.wait_ge(*held[b])
                for u in range(4):
                    hi, lo = unit()
                    for k in range(2):
                        s, c = 2 * u + k, slice(k * w, (k + 1) * w)
                        for t in range(tts):
                            o = bank[t][:, 0:w]
                            xh, xl = NHI[:, s, t * P:(t + 1) * P], NLO[:, s, t * P:(t + 1) * P]
                            nc.tensor.matmul(o, xh, hi[:, c], start=(s == 0), stop=False)
                            nc.tensor.matmul(o, xl, hi[:, c], start=False, stop=False)
                            ins = nc.tensor.matmul(o, xh, lo[:, c], start=False, stop=(s == 7))
                    ins.then_inc(S("unit_done"), 1)
                for b in range(tts):
                    read_by(b, "v_freed")

            def x_lat(s):
                return NHI[:, s, 0:T], NLO[:, s, 0:T]

            def x_all(s):
                return NHI[:, s, :], NLO[:, s, :]

            def stats(n, sq):
                if 4 in held:
                    pe.wait_ge(*held[4])
                for s in range(KS):
                    if s % 2 == 0:
                        pe.wait_ge(S("sq_ready"), me.nth("sq_ready"))
                    ins = nc.tensor.matmul(bank[4][:, 0:n], cst("ones"), sq[:, s, 0:n], start=(s == 0), stop=(s == KS - 1))
                ins.then_inc(S("ms_ready"), 1)
                read_by(4, "ms_eps")

            def attention(items, score, p, out, uc=False):
                n = len(items)
                for i in range(n + 3):
                    if i < n:
                        if i % 2 in held:
                            pe.wait_ge(*held[i % 2])
                        score(items[i], bank[i % 2]).then_inc(S("s_ready"), 1)
                        read_by(i % 2, "s_freed")
                    if 2 <= i < n + 2:
                        j = i - 2
                        b = 2 + j % 2
                        pe.wait_ge(S("p_ready"), me.nth("p_ready"))
                        if b in held:
                            pe.wait_ge(*held[b])
                        for k in range(items[j][2] // P):
                            ins = nc.tensor.transpose(bank[b][:, k * P:(k + 1) * P], p[:, j % 3, k * P:(k + 1) * P], cst("ident"))
                        ins.then_inc(S("pt_ready"), 1)
                        read_by(b, "pt_freed")
                    if i >= 3:
                        j = i - 3
                        h, qt, nk, own = it = items[j]
                        b = 6 + (h // 2) % 2
                        pe.wait_ge(S("pt_freed"), me.nth("pt_freed"))
                        if h % 2 == 0 and qt == 0 and not own:
                            if b in held:
                                pe.wait_ge(*held[b])
                        ins = out(j, it, bank[b])
                        if ends_pair(it, uc):
                            ins.then_inc(S("pv_done"), 1)
                            read_by(b, "o_freed")
                        else:
                            ins.then_inc(S("pv_done"), 1)

            pe.wait_ge(S("ld_cst"), 16)
            pe.wait_ge(S("ch_ready"), me.nth("ch_ready"))
            for l in range(DEPTH):
                for n in range(13):
                    if n < 12:
                        b = me.next_tile()
                        if b in held:
                            pe.wait_ge(*held[b])
                        for u in range(4):
                            hi, lo = unit()
                            for k in range(2):
                                s, c = 2 * u + k, slice(k * 512, (k + 1) * 512)
                                nc.tensor.matmul(bank[b][:], CHV[:, s, :], hi[:, c], start=(s == 0), stop=False)
                                ins = nc.tensor.matmul(bank[b][:], CHV[:, s, :], lo[:, c], start=False, stop=(s == 7))
                            if u < 3:
                                ins.then_inc(S("unit_done"), 1)
                        ins.then_inc(S("unit_done"), 1)
                        read_by(b, "rows_copied")
                    if n == 1:
                        if 6 in held:
                            pe.wait_ge(*held[6])
                    if n > 0:
                        pe.wait_ge(S("rows_copied"), me.nth("rows_copied"))
                        for j in range(4):
                            c = ((n - 1) * 4 + j) * 2
                            ins = nc.tensor.matmul(bank[6][:, c:c + 2], ROWS[0:4, (n - 1) % 2, j * P:(j + 1) * P],
                                                   cst("comb")[0:4, :], start=True, stop=True)
                        if n < 12:
                            ins.then_inc(S("rows_used"), 1)
                ins.then_inc(S("rows_used"), 1)
                read_by(6, "mod_done")

            for l in range(DEPTH):
                stats(T, Y1)
                pe.wait_ge(S("x_split"), me.nth("x_split", KS))
                tm(TT, 512)
                for t in range(NZ1):
                    fm(KS, T, x_lat, "z_freed")
                pe.wait_ge(S("ld_c1"), 16)
                pe.wait_ge(S("ld_p1"), 16 * 3 * (l + 1))
                pe.wait_ge(S("z_freed"), me.nth("z_freed", NZ1))
                for g in range(6):
                    k = 2 if g < 5 else 1
                    if g % 2 in held:
                        pe.wait_ge(*held[g % 2])
                    ins = nc.tensor.matmul(bank[g % 2][:, 0:k * T], c1v("perm"),
                                           Z[:, 2 * g:2 * g + k, :].rearrange("p a t -> p (a t)"), start=True, stop=True)
                    ins.then_inc(S("rot_ready"), 1)
                    read_by(g % 2, "rot_freed")
                for qt in range(TT):
                    if 2 + qt in held:
                        pe.wait_ge(*held[2 + qt])
                    ins = nc.tensor.transpose(bank[2 + qt][:, 0:P], Z[:, Z1["wi"], qt * P:(qt + 1) * P], cst("ident"))
                    ins.then_inc(S("wi_ready"), 1)
                    read_by(2 + qt, "wi_freed")
                pe.wait_ge(S("rope_done"), me.nth("rope_done"))
                for i in range(TT * IDXH):
                    qt, h = i // IDXH, i % IDXH
                    nk = P * (qt + 1)
                    if 4 + i % 2 in held:
                        pe.wait_ge(*held[4 + i % 2])
                    ins = nc.tensor.matmul(bank[4 + i % 2][:, 0:nk], Z[half(h), Z1["qi"] + h // 2, qt * P:(qt + 1) * P],
                                           Z[half(h), Z1["ki"], 0:nk], start=True, stop=True)
                    ins.then_inc(S("idx_ready"), 1)
                    read_by(4 + i % 2, "idx_freed")

                def score1(it, bk):
                    h, qt, nk, _ = it
                    return nc.tensor.matmul(bk[:, 0:nk], Z[half(h), Z1["q"] + h // 2, qt * P:(qt + 1) * P],
                                            Z[half(h), Z1["k"] + h // 2, 0:nk], start=True, stop=True)

                def pv1(j, it, bk):
                    h, qt, nk, _ = it
                    for kt in range(nk // P):
                        ins = nc.tensor.matmul(bk[half(h), qt * P:(qt + 1) * P], V1[:, kt, h * HD:(h + 1) * HD],
                                               PT1[:, j % 2, kt * P:(kt + 1) * P], start=(kt == 0), stop=(kt == nk // P - 1))
                    return ins

                attention(ITEMS1, score1, P1, pv1)
                for src, given, freed in ((CV, "conv_ready", "xc_ready"), (CT, "conv_sq", "cvar_eps")):
                    pe.wait_ge(S(given), me.nth(given))
                    if 4 in held:
                        pe.wait_ge(*held[4])
                    for k in range(2):
                        ins = nc.tensor.matmul(bank[4][:, 0:T], cst("ones256"), src[:, k, :], start=(k == 0), stop=(k == 1))
                    ins.then_inc(S("cstat_ready"), 1)
                    read_by(4, freed)
                pe.wait_ge(S("conv_silu"), me.nth("conv_silu"))
                for m in range(2):
                    if m in held:
                        pe.wait_ge(*held[m])
                    for k in range(2):
                        ins = nc.tensor.matmul(bank[m][:, 0:T], M1[:, k * T + m * P:k * T + (m + 1) * P], CV[:, k, :],
                                               start=(k == 0), stop=(k == 1))
                    ins.then_inc(S("pw_ready"), 1)
                    read_by(m, "pw_freed")
                pe.wait_ge(S("pool_ready"), me.nth("pool_ready"))
                for m in range(2):
                    if 2 + m in held:
                        pe.wait_ge(*held[2 + m])
                    ins = nc.tensor.matmul(bank[2 + m][:, 0:T], M1[:, 512 + m * P:512 + (m + 1) * P], CT[:, m, :],
                                           start=True, stop=True)
                    ins.then_inc(S("pw_ready"), 1)
                    read_by(2 + m, "pw_freed")
                pe.wait_ge(S("y_split"), me.nth("y_split", KS))
                for m in range(KS):
                    fm(KS, T, x_lat, "wo_freed")
                pe.wait_ge(S("ple_split"), me.nth("ple_split"))
                for u in range(2):
                    hi, lo = unit()
                    for j in range(4):
                        b = me.next_tile()
                        if b in held:
                            pe.wait_ge(*held[b])
                        for k in range(2):
                            w = slice((2 * j + k) * P, (2 * j + k + 1) * P)
                            nc.tensor.matmul(bank[b][:, 0:T], hi[:, w], PLEH[:, 0, k, :], start=(k == 0), stop=False)
                            nc.tensor.matmul(bank[b][:, 0:T], hi[:, w], PLEH[:, 1, k, :], start=False, stop=False)
                            ins = nc.tensor.matmul(bank[b][:, 0:T], lo[:, w], PLEH[:, 0, k, :], start=False, stop=(k == 1))
                        ins.then_inc(S("unit_done" if j == 3 else "ple_ready"), 1)
                        read_by(b, "ple_freed")
                pe.wait_ge(S("h_split"), me.nth("h_split", KS))
                for m in range(KS):
                    fm(KS, T, lambda s: (NHI[:, s, T:TC], NLO[:, s, T:TC]), "gate_freed")
            stats(T, Y1)

            for l in range(DEPTH):
                uc = l < DEPTH - 1
                n, rhs = (TC, x_all) if uc else (T, x_lat)
                stats(TC, SQ2)
                pe.wait_ge(S("x_split"), me.nth("x_split", KS))
                for v in range(2):
                    tm(4, VW)
                for name in TILES2:
                    lat = name in LAT_ONLY and not uc
                    fm(KS, T if lat else TC, x_lat if lat else x_all, "z_freed")
                pe.wait_ge(S("ld_c2"), 16 * 2 * (l + 1))
                pe.wait_ge(S("z_freed"), me.nth("z_freed", NZ2))
                for t in range(3):
                    if t % 2 in held:
                        pe.wait_ge(*held[t % 2])
                    ins = nc.tensor.matmul(bank[t % 2][:, 0:T], c2v("perm"), ZB[:, t, 0:T], start=True, stop=True)
                    ins.then_inc(S("rot_ready"), 1)
                    read_by(t % 2, "rot_freed")
                for i in range(4):
                    s, d = i // 2, i % 2
                    if 2 + d in held:
                        pe.wait_ge(*held[2 + d])
                    r = slice(32 * d, 32 * d + 17)
                    for t in range(2):
                        ins = nc.tensor.matmul(bank[2 + d][:, t * 192:(t + 1) * 192],
                                               ZB[r, Z2["glr"], (2 * s + t) * P:(2 * s + t + 1) * P], WG[r, :],
                                               start=True, stop=True)
                    ins.then_inc(S("gate_ready"), 1)
                    read_by(2 + d, "g_ready")
                pe.wait_ge(S("rope_done"), me.nth("rope_done"))
                pe.wait_ge(S("g_ready"), me.nth("g_ready", 4))
                for h in range(GH):
                    for d in range(2):
                        pe.wait_ge(S("g4_ready"), me.nth("g4_ready"))
                        if 2 + d in held:
                            pe.wait_ge(*held[2 + d])
                        u = c2v("uf") if d == 0 else c2v("ub")
                        for s in range(2):
                            for k in range(2):
                                t = k if d == 0 else 1 - k
                                lhs = gates4(2 * h + d)[:, 2 * s + t, :, :].rearrange("p c k -> p (c k)")
                                if k == 0:
                                    o, r = bank[2 + d][:, s * T:(s + 1) * T], u
                                elif d == 0:
                                    o, r = bank[2 + d][:, s * T + P:(s + 1) * T], u[:, 0:P]
                                else:
                                    o, r = bank[2 + d][:, s * T:s * T + P], u[:, P:T]
                                ins = nc.tensor.matmul(o, lhs, r, start=(k == 0), stop=(k == 1))
                        ins.then_inc(S("b_ready"), 1)
                        read_by(2 + d, "b_copied")
                    for w in range(2):
                        if h < 4:
                            t, r0 = 1 - w, 32 * h
                        else:
                            t, r0 = 2, 32 * (h - 4) + (64 if w == 0 else 0)
                        if w in held:
                            pe.wait_ge(*held[w])
                        ins = nc.tensor.matmul(bank[w][:], c2v("rep")[r0:r0 + 32, :], ZB[r0:r0 + 32, t, :], start=True, stop=True)
                        ins.then_inc(S("kq_ready"), 1)
                        read_by(w, "kq_freed")
                    pe.wait_ge(S("dec_ready"), me.nth("dec_ready", 2))
                    seqs = 2 if uc else 1
                    for s in range(seqs):
                        if 4 + s in held:
                            pe.wait_ge(*held[4 + s])
                        for d in range(2):
                            for t in range(2):
                                i = 2 * s + t
                                ins = nc.tensor.matmul(bank[4 + s][:, (2 * d + t) * P:(2 * d + t + 1) * P],
                                                       EY[:, d, 512 + i * P:512 + (i + 1) * P], EY[:, d, i * P:(i + 1) * P],
                                                       start=True, stop=True)
                        ins.then_inc(S("a_ready"), 1)
                        read_by(4 + s, "am_read")
                    if 0 in held:
                        pe.wait_ge(*held[0])
                    for s in range(seqs):
                        for d in range(2):
                            i = 2 * s + (1 - d)
                            ins = nc.tensor.matmul(bank[0][:, (2 * s + d) * P:(2 * s + d + 1) * P],
                                                   EY[:, d, 1024 + s * P:1024 + (s + 1) * P], EY[:, d, i * P:(i + 1) * P],
                                                   start=True, stop=True)
                    ins.then_inc(S("ax_ready"), 1)
                    read_by(0, "ax_freed")
                    if 1 in held:
                        pe.wait_ge(*held[1])
                    for t in range(2):
                        ins = nc.tensor.matmul(bank[1][:, t * T:(t + 1) * T], E0[:, T + t * P:T + (t + 1) * P],
                                               E0[:, 0:T], start=True, stop=True)
                    ins.then_inc(S("ax_ready"), 1)
                    read_by(1, "ax_freed")
                    pe.wait_ge(S("af_ready"), me.nth("af_ready", seqs))
                    pe.wait_ge(S("ax_freed"), me.nth("ax_freed", 2))
                    b, r, vh = 6 + (h // 2) % 2, half(h), slice(h * GDV, (h + 1) * GDV)
                    if h % 2 == 0:
                        if b in held:
                            pe.wait_ge(*held[b])
                    for t in range(2):
                        nc.tensor.matmul(bank[b][r, 0:T], V2[:, t, vh], AF[:, 0, t, :], start=(t == 0), stop=False)
                    for t in range(2):
                        ins = nc.tensor.matmul(bank[b][r, 0:T], V2[:, 2 + t, vh], A0[:, t, :], start=False, stop=(t == 1))
                    if uc:
                        for t in range(2):
                            ins = nc.tensor.matmul(bank[b][r, T:TC], V2[:, 2 + t, vh], AF[:, 1, t, :],
                                                   start=(t == 0), stop=(t == 1))
                    if h % 2 == 0:
                        ins.then_inc(S("gpv_done"), 1)
                    else:
                        ins.then_inc(S("gpv_done"), 1)
                        read_by(b, "og_read")
                        pe.wait_ge(S("osq_ready"), me.nth("osq_ready"))
                        if 5 in held:
                            pe.wait_ge(*held[5])
                        ins = nc.tensor.matmul(bank[5][:, 0:n], cst("blk"), OM[:, 0, 0:n], start=True, stop=True)
                        ins.then_inc(S("oms_ready"), 1)
                        read_by(5, "oms_eps")

                def score2(it, bk):
                    h, qt, nk, own = it
                    o = T if own else 0
                    return nc.tensor.matmul(bk[:, 0:nk], ZB[half(h), Z2["nq"] + h // 2, o + qt * P:o + (qt + 1) * P],
                                            ZB[half(h), Z2["nk"] + h // 2, o:TC], start=True, stop=True)

                def pv2(j, it, bk):
                    h, qt, nk, own = it
                    o, k0 = (T, 2) if own else (0, 0)
                    for kt in range(nk // P):
                        ins = nc.tensor.matmul(bk[half(h), o + qt * P:o + (qt + 1) * P],
                                               V2[:, k0 + kt, VW + h * 64:VW + (h + 1) * 64],
                                               PT2[:, j % 2, kt * P:(kt + 1) * P], start=(kt == 0), stop=(kt == nk // P - 1))
                    return ins

                attention(items2(uc), score2, P2, pv2, uc)
                pe.wait_ge(S("y_split"), me.nth("y_split", KS))
                for m in range(KS):
                    fm(KS, n, rhs, "wo_freed")
                stats(n, SQ2)
                pe.wait_ge(S("x_split"), me.nth("x_split", KS))
                for m in range(2 * FT):
                    fm(KS, n, rhs, "up_freed")
                pe.wait_ge(S("hid_split"), me.nth("hid_split", FT))
                for m in range(KS):
                    fm(FT, n, lambda s: (HHI[:, s, 0:n], HLO[:, s, 0:n]), "wo_freed")
            stats(T, SQ2)

        @block.scalar
        def _(act):
            me = Side(act, "act")
            split = 0

            def A(out, in_, func=ACT.Copy, **kw):
                return nc.scalar.activation(out, in_, func, **kw)

            def split_to(n):
                nonlocal split
                while split < min(n, NU):
                    u = split
                    act.wait_ge(S(f"raw{u % RAW}"), 16 * (u // RAW + 1))
                    if u >= SPL:
                        act.wait_ge(S("unit_done"), u - SPL + 1)
                    w = WIDTHS[u]
                    A(WHI[:, u % SPL, 0:w], RAWB[:, u % RAW, 0:w]).then_inc(S("hi_ready"), 1)
                    split += 1

            def rest(n=1):
                for _ in range(n):
                    me.u += 1
                    split_to(me.u + AHEAD)

            def unit(n=1):
                rest(n)
                act.wait_ge(S("unit_done"), me.u)

            def stats(n, ms, sq):
                for s in range(0, KS, 2):
                    A(sq[:, s:s + 2, 0:n], X[:, s:s + 2, 0:n], ACT.Square).then_inc(S("sq_ready"), 1)
                act.wait_ge(S("ms_eps"), me.nth("ms_eps"))
                A(ms[:, 1, 0:n], ms[:, 0, 0:n], ACT.Ln).then_inc(S("act_chain"), 1)
                act.wait_ge(S("act_chain"), me.nth("act_chain"))
                A(ms[:, 2, 0:n], ms[:, 1, 0:n], ACT.Exp, scale=-0.5).then_inc(S("rs_guess"), 1)

            def split_hi(n, src, o, given):
                for s in range(KS):
                    act.wait_ge(S(given), me.nth(given))
                    A(NHI[:, s, o:o + n], src[:, s, 0:n]).then_inc(S("xh_ready"), 1)

            def softmax(items, lbuf, pbuf, ptbuf, stb, scale, done):
                n = len(items)
                for i in range(n + 2):
                    if i < n:
                        k, nk = i % 3, items[i][2]
                        act.wait_ge(S("l_ready"), me.nth("l_ready"))
                        A(pbuf[:, k, 0:nk], lbuf[:, k, 0:nk], ACT.Exp, bias=stb[:, k, 1:2], scale=scale,
                          accum_out=stb[:, k, 2:3]).then_inc(S("e_ready"), 1)
                    if i >= 2:
                        j = i - 2
                        act.wait_ge(S("pt_ready"), me.nth("pt_ready"))
                        if j >= 2:
                            act.wait_ge(S("pv_done"), me.nth("pv_done"))
                            done(items[j - 2])
                        A(ptbuf[:, j % 2, 0:items[j][2]], bank[2 + j % 2][:, 0:items[j][2]]).then_inc(S("pt_freed"), 1)
                for j in (n - 2, n - 1):
                    act.wait_ge(S("pv_done"), me.nth("pv_done"))
                    done(items[j])

            act.wait_ge(S("ld_prm"), 16)
            A(CS[:], prm_col("cvec", 0, 2 * KS).rearrange("p (s c) -> p s c", c=2), ACT.Silu).then_inc(S("act_chain"), 1)
            act.wait_ge(S("act_chain"), me.nth("act_chain"))
            act.wait_ge(S("ch_zero"), me.nth("ch_zero"))
            A(CHV[:, :, 0:2], CS[:]).then_inc(S("ch_hi"), 1)
            split_to(AHEAD)
            for l in range(DEPTH):
                for n in range(12):
                    unit(4)
                    if n >= 2:
                        act.wait_ge(S("rows_used"), me.nth("rows_used"))
                    A(ROWS[0:4, n % 2, :], bank[me.next_tile()][0:4, :]).then_inc(S("rows_copied"), 1)
                act.wait_ge(S("rows_used"), me.nth("rows_used", 2))

            act.wait_ge(S("ld_x"), 16)
            for l in range(DEPTH):
                stats(T, MS1, Y1)
                split_hi(T, Y1, 0, "t_ready")
                rest(4)
                for t in range(NZ1):
                    unit()
                    A(Z[:, t, :], bank[me.next_tile()][:, 0:T], ACT.Identity, bias=prm_col(f"bin{l}", t)).then_inc(S("z_freed"), 1)
                for qt in range(TT):
                    act.wait_ge(S("wi_ready"), me.nth("wi_ready"))
                    A(WI[:, qt, :], bank[2 + qt][:, 0:IDXH]).then_inc(S("wi_freed"), 1)
                for i in range(TT * IDXH):
                    nk = P * (i // IDXH + 1)
                    act.wait_ge(S("idx_ready"), me.nth("idx_ready"))
                    if i >= 2:
                        act.wait_ge(S("rl_used"), me.nth("rl_used"))
                    A(RL[:, i % 2, 0:nk], bank[4 + i % 2][:, 0:nk], ACT.Relu, scale=HD ** -0.5).then_inc(S("idx_freed"), 1)
                act.wait_ge(S("rl_used"), me.nth("rl_used", 2))

                def done1(it):
                    if ends_pair(it):
                        A(OB[:, it[0] // 2, :], bank[6 + (it[0] // 2) % 2][:, 0:T]).then_inc(S("o_freed"), 1)

                softmax(ITEMS1, L1, P1, PT1, ST1, HD ** -0.5, done1)
                act.wait_ge(S("z_freed"), me.nth("z_freed", NZ1))
                A(SG[:], Z[:, Z1["glu"]:Z1["glu"] + 2, :], ACT.Sigmoid).then_inc(S("glu_ready"), 1)
                A(GT1[:, 0:2, :], Z[:, Z1["cgate"]:Z1["cgate"] + 2, :], ACT.Silu)
                A(GT1[:, 2:4, :], Z[:, Z1["pgate"]:Z1["pgate"] + 2, :], ACT.Silu)
                A(GT1[:, 4:8, :], Z[:, Z1["agate"]:Z1["agate"] + 4, :], ACT.Silu).then_inc(S("silu_ready"), 1)
                act.wait_ge(S("xc_ready"), me.nth("xc_ready"))
                A(CT[:], CV[:], ACT.Square).then_inc(S("conv_sq"), 1)
                act.wait_ge(S("cvar_eps"), me.nth("cvar_eps"))
                A(MS1[:, 1, :], MS1[:, 0, :], ACT.Ln).then_inc(S("act_chain"), 1)
                act.wait_ge(S("act_chain"), me.nth("act_chain"))
                A(MS1[:, 2, :], MS1[:, 1, :], ACT.Exp, scale=-0.5).then_inc(S("rs_guess"), 1)
                act.wait_ge(S("cn_ready"), me.nth("cn_ready"))
                for k in range(2):
                    ins = A(CV[:, k, :], CV[:, k, :], ACT.Silu, bias=prm_col(f"lnb{l}", k), scale=prm_col(f"lng{l}", k))
                ins.then_inc(S("conv_silu"), 1)
                for m in range(2):
                    act.wait_ge(S("pw_ready"), me.nth("pw_ready"))
                    A(Y1[:, m, :], bank[m][:, 0:T], ACT.Identity, bias=prm_col(f"pwb{l}", m)).then_inc(S("pw_freed"), 1)
                act.wait_ge(S("pool_ready"), me.nth("pool_ready"))
                for m in range(2):
                    act.wait_ge(S("pw_ready"), me.nth("pw_ready"))
                    A(Y1[:, 2 + m, :], bank[2 + m][:, 0:T], ACT.Identity, bias=PB[:, m:m + 1],
                      scale=prm_col(f"pools{l}", m)).then_inc(S("pw_freed"), 1)
                split_hi(T, Y1, 0, "y_ready")
                act.wait_ge(S("ld_p1"), 16 * 3 * (l + 1))
                A(PLEH[:, 0, :, :], PIN[:]).then_inc(S("ple_hi"), 1)
                rest(KS)
                me.tile += KS
                split_hi(T, X, T, "wo_freed")
                for u in range(2):
                    for j in range(4):
                        if j == 3:
                            unit()
                        else:
                            act.wait_ge(S("ple_ready"), me.nth("ple_ready"))
                        A(Y1[:, 4 * u + j, :], bank[me.next_tile()][:, 0:T]).then_inc(S("ple_freed"), 1)
                for m in range(KS):
                    unit()
                    if m >= 2:
                        act.wait_ge(S("x_new"), me.nth("x_new"))
                    A(SG[:, m % 2, :], bank[me.next_tile()][:, 0:T], ACT.Sigmoid).then_inc(S("gate_freed"), 1)
                act.wait_ge(S("x_new"), me.nth("x_new", 2))
            stats(T, MS1, Y1)
            act.wait_ge(S("x_new"), me.nth("x_new", KS))

            act.wait_ge(S("x_split"), me.nth("x_split", KS * DEPTH))
            act.wait_ge(S("y_split"), me.nth("y_split", KS * DEPTH))
            act.wait_ge(S("pw_freed"), me.nth("pw_freed", 4 * DEPTH))
            for l in range(DEPTH):
                uc = l < DEPTH - 1
                n = TC if uc else T
                stats(TC, MS2, SQ2)
                split_hi(TC, TB2, 0, "t_ready")
                act.wait_ge(S("x_split"), me.nth("x_split", KS))
                for v in range(2):
                    unit(4)
                    for t in range(4):
                        A(V2[:, t, v * VW:(v + 1) * VW], bank[t][:, 0:VW]).then_inc(S("v_freed"), 1)
                for i, name in enumerate(TILES2):
                    unit()
                    w = T if name in LAT_ONLY and not uc else TC
                    z, g = ZB[:, i, 0:w], bank[me.next_tile()][:, 0:w]
                    if name == "glr":
                        ins = A(z, g, ACT.Identity, bias=cst("glrone"))
                    elif name == "nq":
                        ins = A(z, g, scale=64 ** -0.5)
                    else:
                        ins = A(z, g)
                    ins.then_inc(S("z_freed"), 1)
                for i in range(4):
                    act.wait_ge(S("gate_ready"), me.nth("gate_ready"))
                    g = gate_part(GTA, i)
                    A(g, bank[2 + i % 2][:, 0:VW].rearrange("p (t k) -> p t k", t=2), ACT.Abs).then_inc(S("act_chain"), 1)
                    act.wait_ge(S("act_chain"), me.nth("act_chain"))
                    A(g, g, ACT.Exp, scale=-1.0).then_inc(S("act_chain"), 1)
                    act.wait_ge(S("act_chain"), me.nth("act_chain"))
                    A(g, g, ACT.Ln, bias=1.0).then_inc(S("gln_ready"), 1)
                for h in range(GH):
                    for d in range(2):
                        act.wait_ge(S("b_ready"), me.nth("b_ready"))
                        A(EY[:, d, 0:512], bank[2 + d][:]).then_inc(S("b_copied"), 1)
                    if h > 0:
                        act.wait_ge(S("dec_ready"), me.nth("dec_ready", 2))
                    for w in range(2):
                        act.wait_ge(S("kq_ready"), me.nth("kq_ready"))
                        A(KQ[:, w, :], bank[w][:], scale=1.0 if w == 0 else GDK ** -0.5).then_inc(S("kq_freed"), 1)
                    for d in range(2):
                        act.wait_ge(S("bm_ready"), me.nth("bm_ready"))
                        r = slice(32 * d, 32 * d + 32)
                        A(E0[r, 0:T], EY[r, d, 0:T], ACT.Exp)
                        A(E0[r, T:TC], EY[r, d, T:TC], ACT.Exp, scale=-1.0, bias=BM[r, d, 4:5]).then_inc(S("e0_ready"), 1)
                        act.wait_ge(S("e0_ready"), me.nth("e0_ready"))
                        act.wait_ge(S("ex_ready"), me.nth("ex_ready"))
                        A(EY[:, d, :], EX[:], ACT.Exp).then_inc(S("ey_ready"), 1)
                    act.wait_ge(S("ax_ready"), me.nth("ax_ready"))
                    for s in range(2 if uc else 1):
                        ins = A(AF[:, s, :, :].rearrange("p a t -> p (a t)")[:, P:3 * P], bank[0][:, 2 * s * P:(2 * s + 2) * P])
                    ins.then_inc(S("ax_freed"), 1)
                    act.wait_ge(S("ax_ready"), me.nth("ax_ready"))
                    A(A0[:].rearrange("p a t -> p (a t)"), bank[1][:]).then_inc(S("ax_freed"), 1)
                    act.wait_ge(S("gpv_done"), me.nth("gpv_done"))
                    if h % 2 == 1:
                        A(OM[:, 0, 0:n], bank[6 + (h // 2) % 2][:, 0:n], ACT.Square).then_inc(S("osq_ready"), 1)
                        act.wait_ge(S("oms_eps"), me.nth("oms_eps"))
                        A(OM[:, 3, 0:n], OM[:, 1, 0:n], ACT.Ln).then_inc(S("act_chain"), 1)
                        act.wait_ge(S("act_chain"), me.nth("act_chain"))
                        A(OM[:, 3, 0:n], OM[:, 3, 0:n], ACT.Exp, scale=-0.5).then_inc(S("rs_guess"), 1)
                        A(OM[:, 2, 0:n], ZB[:, Z2["r"] + h // 2, 0:n], ACT.Silu).then_inc(S("rsilu_ready"), 1)
                        act.wait_ge(S("yo_ready"), me.nth("yo_ready"))
                        A(NHI[:, h // 2, 0:n], OG[:, 0:n]).then_inc(S("xh_ready"), 1)
                act.wait_ge(S("dec_ready"), me.nth("dec_ready", 2))
                for k in range(2):
                    act.wait_ge(S("yo_ready"), me.nth("yo_ready"))
                    A(NHI[:, 3 + k, 0:n], ZB[:, Z2["scx"] + k, 0:n]).then_inc(S("xh_ready"), 1)
                act.wait_ge(S("y_split"), me.nth("y_split", 5))

                def done2(it):
                    if ends_pair(it, uc):
                        k = it[0] // 2
                        A(OY[:, k, 0:n], bank[6 + k % 2][:, 0:n]).then_inc(S("o_freed"), 1)
                        act.wait_ge(S("o_freed"), me.nth("o_freed"))
                        A(NHI[:, 5 + k, 0:n], OY[:, k, 0:n]).then_inc(S("xh_ready"), 1)

                if l == 0:
                    act.wait_ge(S("o_freed"), me.nth("o_freed", 4 * DEPTH))
                softmax(items2(uc), L2, P2, PT2, ST2, 1.0, done2)
                act.wait_ge(S("y_split"), me.nth("y_split", 3))
                rest(KS)
                me.tile += KS
                act.wait_ge(S("wo_freed"), me.nth("wo_freed", KS))
                stats(n, MS2, SQ2)
                split_hi(n, TB2, 0, "t_ready")
                act.wait_ge(S("x_split"), me.nth("x_split", KS))
                for p in range(FT + 2):
                    if p < FT:
                        for w in range(2):
                            unit()
                            j = w * FT + p
                            if w == 0 and p >= 3:
                                act.wait_ge(S("hid_split"), me.nth("hid_split"))
                            A(CF[:, w, p % 3, 0:n], bank[me.next_tile()][:, 0:n], ACT.Identity,
                              bias=prm_col(f"fb{l}", j), scale=prm_col(f"fw{l}", 2 * FT + j)).then_inc(S("centre_ready"), 1)
                    if 1 <= p < FT + 1:
                        act.wait_ge(S("up_freed"), me.nth("up_freed", 2))
                        A(CF[:, 0, (p - 1) % 3, 0:n], CF[:, 0, (p - 1) % 3, 0:n], ACT.Silu).then_inc(S("fsilu_ready"), 1)
                    if p >= 2:
                        act.wait_ge(S("hid_ready"), me.nth("hid_ready"))
                        A(HHI[:, p - 2, 0:n], CF[:, 1, (p - 2) % 3, 0:n]).then_inc(S("hh_ready"), 1)
                act.wait_ge(S("hid_split"), me.nth("hid_split", 3))
                rest(3 * KS)
                me.tile += KS
                act.wait_ge(S("wo_freed"), me.nth("wo_freed", KS))
            stats(T, MS2, SQ2)

        @block.vector
        def _(dve):
            me = Side(dve, "dve")
            V = nc.vector
            split = 0

            def split_to(n):
                nonlocal split
                while split < min(n, NU):
                    u = split
                    dve.wait_ge(S("hi_ready"), u + 1)
                    w = WIDTHS[u]
                    V.tensor_tensor(WLO[:, u % SPL, 0:w], RAWB[:, u % RAW, 0:w], WHI[:, u % SPL, 0:w].bitcast(F32),
                                    ALU.subtract).then_inc(S("lo_ready"), 1)
                    split += 1

            def rest(n=1):
                for _ in range(n):
                    me.u += 1
                    split_to(me.u + AHEAD)

            def unit(n=1):
                rest(n)
                dve.wait_ge(S("unit_done"), me.u)

            def rsqrt(m, g, t, out):
                V.tensor_tensor(t, g, g, ALU.mult).then_inc(S("dve_chain"), 1)
                dve.wait_ge(S("dve_chain"), me.nth("dve_chain"))
                V.tensor_tensor(t, t, m, ALU.mult).then_inc(S("dve_chain"), 1)
                dve.wait_ge(S("dve_chain"), me.nth("dve_chain"))
                V.tensor_scalar(t, t, -0.5, 1.5, ALU.mult, ALU.add).then_inc(S("dve_chain"), 1)
                dve.wait_ge(S("dve_chain"), me.nth("dve_chain"))
                V.tensor_tensor(out, g, t, ALU.mult).then_inc(S("dve_chain"), 1)
                dve.wait_ge(S("dve_chain"), me.nth("dve_chain"))

            def stats(n, ms):
                dve.wait_ge(S("ms_ready"), me.nth("ms_ready"))
                V.tensor_scalar(ms[:, 0, 0:n], bank[4][:, 0:n], EPS, None, ALU.add).then_inc(S("ms_eps"), 1)
                dve.wait_ge(S("rs_guess"), me.nth("rs_guess"))
                rsqrt(ms[:, 0, 0:n], ms[:, 2, 0:n], ms[:, 1, 0:n], ms[:, 3, 0:n])

            def split_lo(n, src, o, done):
                for s in range(KS):
                    dve.wait_ge(S("xh_ready"), me.nth("xh_ready"))
                    V.tensor_tensor(NLO[:, s, o:o + n], src[:, s, 0:n], NHI[:, s, o:o + n].bitcast(F32), ALU.subtract).then_inc(S(done), 1)

            def softmax(items, bias, lbuf, pbuf, stb, scale):
                n = len(items)
                for i in range(n + 1):
                    if i < n:
                        k, nk = i % 3, items[i][2]
                        b = bias(items[i])
                        dve.wait_ge(S("s_ready"), me.nth("s_ready"))
                        if b is None:
                            V.tensor_copy(lbuf[:, k, 0:nk], bank[i % 2][:, 0:nk])
                            V.reduce_max(stb[:, k, 0:1], bank[i % 2][:, 0:nk], AX_X).then_inc(S("s_freed"), 1)
                        else:
                            V.tensor_tensor_reduce(out=lbuf[:, k, 0:nk], in0=bank[i % 2][:, 0:nk], in1=b, scale=1.0,
                                                   scalar=-3.0e38, op0=ALU.add, op1=ALU.max,
                                                   accum_out=stb[:, k, 0:1]).then_inc(S("s_freed"), 1)
                        dve.wait_ge(S("s_freed"), me.nth("s_freed"))
                        V.tensor_scalar(stb[:, k, 1:2], stb[:, k, 0:1], -scale, None, ALU.mult).then_inc(S("l_ready"), 1)
                    if i >= 1:
                        k, nk = (i - 1) % 3, items[i - 1][2]
                        dve.wait_ge(S("e_ready"), me.nth("e_ready"))
                        V.reciprocal(stb[:, k, 3:4], stb[:, k, 2:3]).then_inc(S("dve_chain"), 1)
                        dve.wait_ge(S("dve_chain"), me.nth("dve_chain"))
                        V.tensor_scalar(pbuf[:, k, 0:nk], pbuf[:, k, 0:nk], stb[:, k, 3:4], None, ALU.mult).then_inc(S("p_ready"), 1)

            dve.wait_ge(S("ld_prm"), 16)
            dve.wait_ge(S("ch_hi"), me.nth("ch_hi"))
            V.tensor_tensor(CHV[:, :, 2:4], CS[:], CHV[:, :, 0:2].bitcast(F32), ALU.subtract).then_inc(S("ch_ready"), 1)
            split_to(AHEAD)
            for l in range(DEPTH):
                rest(48)
                me.tile += 12
                dve.wait_ge(S("rows_used"), me.nth("rows_used", 12))
                V.tensor_tensor(MOD[:, l, :, :], bank[6][:, 0:96].rearrange("p (j c) -> p j c", c=2),
                                bl(prm_col(f"bada{l}", 0, 48), 2), ALU.add).then_inc(S("mod_done"), 1)

            dve.wait_ge(S("ld_x"), 16)
            V.memset(UP[:, :, 0:CONV_K - 1], 0.0)
            V.memset(PP[:, :, 0:16], 0.0)
            V.memset(PS[:, :, :, 0:16], 0.0).then_inc(S("dve_chain"), 1)
            dve.wait_ge(S("dve_chain"), me.nth("dve_chain"))
            dve.wait_ge(S("ld_c1"), 16)
            for l in range(DEPTH):
                dve.wait_ge(S("ld_p1"), 16 * 3 * (l + 1))
                stats(T, MS1)
                for s in range(KS):
                    V.scalar_tensor_tensor(Y1[:, s, :], X[:, s, 0:T], prm_col(f"norm{l}", s), MS1[:, 3, :],
                                           ALU.mult, ALU.mult).then_inc(S("t_ready"), 1)
                split_lo(T, Y1, 0, "x_split")
                unit(4)
                for t in range(TT):
                    V.tensor_tensor(V1[:, t, :], bank[t][:], BV[:], ALU.add).then_inc(S("v_freed"), 1)
                rest(NZ1)
                me.tile += NZ1
                dve.wait_ge(S("z_freed"), me.nth("z_freed", NZ1))
                for g in range(6):
                    k = 2 if g < 5 else 1
                    z = Z[:, 2 * g:2 * g + k, :]
                    rt = RT[:, 0:k * T].rearrange("p (a t) -> p a t", a=k)
                    dve.wait_ge(S("rot_ready"), me.nth("rot_ready"))
                    V.tensor_tensor(rt, bank[g % 2][:, 0:k * T].rearrange("p (a t) -> p a t", a=k),
                                    bc(c1v("sin"), k), ALU.mult).then_inc(S("rot_freed"), 1)
                    V.tensor_tensor(z, z, bc(c1v("cos"), k), ALU.mult).then_inc(S("dve_chain"), 1)
                    dve.wait_ge(S("dve_chain"), me.nth("dve_chain"))
                    ins = V.tensor_tensor(z, z, rt, ALU.add)
                    if g < 5:
                        ins.then_inc(S("dve_chain"), 1)
                        dve.wait_ge(S("dve_chain"), me.nth("dve_chain"))
                ins.then_inc(S("rope_done"), 1)
                dve.wait_ge(S("wi_freed"), me.nth("wi_freed", TT))
                for i in range(TT * IDXH):
                    qt, h = i // IDXH, i % IDXH
                    nk = P * (qt + 1)
                    dve.wait_ge(S("idx_freed"), me.nth("idx_freed"))
                    if h == 0:
                        ins = V.tensor_scalar(SC[:, qt, 0:nk], RL[:, i % 2, 0:nk], WI[:, qt, h:h + 1], None, ALU.mult)
                    else:
                        ins = V.scalar_tensor_tensor(SC[:, qt, 0:nk], RL[:, i % 2, 0:nk], WI[:, qt, h:h + 1],
                                                     SC[:, qt, 0:nk], ALU.mult, ALU.add)
                    ins.then_inc(S("rl_used"), 1)
                    dve.wait_ge(S("rl_used"), me.nth("rl_used"))
                for qt in range(TT):
                    nk = P * (qt + 1)
                    sc, causal = SC[:, qt, 0:nk], c1v("causal")[:, qt * T:qt * T + nk]
                    V.tensor_tensor(sc, sc, causal, ALU.add).then_inc(S("dve_chain"), 1)
                    dve.wait_ge(S("dve_chain"), me.nth("dve_chain"))
                    for _ in range(TOPK // 8):
                        V.max(M8[:], sc).then_inc(S("dve_chain"), 1)
                        dve.wait_ge(S("dve_chain"), me.nth("dve_chain"))
                        V.match_replace(out=sc, in_to_replace=M8[:], in_values=sc, imm_value=-3.0e38).then_inc(S("dve_chain"), 1)
                        dve.wait_ge(S("dve_chain"), me.nth("dve_chain"))
                    V.tensor_scalar(MB[:, qt, 0:nk], sc, -2.0e38, -1.0e30, ALU.is_gt, ALU.mult).then_inc(S("dve_chain"), 1)
                    dve.wait_ge(S("dve_chain"), me.nth("dve_chain"))
                    V.tensor_tensor(MB[:, qt, 0:nk], MB[:, qt, 0:nk], causal, ALU.add).then_inc(S("dve_chain"), 1)
                    dve.wait_ge(S("dve_chain"), me.nth("dve_chain"))
                softmax(ITEMS1, lambda it: MB[:, it[1], 0:it[2]], L1, P1, ST1, HD ** -0.5)
                dve.wait_ge(S("glu_ready"), me.nth("glu_ready"))
                V.tensor_tensor(UP[:, :, CONV_K - 1:], Z[:, Z1["val"]:Z1["val"] + 2, :], SG[:], ALU.mult).then_inc(S("dve_chain"), 1)
                dve.wait_ge(S("dve_chain"), me.nth("dve_chain"))
                for k in range(CONV_K):
                    for m in range(2):
                        w, src = prm_col(f"dww{l}", m * CONV_K + k), UP[:, m, k:k + T]
                        if k == 0:
                            ins = V.tensor_scalar(CV[:, m, :], src, w, prm_col(f"dwb{l}", m), ALU.mult, ALU.add)
                        else:
                            ins = V.scalar_tensor_tensor(CV[:, m, :], src, w, CV[:, m, :], ALU.mult, ALU.add)
                    if k < CONV_K - 1:
                        ins.then_inc(S("dve_chain"), 1)
                        dve.wait_ge(S("dve_chain"), me.nth("dve_chain"))
                ins.then_inc(S("conv_ready"), 1)
                dve.wait_ge(S("conv_ready"), me.nth("conv_ready"))
                dve.wait_ge(S("cstat_ready"), me.nth("cstat_ready"))
                V.tensor_tensor(CV[:], CV[:], bc(bank[4][:, 0:T], 2), ALU.subtract).then_inc(S("xc_ready"), 1)
                dve.wait_ge(S("xc_ready"), me.nth("xc_ready"))
                V.tensor_copy(PP[:, :, 16:], Z[:, Z1["pin"]:Z1["pin"] + 2, :]).then_inc(S("dve_chain"), 1)
                dve.wait_ge(S("dve_chain"), me.nth("dve_chain"))
                src = PP
                for j in range(4):
                    s = src[:] if j == 0 else PS[:, j - 1, :, :]
                    V.tensor_tensor(PS[:, j, :, 16:], s[:, :, 16:], s[:, :, 16 - (1 << j):16 + T - (1 << j)], ALU.add).then_inc(S("dve_chain"), 1)
                    dve.wait_ge(S("dve_chain"), me.nth("dve_chain"))
                V.tensor_tensor(PB[:], prm_col(f"poolb{l}", 0, 2), prm_col(f"pools{l}", 0, 2), ALU.mult).then_inc(S("dve_chain"), 1)
                dve.wait_ge(S("dve_chain"), me.nth("dve_chain"))
                dve.wait_ge(S("cstat_ready"), me.nth("cstat_ready"))
                V.tensor_scalar(MS1[:, 0, :], bank[4][:, 0:T], EPS, None, ALU.add).then_inc(S("cvar_eps"), 1)
                dve.wait_ge(S("rs_guess"), me.nth("rs_guess"))
                rsqrt(MS1[:, 0, :], MS1[:, 2, :], MS1[:, 1, :], MS1[:, 3, :])
                V.tensor_tensor(CV[:], CV[:], bc(MS1[:, 3, :], 2), ALU.mult).then_inc(S("cn_ready"), 1)
                for g in range(4):
                    r, m = half(g), g // 2
                    ins = V.tensor_tensor(CT[r, m, :], PS[r, g, m, 16:], c1v("icnt")[r, m * T:(m + 1) * T], ALU.mult)
                ins.then_inc(S("dve_chain"), 1)
                dve.wait_ge(S("dve_chain"), me.nth("dve_chain"))
                V.tensor_tensor(CT[:], CT[:], PP[:, :, 16:], ALU.subtract).then_inc(S("pool_ready"), 1)
                dve.wait_ge(S("silu_ready"), me.nth("silu_ready"))
                dve.wait_ge(S("o_freed"), me.nth("o_freed", 4))
                for m in range(KS):
                    if m < 4:
                        dve.wait_ge(S("pw_freed"), me.nth("pw_freed"))
                    V.tensor_tensor(Y1[:, m, :], Y1[:, m, :] if m < 4 else OB[:, m - 4, :], GT1[:, m, :], ALU.mult).then_inc(S("y_ready"), 1)
                split_lo(T, Y1, 0, "y_split")
                dve.wait_ge(S("ple_hi"), me.nth("ple_hi"))
                V.tensor_tensor(PLEH[:, 1, :, :], PIN[:], PLEH[:, 0, :, :].bitcast(F32), ALU.subtract).then_inc(S("ple_split"), 1)
                for m in range(KS):
                    unit()
                    V.tensor_tensor(X[:, m, 0:T], X[:, m, 0:T], bank[me.next_tile()][:, 0:T], ALU.add).then_inc(S("wo_freed"), 1)
                split_lo(T, X, T, "h_split")
                rest(2)
                dve.wait_ge(S("ple_freed"), me.nth("ple_freed", KS))
                me.tile += 2 * KS
                for m in range(KS):
                    rest()
                    dve.wait_ge(S("gate_freed"), me.nth("gate_freed"))
                    V.tensor_tensor(Y1[:, m, :], Y1[:, m, :], SG[:, m % 2, :], ALU.mult).then_inc(S("dve_chain"), 1)
                    dve.wait_ge(S("dve_chain"), me.nth("dve_chain"))
                    V.tensor_tensor(X[:, m, 0:T], X[:, m, 0:T], Y1[:, m, :], ALU.add).then_inc(S("x_new"), 1)
            stats(T, MS1)
            for s in range(KS):
                V.scalar_tensor_tensor(X[:, s, 0:T], X[:, s, 0:T], prm_col("fin1", s), MS1[:, 3, :],
                                       ALU.mult, ALU.mult).then_inc(S("x_new"), 1)

            def modulate(l, n, gain, shift, scale):
                V.scalar_tensor_tensor(GM[:], MOD[:, l, scale:scale + KS, :], 1.0, bl(prm_col(gain, 0, KS), 2),
                                       ALU.add, ALU.mult).then_inc(S("dve_chain"), 1)
                dve.wait_ge(S("dve_chain"), me.nth("dve_chain"))
                for s in range(KS):
                    for c in range(n // T):
                        w = slice(c * T, (c + 1) * T)
                        ins = V.scalar_tensor_tensor(TB2[:, s, w], X[:, s, w], GM[:, s, c:c + 1], MS2[:, 3, w], ALU.mult, ALU.mult)
                    ins.then_inc(S("dve_chain"), 1)
                    dve.wait_ge(S("dve_chain"), me.nth("dve_chain"))
                    for c in range(n // T):
                        w = slice(c * T, (c + 1) * T)
                        ins = V.tensor_scalar(TB2[:, s, w], TB2[:, s, w], MOD[:, l, shift + s, c:c + 1], None, ALU.add)
                    ins.then_inc(S("t_ready"), 1)
                split_lo(n, TB2, 0, "x_split")

            def residual(l, n, gate, units):
                for m in range(KS):
                    unit(units)
                    b = bank[me.next_tile()]
                    for c in range(n // T):
                        w = slice(c * T, (c + 1) * T)
                        ins = V.scalar_tensor_tensor(X[:, m, w], b[:, w], MOD[:, l, gate + m, c:c + 1], X[:, m, w],
                                                     ALU.mult, ALU.add)
                    ins.then_inc(S("wo_freed"), 1)

            def seq(ap, n):
                return ap.rearrange("p (s t) -> p s t", t=T)

            dve.wait_ge(S("x_new"), me.nth("x_new", KS * (DEPTH + 1)))
            dve.wait_ge(S("s_freed"), me.nth("s_freed", 0))
            for l in range(DEPTH):
                uc = l < DEPTH - 1
                n = TC if uc else T
                stats(TC, MS2)
                modulate(l, TC, f"nmix{l}", SH1, SC1)
                rest(8 + NZ2)
                me.tile += NZ2
                dve.wait_ge(S("ld_c2"), 16 * 2 * (l + 1))
                dve.wait_ge(S("z_freed"), me.nth("z_freed", NZ2))
                for t in range(3):
                    z = ZB[:, t, 0:T]
                    dve.wait_ge(S("rot_ready"), me.nth("rot_ready"))
                    V.tensor_tensor(AM[:, 0:T], bank[t % 2][:, 0:T], c2v("sin"), ALU.mult).then_inc(S("rot_freed"), 1)
                    V.tensor_tensor(z, z, c2v("cos"), ALU.mult).then_inc(S("dve_chain"), 1)
                    dve.wait_ge(S("dve_chain"), me.nth("dve_chain"))
                    ins = V.tensor_tensor(z, z, AM[:, 0:T], ALU.add)
                    if t < 2:
                        ins.then_inc(S("dve_chain"), 1)
                        dve.wait_ge(S("dve_chain"), me.nth("dve_chain"))
                ins.then_inc(S("rope_done"), 1)
                for i in range(4):
                    dve.wait_ge(S("gln_ready"), me.nth("gln_ready"))
                    V.scalar_tensor_tensor(gate_part(GT, i), bank[2 + i % 2][:, 0:VW].rearrange("p (t k) -> p t k", t=2),
                                           0.0, gate_part(GTA, i), ALU.min, ALU.subtract).then_inc(S("g_ready"), 1)
                for h in range(GH):
                    def middles(d):
                        dve.wait_ge(S("b_copied"), me.nth("b_copied"))
                        b = EY[:, d, 0:TC]
                        for c in range(NCH):
                            r = slice(CH * c, CH * (c + 1))
                            V.tensor_copy(BM[r, d, 0:4], EY[r, d, 0:TC].rearrange("p (i t) -> p i t", t=P)[
                                :, :, CH * c + CH // 2 - 1 + d])
                        e = TC - 1 if d == 0 else T
                        V.tensor_copy(BM[:, d, 4:5], b[:, e:e + 1]).then_inc(S("bm_ready"), 1)
                        dve.wait_ge(S("bm_ready"), me.nth("bm_ready"))
                        V.tensor_tensor(AM[:].rearrange("p (i t) -> p i t", t=P),
                                        b.rearrange("p (i t) -> p i t", t=P),
                                        bl(BM[:, d, 0:4], P), ALU.subtract).then_inc(S("dve_chain"), 1)
                        dve.wait_ge(S("dve_chain"), me.nth("dve_chain"))

                    def exponents(d):
                        am = AM[:].rearrange("p (i t) -> p i t", t=P)
                        cap = c2v("capkf") if d == 0 else c2v("capkb")
                        V.tensor_tensor(EX[:, 0:512].rearrange("p (i t) -> p i t", t=P), am, bc(c2v("capq"), 4), ALU.min)
                        V.scalar_tensor_tensor(EX[:, 512:1024].rearrange("p (i t) -> p i t", t=P), am, -1.0,
                                               bc(cap, 4), ALU.mult, ALU.min)
                        V.tensor_tensor(EX[:, 1024:].rearrange("p (s t) -> p s t", t=P),
                                        bl(BM[:, d, 1 - d:4:2], P),
                                        EY[:, d, 0:TC].rearrange("p (s i t) -> p s i t", i=2, t=P)[:, :, d, :],
                                        ALU.subtract).then_inc(S("ex_ready"), 1)

                    def decay(d):
                        V.tensor_tensor(EY[:, d, 0:512], EY[:, d, 0:512], KQ[:, 1, :], ALU.mult)
                        V.tensor_tensor(EY[:, d, 512:1024], EY[:, d, 512:1024], KQ[:, 0, :], ALU.mult)
                        dve.wait_ge(S("e0_ready"), me.nth("e0_ready"))
                        if d == 1:
                            V.tensor_tensor(E0[:, 0:T], E0[:, 0:T], KQ[0:64, 1, 0:T], ALU.mult)
                            V.tensor_tensor(E0[:, T:], E0[:, T:], KQ[0:64, 0, T:], ALU.mult)
                        ey = EY[:, d, 1024:].rearrange("p (s t) -> p s t", t=P)
                        V.tensor_tensor(ey, ey, KQ[:, 0, :].rearrange("p (s i t) -> p s i t", i=2, t=P)[:, :, d, :],
                                        ALU.mult).then_inc(S("dec_ready"), 1)

                    middles(0)
                    exponents(0)
                    middles(1)
                    dve.wait_ge(S("ey_ready"), me.nth("ey_ready"))
                    exponents(1)
                    dve.wait_ge(S("kq_freed"), me.nth("kq_freed", 2))
                    decay(0)
                    dve.wait_ge(S("ey_ready"), me.nth("ey_ready"))
                    decay(1)
                    if h > 0:
                        dve.wait_ge(S("gpv_done"), me.nth("gpv_done"))
                    for s in range(2 if uc else 1):
                        dve.wait_ge(S("a_ready"), me.nth("a_ready"))
                        V.tensor_tensor(AM[:], bank[4 + s][:], c2v("mask"), ALU.mult).then_inc(S("am_read"), 1)
                        dve.wait_ge(S("am_read"), me.nth("am_read"))
                        o = AF[:, s, :, :].rearrange("p a (b t) -> p (a b) t", t=P)[:, 0:4:3, :]
                        V.tensor_tensor(o, AM[:, 0:T].rearrange("p (a t) -> p a t", t=P),
                                        AM[:, T:].rearrange("p (a t) -> p a t", t=P), ALU.add).then_inc(S("af_ready"), 1)
                        dve.wait_ge(S("af_ready"), me.nth("af_ready"))
                    if h % 2 == 1:
                        k = h // 2
                        dve.wait_ge(S("oms_ready"), me.nth("oms_ready"))
                        V.tensor_scalar(OM[:, 1, 0:n], bank[5][:, 0:n], EPS, None, ALU.add).then_inc(S("oms_eps"), 1)
                        dve.wait_ge(S("rs_guess"), me.nth("rs_guess"))
                        rsqrt(OM[:, 1, 0:n], OM[:, 3, 0:n], OM[:, 0, 0:n], OM[:, 3, 0:n])
                        V.tensor_tensor(OG[:, 0:n], bank[6 + k % 2][:, 0:n], OM[:, 3, 0:n], ALU.mult).then_inc(S("og_read"), 1)
                        dve.wait_ge(S("og_read"), me.nth("og_read"))
                        dve.wait_ge(S("rsilu_ready"), me.nth("rsilu_ready"))
                        V.scalar_tensor_tensor(OG[:, 0:n], OG[:, 0:n], prm_col(f"glag{l}"), OM[:, 2, 0:n],
                                               ALU.mult, ALU.mult).then_inc(S("yo_ready"), 1)
                        dve.wait_ge(S("yo_ready"), me.nth("yo_ready"))
                        dve.wait_ge(S("xh_ready"), me.nth("xh_ready"))
                        V.tensor_tensor(NLO[:, k, 0:n], OG[:, 0:n], NHI[:, k, 0:n].bitcast(F32), ALU.subtract).then_inc(S("y_split"), 1)
                dve.wait_ge(S("gpv_done"), me.nth("gpv_done"))
                cc_, xx = ZB[:, Z2["scc"]:Z2["scc"] + 2, 0:n], ZB[:, Z2["scx"]:Z2["scx"] + 2, 0:n]
                V.tensor_tensor(cc_, cc_, xx, ALU.mult).then_inc(S("dve_chain"), 1)
                dve.wait_ge(S("dve_chain"), me.nth("dve_chain"))
                for k in range(2):
                    a, x = ZB[:, Z2["scc"] + k, 0:n], ZB[:, Z2["scx"] + k, 0:n]
                    w = [prm_col(f"scw{l}", 2 * tap + k) for tap in range(3)]
                    V.tensor_scalar(x, a, w[1], prm_col(f"scbias{l}", k), ALU.mult, ALU.add).then_inc(S("dve_chain"), 1)
                    dve.wait_ge(S("dve_chain"), me.nth("dve_chain"))
                    a, y = seq(a, n), seq(x, n)
                    V.scalar_tensor_tensor(y[:, :, 1:], a[:, :, :-1], w[0], y[:, :, 1:], ALU.mult, ALU.add).then_inc(S("dve_chain"), 1)
                    dve.wait_ge(S("dve_chain"), me.nth("dve_chain"))
                    V.scalar_tensor_tensor(y[:, :, :-1], a[:, :, 1:], w[2], y[:, :, :-1], ALU.mult, ALU.add).then_inc(S("dve_chain"), 1)
                    dve.wait_ge(S("dve_chain"), me.nth("dve_chain"))
                    V.tensor_tensor(x, x, ZB[:, Z2["scb"] + k, 0:n], ALU.mult).then_inc(S("yo_ready"), 1)
                    dve.wait_ge(S("yo_ready"), me.nth("yo_ready"))
                for k in range(2):
                    dve.wait_ge(S("xh_ready"), me.nth("xh_ready"))
                    V.tensor_tensor(NLO[:, 3 + k, 0:n], ZB[:, Z2["scx"] + k, 0:n], NHI[:, 3 + k, 0:n].bitcast(F32),
                                    ALU.subtract).then_inc(S("y_split"), 1)
                V.memset(NB[:, :, :, T:], 0.0).then_inc(S("dve_chain"), 1)
                dve.wait_ge(S("dve_chain"), me.nth("dve_chain"))
                half_loads = [0, 0]

                def bias2(it):
                    h, qt, nk, own = it
                    if own:
                        return None
                    if qt == 0:
                        half_loads[h % 2] += 1
                        dve.wait_ge(S(f"ld_nb{h % 2}"), 16 * (NAH // 2 * l + half_loads[h % 2]))
                    return NB[:, h % 2, qt, :]

                if l == 0:
                    me.seen["s_freed"] = len(ITEMS1) * DEPTH
                softmax(items2(uc), bias2, L2, P2, ST2, 1.0)
                for k in range(3):
                    dve.wait_ge(S("xh_ready"), me.nth("xh_ready"))
                    V.tensor_tensor(NLO[:, 5 + k, 0:n], OY[:, k, 0:n], NHI[:, 5 + k, 0:n].bitcast(F32),
                                    ALU.subtract).then_inc(S("y_split"), 1)
                residual(l, n, G1, 1)
                dve.wait_ge(S("wo_freed"), me.nth("wo_freed", KS))
                stats(n, MS2)
                modulate(l, n, f"nffn{l}", SH2, SC2)
                for p in range(FT + 2):
                    if p < FT:
                        for w in range(2):
                            unit()
                            dve.wait_ge(S("centre_ready"), me.nth("centre_ready"))
                            b = seq(bank[me.next_tile()][:, 0:n], n)
                            y = seq(CF[:, w, p % 3, 0:n], n)
                            j = w * FT + p
                            V.scalar_tensor_tensor(y[:, :, 1:], b[:, :, :-1], prm_col(f"fw{l}", j),
                                                   y[:, :, 1:], ALU.mult, ALU.add).then_inc(S("dve_chain"), 1)
                            dve.wait_ge(S("dve_chain"), me.nth("dve_chain"))
                            V.scalar_tensor_tensor(y[:, :, :-1], b[:, :, 1:], prm_col(f"fw{l}", 4 * FT + j),
                                                   y[:, :, :-1], ALU.mult, ALU.add).then_inc(S("up_freed"), 1)
                    if 1 <= p < FT + 1:
                        k = (p - 1) % 3
                        dve.wait_ge(S("fsilu_ready"), me.nth("fsilu_ready"))
                        V.tensor_tensor(CF[:, 1, k, 0:n], CF[:, 1, k, 0:n], CF[:, 0, k, 0:n], ALU.mult).then_inc(S("hid_ready"), 1)
                    if p >= 2:
                        dve.wait_ge(S("hh_ready"), me.nth("hh_ready"))
                        V.tensor_tensor(HLO[:, p - 2, 0:n], CF[:, 1, (p - 2) % 3, 0:n],
                                        HHI[:, p - 2, 0:n].bitcast(F32), ALU.subtract).then_inc(S("hid_split"), 1)
                dve.wait_ge(S("up_freed"), me.nth("up_freed", 2 * FT))
                dve.wait_ge(S("hid_ready"), me.nth("hid_ready", FT))
                residual(l, n, G2, 3)
                dve.wait_ge(S("wo_freed"), me.nth("wo_freed", KS))
            stats(T, MS2)
            for s in range(KS):
                V.scalar_tensor_tensor(X[:, s, 0:T], X[:, s, 0:T], prm_col("fin2", s), MS2[:, 3, 0:T],
                                       ALU.mult, ALU.mult).then_inc(S("x_new"), 1)


def fm_units(w, cols):
    cols = np.asarray(cols)
    t = np.zeros((w.shape[0], P), np.float32)
    ok = cols >= 0
    t[:, :len(cols)][:, ok] = w[:, cols[ok]]
    t = t.reshape(-1, P, P).transpose(1, 0, 2)
    return [t[:, s:s + 8].reshape(P, -1) for s in range(0, t.shape[1], 8)]


def tm_units(w):
    t = w.reshape(KS, P, -1).transpose(1, 0, 2)
    return [t[:, s:s + 2].reshape(P, -1) for s in range(0, KS, 2)]


def columns1():
    o = np.cumsum([0, 256, 256, 256, 256, 256, 512, 512, 512, 512, 256, 64, 4])
    val, glu, cg, pin, pg, q, k, v, ag, qi, ki, wi = o[:12]
    base = {"q": q, "k": k, "qi": qi, "val": val, "glu": glu, "cgate": cg, "pin": pin, "pgate": pg, "agate": ag}
    out = []
    for t, name in enumerate(TILES1):
        if name == "ki":
            out.append(np.concatenate([ki + np.arange(64)] * 2))
        elif name == "wi":
            out.append(np.concatenate([wi + np.arange(4), np.full(124, -1)]))
        else:
            out.append(base[name] + (t - Z1[name]) * P + np.arange(P))
    return out, v


def columns2():
    o = np.cumsum([0, 192, 192, 384, 16, 16, 384, 256, 256, 256, 384, 384, 384])
    q, k, v, lf, lb, r, sb_, sc_, sx, nq, nk, nv = o[:12]
    base = {"nk": nk, "nq": nq, "r": r, "scb": sb_, "scc": sc_, "scx": sx}
    pad = np.full(16, -1)
    out = []
    for t, name in enumerate(TILES2):
        if name == "gqa":
            out.append(q + np.arange(P))
        elif name == "gka":
            out.append(k + np.arange(P))
        elif name == "gqk":
            out.append(np.concatenate([q + P + np.arange(64), k + P + np.arange(64)]))
        elif name == "glr":
            out.append(np.concatenate([lf + np.arange(16), pad, lb + np.arange(16), np.full(80, -1)]))
        else:
            out.append(base[name] + (t - Z2[name]) * P + np.arange(P))
    return out, v, nv


def constants():
    f = np.float32
    cc, c1, c2 = np.zeros((P, NCC), f), np.zeros((P, NC1), f), np.zeros((P, NC2), f)

    def put(arr, table, name, value):
        a, n = table[name]
        arr[:, a:a + n] = value

    i = np.arange(P)
    put(cc, CC, "ident", np.eye(P))
    put(cc, CC, "ones", 1.0 / D)
    put(cc, CC, "ones256", 1.0 / CONV_W)
    put(cc, CC, "blk", (i[:, None] // 64 == i[None, :] // 64) / 64.0)
    comb = np.zeros((P, 2))
    comb[[0, 2], 0] = 1.0
    comb[[1, 3], 1] = 1.0
    put(cc, CC, "comb", comb)
    put(cc, CC, "glrone", ((i == 16) | (i == 48))[:, None])

    perm = np.zeros((P, P))
    for d in range(P):
        if d % 64 < 32:
            perm[d + 32, d] = -1.0
        else:
            perm[d - 32, d] = 1.0
    put(c1, C1, "perm", perm)
    t = np.arange(T)
    inv = (f(10000.0) ** (-np.arange(32, dtype=f) / f(32))).astype(f)
    ang = (inv[i % 32][:, None] * t.astype(f)[None, :]).astype(f)
    put(c1, C1, "cos", np.cos(ang))
    put(c1, C1, "sin", np.sin(ang))
    put(c1, C1, "causal", np.concatenate([np.where(t[None, :] <= qt * P + i[:, None], 0.0, -1.0e30) for qt in range(TT)], 1))
    put(c1, C1, "icnt", np.concatenate([1.0 / np.minimum(t[None, :] + 1, np.array(POOL_WINDOWS)[2 * m + i // 64][:, None])
                                        for m in range(2)], 1))

    perm = np.zeros((P, P))
    perm[i[1::2], i[0::2]] = -1.0
    perm[i[0::2], i[1::2]] = 1.0
    put(c2, C2, "perm", perm)
    inv = (f(10000.0) ** (-np.arange(8, dtype=f) / f(8))).astype(f)
    ang = np.concatenate([(t // 64).astype(f)[:, None] * inv, (t % 64).astype(f)[:, None] * inv], 1).astype(f)
    ang = ang.T[(i % 32) // 2]
    put(c2, C2, "cos", np.cos(ang))
    put(c2, C2, "sin", np.sin(ang))
    put(c2, C2, "rep", i[:, None] % 32 == i[None, :] % 32)
    tri = (i[:, None] <= i[None, :]) / 16.0
    put(c2, C2, "uf", np.concatenate([tri, np.full((P, P), 1 / 16.0)], 1))
    put(c2, C2, "ub", np.concatenate([np.full((P, P), 1 / 16.0), tri.T], 1))
    c = i[:, None] // CH
    put(c2, C2, "capkf", np.where(i[None, :] < CH * (c + 1), CAP, -200.0))
    put(c2, C2, "capkb", np.where(i[None, :] >= CH * c, CAP, -200.0))
    put(c2, C2, "capq", np.where(i[None, :] // CH == c, CAP, -200.0))
    mf = (i[:, None] <= i[None, :]) * 1.0
    put(c2, C2, "mask", np.concatenate([mf, mf, mf.T, mf.T], 1))
    return cc, c1, c2


def bias_index():
    t = np.arange(T)
    r, c = t // 64, t % 64
    start = np.clip(c - 8, 0, 64 - 16)
    inside = (c[None, :] >= start[:, None]) & (c[None, :] < start[:, None] + 16)
    dr = r[None, :] - r[:, None] + 7
    dc = np.clip(c[None, :] - c[:, None] + 15, 0, 30)
    return dr, dc, inside


def kernel(**inp):
    import concourse.bacc as bacc
    from concourse.bass_utils import run_bass_kernel_spmd

    a = {k: np.ascontiguousarray(v) for k, v in inp.items()}
    f = np.float32
    ws = np.zeros((NU, P, UNIT), f)
    at = 0

    def put(units):
        nonlocal at
        for u in units:
            assert u.shape[1] == WIDTHS[at]
            ws[at, :, 0:u.shape[1]] = u
            at += 1

    def tiles(w, n=None):
        for m in range((w.shape[1] if n is None else n) // P):
            put(fm_units(w, m * P + np.arange(P)))

    for l in range(DEPTH):
        for n in range(12):
            put(tm_units(a["w_ada_2"][l][:, n * 512:(n + 1) * 512]))
    cols, v = columns1()
    for l in range(DEPTH):
        w = a["w_in"][l]
        put(tm_units(w[:, v:v + 512]))
        for c in cols:
            put(fm_units(w, c))
        tiles(a["w_out"][l])
        pw = a["ple_w"][l].reshape(2, P, KS, P).transpose(1, 2, 0, 3)
        put([pw[:, 4 * u:4 * u + 4].reshape(P, -1) for u in range(2)])
        tiles(a["ple_gate_w"][l])
    cols2, v, nv = columns2()
    for l in range(DEPTH):
        w = a["w_in_2"][l]
        put(tm_units(w[:, v:v + VW]))
        put(tm_units(w[:, nv:nv + VW]))
        for c in cols2:
            put(fm_units(w, c))
        tiles(a["w_out_2"][l])
        for m in range(FT):
            for o in (0, FFN):
                put(fm_units(a["ffn_w_up_2"][l], o + m * P + np.arange(P)))
        tiles(a["ffn_w_down_2"][l])
    assert at == NU

    prm = np.zeros((P, NPC), f)

    def par(name, vec):
        vec = vec.reshape(-1, P).T
        prm[:, PC[name]:PC[name] + vec.shape[1]] = vec

    for l in range(DEPTH):
        par(f"norm{l}", a["norm_g"][l])
        b = a["b_in"][l]
        par(f"bin{l}", np.concatenate([np.where(c >= 0, b[c], f(0)) for c in cols]))
        prm[:, PC[f"dww{l}"]:PC[f"dww{l}"] + 62] = a["conv_dw_w"][l].reshape(CONV_K, 2, P).transpose(2, 1, 0).reshape(P, 62)
        for name, src in (("dwb", "conv_dw_b"), ("lng", "conv_ln_g"), ("lnb", "conv_ln_b"), ("pwb", "conv_pw_b"),
                          ("poolb", "pool_b"), ("pools", "pool_scale"), ("nmix", "norm_mix_g_2"), ("nffn", "norm_ffn_g_2"),
                          ("bada", "b_ada_2"), ("scbias", "sc_conv_b_2"), ("fb", "ffn_conv_b_2"), ("scw", "sc_conv_w_2"),
                          ("fw", "ffn_conv_w_2")):
            par(f"{name}{l}", a[src][l])
        par(f"glag{l}", np.concatenate([a["gla_norm_g_2"][l]] * 2))
    par("fin1", a["final_norm_g"])
    par("fin2", a["final_norm_g_2"])
    cv = np.stack([a["c_2"][0], a["c_ctx_2"]], 1)
    prm[:, PC["cvec"]:] = cv.reshape(KS, P, 2).transpose(1, 0, 2).reshape(P, 2 * KS)

    mat1 = np.zeros((DEPTH, P, 768), f)
    mat1[:, :, 0:512] = a["conv_pw_w"].reshape(DEPTH, 2, P, 256).transpose(0, 2, 1, 3).reshape(DEPTH, P, 512)
    for g in range(4):
        r, o = 64 * (g % 2), 512 + P * (g // 2) + 64 * (g % 2)
        mat1[:, r:r + 64, o:o + 64] = a["pool_w"][:, g]
    wgp = np.zeros((DEPTH, 64, 192), f)
    wgp[:, 0:16], wgp[:, 16] = a["gla_wg2_fw_2"], a["gla_bg_fw_2"]
    wgp[:, 32:48], wgp[:, 48] = a["gla_wg2_bw_2"], a["gla_bg_bw_2"]
    dr, dc, inside = bias_index()
    nab = np.where(inside, a["na_rpb_2"][:, :, dr, dc], f(-1.0e30)).astype(f)
    nab = np.ascontiguousarray(nab.reshape(DEPTH, NAH, TT, P, T).transpose(0, 1, 3, 2, 4))

    def slabs(x):
        return x.T.reshape(-1, P, x.shape[0]).transpose(1, 0, 2)

    xt = np.ascontiguousarray(np.concatenate([slabs(a["x"][0]), slabs(a["ctx_2"][0])], 2))
    ptin = np.ascontiguousarray(np.stack([slabs(a["p"][l, 0]) for l in range(DEPTH)]))
    bv1 = np.ascontiguousarray(a["b_in"][:, columns1()[1]:columns1()[1] + 512])
    cc, c1, c2 = constants()

    nc = bacc.Bacc("TRN2", target_bir_lowering=False, num_devices=1)
    arrays = dict(ws=ws, prm=prm, cc=cc, c1=c1, c2=c2, xt=xt, ptin=ptin, mat1=mat1, bv1=bv1, wgp=wgp, nab=nab)
    aps = {k: nc.dram_tensor(f"in_{k}", v.shape, F32, kind="ExternalInput").ap() for k, v in arrays.items()}
    out = nc.dram_tensor("out_x", (P, KS, T), F32, kind="ExternalOutput").ap()
    build(nc, out=out, **aps)
    r = run_bass_kernel_spmd(nc, [{f"in_{k}": v for k, v in arrays.items()}], core_ids=[0])
    y = r.results[0]["out_x"]
    return np.ascontiguousarray(y.transpose(2, 1, 0).reshape(1, T, D))
```

```python
from contextlib import ExitStack

import numpy as np

import concourse.bass as bass
from concourse import mybir

F32 = mybir.dt.float32
F32R = mybir.dt.float32r
ALU = mybir.AluOpType
ACT = mybir.ActivationFunctionType
AX_X = mybir.AxisListType.X

P = 128
T = 256
TC = 512
TT = T // P
D = 1024
KS = D // P
DEPTH = 2
UNIT = 1024
EPS = 1e-6

CONV_W, CONV_K, POOL_W = 256, 31, 256
POOL_WINDOWS = (2, 4, 8, 16)
HD, NH1 = 64, 8
IDXH = 4
TOPK = T // 4
PLE = 256
TILES1 = ["q"] * 4 + ["k"] * 4 + ["qi"] * 2 + ["ki", "wi"] + ["val"] * 2 + ["glu"] * 2 + \
    ["cgate"] * 2 + ["pin"] * 2 + ["pgate"] * 2 + ["agate"] * 4
Z1 = {n: TILES1.index(n) for n in TILES1}
NZ1 = len(TILES1)

GH, GDK, GDV = 6, 32, 64
NAH = 6
FFN = 2816
FT = FFN // P
CH = 32
NCH = P // CH
CAP = 80.0
TILES2 = ["gqa", "gka", "gqk", "glr"] + ["nk"] * 3 + ["nq"] * 3 + ["r"] * 3 + ["scb"] * 2 + \
    ["scc"] * 2 + ["scx"] * 2
Z2 = {n: TILES2.index(n) for n in TILES2}
NZ2 = len(TILES2)
LAT_ONLY = ("nq", "r", "scb", "scc", "scx")
VW = 384

def param_columns():
    cols, at = {}, 0
    def add(name, n):
        nonlocal at
        cols[name] = at
        at += n
    for l in range(DEPTH):
        for name, n in (("norm", KS), ("bin", NZ1), ("dww", 2 * CONV_K), ("dwb", 2), ("lng", 2), ("lnb", 2),
                        ("pwb", 2), ("poolb", 2), ("pools", 2)):
            add(f"{name}{l}", n)
    add("fin1", KS)
    for l in range(DEPTH):
        for name, n in (("nmix", KS), ("nffn", KS), ("bada", 48), ("glag", 1), ("scw", 6), ("scbias", 2),
                        ("fw", 3 * 2 * FT), ("fb", 2 * FT)):
            add(f"{name}{l}", n)
    add("fin2", KS)
    add("cvec", 2 * KS)
    return cols, at


PC, NPC = param_columns()

ROW_U = 4
ROW_TILES = 12


def unit_widths():
    w, plain = [], []

    def add(widths):
        w.extend(widths)
        plain.extend([False] * len(widths))

    def rows(n):
        w.extend([UNIT] * (n * ROW_U))
        plain.extend([True] * (n * ROW_U))

    for _ in range(DEPTH):
        rows(2)
        add([UNIT] * (4 + NZ1))
        rows(3)
        add([UNIT] * (KS + 2))
        rows(1)
        add([UNIT] * KS)
    rows(1)
    for l in range(DEPTH):
        rows(2 if l == 0 else 0)
        add([2 * VW] * 8 + [UNIT] * NZ2)
        rows(1 + GH if l == 0 else 0)
        add([UNIT] * KS)
        rows(2 if l == 0 else 0)
        add([UNIT] * 2 * FT + [UNIT, UNIT, 6 * P] * KS)
    return w, plain


WIDTHS, PLAIN = unit_widths()
NU = len(WIDTHS)
SPLIT_UNITS = [u for u in range(NU) if not PLAIN[u]]
SPLIT_NO = [sum(not p for p in PLAIN[:u]) for u in range(NU)]
RAW, SPL, AHEAD = 4, 3, 2

def layout(names):
    out, at = {}, 0
    for name, n in names:
        out[name] = (at, n)
        at += n
    return out, at


CC, NCC = layout([("ident", P), ("ones", P), ("ones256", P), ("blk", P), ("glrone", 1)])
C1, NC1 = layout([("perm", P), ("cos", T), ("sin", T), ("causal", 2 * T), ("icnt", 2 * T)])
C2, NC2 = layout([("perm", P), ("cos", T), ("sin", T), ("rep", P), ("uf", T), ("ub", T),
                  ("capkf", P), ("capkb", P), ("capq", P), ("mask", 4 * P)])


def build(nc, ws, prm, cc, c1, c2, xt, ptin, mat1, bv1, wgp, nab, out):
    with ExitStack() as ctx:
        sems = {}

        def S(name):
            if name not in sems:
                sems[name] = ctx.enter_context(nc.semaphore(name))
            return sems[name]

        def sb(stack, name, shape, dt=F32):
            return stack.enter_context(nc.sbuf_tensor(name, shape, dt))

        X = sb(ctx, "X", [P, KS, TC])
        NHI = sb(ctx, "NHI", [P, KS, TC], F32R)
        NLO = sb(ctx, "NLO", [P, KS, TC], F32R)
        RAWB = sb(ctx, "RAWB", [P, RAW, UNIT])
        WHI = sb(ctx, "WHI", [P, SPL, UNIT], F32R)
        WLO = sb(ctx, "WLO", [P, SPL, UNIT], F32R)
        CST = sb(ctx, "CST", [P, NCC])
        PRM = sb(ctx, "PRM", [P, NPC])
        MOD = sb(ctx, "MOD", [P, DEPTH, 48, 2])
        GM = sb(ctx, "GM", [P, KS, 2])
        CV2 = sb(ctx, "CV2", [P, KS, 2])
        ROWS = sb(ctx, "ROWS", [2, 512])

        def cst(name):
            a, n = CC[name]
            return CST[:, a:a + n]

        def prm_col(name, i=0, n=1):
            a = PC[name] + i
            return PRM[:, a:a + n]

        st = ExitStack()
        K1 = sb(st, "K1", [P, NC1])
        Z = sb(st, "Z", [P, NZ1, T])
        V1 = sb(st, "V1", [P, TT, 512])
        BV = sb(st, "BV", [P, 512])
        M1 = sb(st, "M1", [P, 768])
        PLEH = sb(st, "PLEH", [P, 2, 2, T], F32R)
        PIN = sb(st, "PIN", [P, 2, T])
        RT = sb(st, "RT", [P, 512])
        WI = sb(st, "WI", [P, TT, IDXH])
        RL = sb(st, "RL", [P, 2, T])
        SC = sb(st, "SC", [P, TT, T])
        MB = sb(st, "MB", [P, TT, T])
        M8 = sb(st, "M8", [P, 8])
        L1 = sb(st, "L1", [P, 3, T])
        P1 = sb(st, "P1", [P, 3, T])
        PT1 = sb(st, "PT1", [P, 2, T])
        ST1 = sb(st, "ST1", [P, 3, 4])
        OB = sb(st, "OB", [P, 4, T])
        UP = sb(st, "UP", [P, 2, CONV_K - 1 + T])
        CV = sb(st, "CV", [P, 2, T])
        CT = sb(st, "CT", [P, 2, T])
        PD = sb(st, "PD", [P, 2, T])
        PP = sb(st, "PP", [P, 2, 16 + T])
        PS = sb(st, "PS", [P, 4, 2, 16 + T])
        PB = sb(st, "PB", [P, 2])
        GT1 = sb(st, "GT1", [P, 8, T])
        SG = sb(st, "SG", [P, 2, T])
        Y1 = sb(st, "Y1", [P, KS, T])
        MS1 = sb(st, "MS1", [P, 4, T])
        st.close()

        mix = ExitStack()
        K2 = sb(mix, "K2", [P, NC2])
        ZB = sb(mix, "ZB", [P, NZ2, TC])
        V2 = sb(mix, "V2", [P, 4, 2 * VW])
        st = ExitStack()
        WG = sb(st, "WG", [64, 192])
        GT = sb(st, "GT", [P, 4, VW])
        GTA = sb(st, "GTA", [P, 4, VW])
        KQ = sb(st, "KQ", [P, 2, TC])
        BM = sb(st, "BM", [P, 2, 6])
        EX = sb(st, "EX", [P, 1280])
        EY = sb(st, "EY", [P, 2, 1280])
        E0 = sb(st, "E0", [64, TC])
        AM = sb(st, "AM", [P, TC])
        AF = sb(st, "AF", [P, 2, 2, T])
        A0 = sb(st, "A0", [P, 2, T])
        OG = sb(st, "OG", [P, TC])
        OM = sb(st, "OM", [P, 4, TC])
        st.close()
        st = ExitStack()
        NB = sb(st, "NB", [P, 2, TT, TC])
        L2 = sb(st, "L2", [P, 3, TC])
        P2 = sb(st, "P2", [P, 3, TC])
        PT2 = sb(st, "PT2", [P, 2, TC])
        ST2 = sb(st, "ST2", [P, 3, 4])
        OY = sb(st, "OY", [P, 3, TC])
        st.close()
        mix.close()
        st = ExitStack()
        SQ2 = sb(st, "SQ2", [P, KS, TC])
        TB2 = sb(st, "TB2", [P, KS, TC])
        MS2 = sb(st, "MS2", [P, 4, TC])
        st.close()
        st = ExitStack()
        HHI = sb(st, "HHI", [P, FT, TC], F32R)
        HLO = sb(st, "HLO", [P, FT, TC], F32R)
        CF = sb(st, "CF", [P, 2, 3, TC])
        st.close()

        bank = [ctx.enter_context(nc.psum_tensor(f"bank{i}", [P, 512], F32)) for i in range(8)]

        def c1v(name):
            a, n = C1[name]
            return K1[:, a:a + n]

        def c2v(name):
            a, n = C2[name]
            return K2[:, a:a + n]

        def bc(ap, n):
            return ap.unsqueeze(1).broadcast_to([ap.shape[0], n, ap.shape[1]])

        def bl(ap, n):
            return ap.unsqueeze(2).broadcast_to([ap.shape[0], ap.shape[1], n])

        def half(h):
            return slice(64 * (h % 2), 64 * (h % 2) + 64)

        def gates4(i):
            g = GTA[:].rearrange("p a b -> p (a b)")[:, (i % 3) * 512:(i % 3 + 1) * 512]
            return g.rearrange("p (i c k) -> p i c k", i=4, c=NCH)

        def gate_part(g, i):
            s, d = i // 2, i % 2
            return g[:, 2 * s:2 * s + 2, d * 192:(d + 1) * 192]

        class Side:

            def __init__(self, eng, name):
                self.eng, self.name, self.seen, self.u, self.tile = eng, name, {}, 0, 0

            def nth(self, name, k=1):
                self.seen[name] = self.seen.get(name, 0) + k
                return self.seen[name]

            def next_tile(self):
                self.tile += 1
                return (self.tile - 1) % 4

        ITEMS1 = [(h, qt, P * (qt + 1), False) for h in range(NH1) for qt in range(TT)]

        def items2(uc):
            return [(h, qt, T if own else TC, own) for h in range(NAH) for own in ((False, True) if uc else (False,))
                    for qt in range(TT)]

        def ends_pair(it, uc=False):
            return it[0] % 2 == 1 and it[1] == TT - 1 and it[3] == uc

        SH1, SC1, G1, SH2, SC2, G2 = (KS * i for i in range(6))

        block = ctx.enter_context(nc.Block())

        @block.sync
        def _(sp):
            for u in range(NU):
                if u >= RAW:
                    if PLAIN[u - RAW]:
                        sp.wait_ge(S("unit_done"), u - RAW + 1)
                    else:
                        sp.wait_ge(S("lo_ready"), SPLIT_NO[u - RAW] + 1)
                w = WIDTHS[u]
                sp.dma_start(RAWB[:, u % RAW, 0:w], ws[u, :, 0:w]).then_inc(S(f"raw{u % RAW}"), 16)
            sp.wait_ge(S("x_new"), KS * (DEPTH + 2))
            sp.dma_start(out, X[:, :, 0:T]).then_inc(S("stored"), 16)
            sp.wait_ge(S("stored"), 16)

        @block.gpsimd
        def _(pool):
            me = Side(pool, "pool")

            pool.dma_start(PRM[:], prm).then_inc(S("ld_prm"), 16)
            pool.dma_start(CST[:], cc).then_inc(S("ld_cst"), 16)
            pool.dma_start(K1[:], c1).then_inc(S("ld_c1"), 16)
            for l in range(DEPTH):
                if l > 0:
                    pool.wait_ge(S("x_new"), me.nth("x_new", KS))
                pool.dma_start(BV[:], bv1[l:l + 1, :].broadcast_to([P, 512])).then_inc(S("ld_p1"), 16)
                pool.dma_start(M1[:], mat1[l]).then_inc(S("ld_p1"), 16)
                pool.dma_start(PIN[:], ptin[l]).then_inc(S("ld_p1"), 16)
                if l == 0:
                    pool.dma_start(X[:, :, T:TC], xt[:, :, T:TC]).then_inc(S("ld_ctx"), 16)
            pool.wait_ge(S("x_split"), me.nth("x_split", KS * DEPTH))
            pool.wait_ge(S("s_freed"), me.nth("s_freed", len(ITEMS1) * DEPTH))
            pool.wait_ge(S("y_split"), me.nth("y_split", KS * DEPTH))
            for l in range(DEPTH):
                pool.wait_ge(S("x_split"), me.nth("x_split", KS))
                pool.dma_start(K2[:], c2).then_inc(S("ld_c2"), 16)
                pool.dma_start(WG[:], wgp[l]).then_inc(S("ld_c2"), 16)
                pool.wait_ge(S("g_ready"), me.nth("g_ready", 4))
                for i in range(2 * GH):
                    h, d = i // 2, i % 2
                    if i >= 3:
                        pool.wait_ge(S("b_ready"), me.nth("b_ready"))
                    g = GT[:, :, d * 192 + h * GDK:d * 192 + (h + 1) * GDK]
                    nc.gpsimd.tensor_copy(gates4(i), g.unsqueeze(2).broadcast_to([P, 4, NCH, GDK])).then_inc(S("g4_ready"), 1)
                pool.wait_ge(S("b_ready"), me.nth("b_ready", 3))
                pool.wait_ge(S("y_split"), me.nth("y_split", 5))
                per_head = TT * (2 if l < DEPTH - 1 else 1)
                for h in range(NAH):
                    if h >= 2:
                        pool.wait_ge(S("s_freed"), me.nth("s_freed", per_head))
                    pool.dma_start(NB[:, h % 2, :, 0:T], nab[l, h]).then_inc(S(f"ld_nb{h % 2}"), 16)
                pool.wait_ge(S("s_freed"), me.nth("s_freed", 2 * per_head))
                pool.wait_ge(S("y_split"), me.nth("y_split", 3))
                pool.wait_ge(S("x_split"), me.nth("x_split", KS))

        @block.tensor
        def _(pe):
            me = Side(pe, "pe")
            held, made = {}, {}

            def read_by(b, freed):
                made[freed] = made.get(freed, 0) + 1
                held[b] = (S(freed), made[freed])

            def unit():
                u = me.u
                me.u += 1
                k = SPLIT_NO[u]
                pe.wait_ge(S("lo_ready"), k + 1)
                return WHI[:, k % SPL, :], WLO[:, k % SPL, :]

            def rows(b, s0=0, s1=KS):
                if s0 == 0 and b in held:
                    pe.wait_ge(*held[b])
                for s in range(s0, s1):
                    u = me.u
                    if s % 2 == 0:
                        pe.wait_ge(S(f"raw{u % RAW}"), 16 * (u // RAW + 1))
                    ins = nc.tensor.matmul(bank[b][0:2, :], CV2[:, s, :], RAWB[:, u % RAW, (s % 2) * 512:(s % 2 + 1) * 512],
                                           start=(s == 0), stop=(s == KS - 1))
                    if s % 2 == 1:
                        ins.then_inc(S("unit_done"), 1)
                        me.u += 1

            def columns(b):
                pe.wait_ge(S("rows_copied"), me.nth("rows_copied"))
                for j in range(4):
                    ins = nc.tensor.matmul(bank[b][:, 2 * j:2 * j + 2], ROWS[:, j * P:(j + 1) * P], cst("ident")[0:2, 0:2],
                                           start=True, stop=True)
                ins.then_inc(S("cols_ready"), 1)
                read_by(b, "mod_done")

            def fm(slabs, n, rhs, freed):
                b = me.next_tile()
                if b in held:
                    pe.wait_ge(*held[b])
                o = bank[b][:, 0:n]
                for s in range(slabs):
                    if s % 8 == 0:
                        hi, lo = unit()
                    w = slice((s % 8) * P, (s % 8 + 1) * P)
                    xh, xl = rhs(s)
                    nc.tensor.matmul(o, hi[:, w], xh, start=(s == 0), stop=False)
                    nc.tensor.matmul(o, hi[:, w], xl, start=False, stop=False)
                    ins = nc.tensor.matmul(o, lo[:, w], xh, start=False, stop=(s == slabs - 1))
                    if s % 8 == 7 and s != slabs - 1:
                        ins.then_inc(S("unit_done"), 1)
                ins.then_inc(S("unit_done"), 1)
                read_by(b, freed)

            def tm(tts, w):
                for b in range(tts):
                    if b in held:
                        pe.wait_ge(*held[b])
                for u in range(4):
                    hi, lo = unit()
                    for k in range(2):
                        s, c = 2 * u + k, slice(k * w, (k + 1) * w)
                        for t in range(tts):
                            o = bank[t][:, 0:w]
                            xh, xl = NHI[:, s, t * P:(t + 1) * P], NLO[:, s, t * P:(t + 1) * P]
                            nc.tensor.matmul(o, xh, hi[:, c], start=(s == 0), stop=False)
                            nc.tensor.matmul(o, xl, hi[:, c], start=False, stop=False)
                            ins = nc.tensor.matmul(o, xh, lo[:, c], start=False, stop=(s == 7))
                    ins.then_inc(S("unit_done"), 1)
                for b in range(tts):
                    read_by(b, "v_freed")

            def x_lat(s):
                return NHI[:, s, 0:T], NLO[:, s, 0:T]

            def x_all(s):
                return NHI[:, s, :], NLO[:, s, :]

            def stats(n, sq):
                if 4 in held:
                    pe.wait_ge(*held[4])
                for s in range(KS):
                    if s % 2 == 0:
                        pe.wait_ge(S("sq_ready"), me.nth("sq_ready"))
                    ins = nc.tensor.matmul(bank[4][:, 0:n], cst("ones"), sq[:, s, 0:n], start=(s == 0), stop=(s == KS - 1))
                ins.then_inc(S("ms_ready"), 1)
                read_by(4, "ms_eps")

            def attention(items, score, p, out, uc=False, between=None):
                n = len(items)
                for i in range(n + 3):
                    if i < n:
                        if i % 2 in held:
                            pe.wait_ge(*held[i % 2])
                        score(items[i], bank[i % 2]).then_inc(S("s_ready"), 1)
                        read_by(i % 2, "s_freed")
                    if between is not None:
                        between(i)
                    if 2 <= i < n + 2:
                        j = i - 2
                        b = 2 + j % 2
                        pe.wait_ge(S("p_ready"), me.nth("p_ready"))
                        if b in held:
                            pe.wait_ge(*held[b])
                        for k in range(items[j][2] // P):
                            ins = nc.tensor.transpose(bank[b][:, k * P:(k + 1) * P], p[:, j % 3, k * P:(k + 1) * P], cst("ident"))
                        ins.then_inc(S("pt_ready"), 1)
                        read_by(b, "pt_freed")
                    if i >= 3:
                        j = i - 3
                        h, qt, nk, own = it = items[j]
                        b = 6 + (h // 2) % 2
                        pe.wait_ge(S("pt_freed"), me.nth("pt_freed"))
                        if h % 2 == 0 and qt == 0 and not own:
                            if b in held:
                                pe.wait_ge(*held[b])
                        ins = out(j, it, bank[b])
                        if ends_pair(it, uc):
                            ins.then_inc(S("pv_done"), 1)
                            read_by(b, "o_freed")
                        else:
                            ins.then_inc(S("pv_done"), 1)

            pe.wait_ge(S("ld_cst"), 16)
            pe.wait_ge(S("c_ready"), me.nth("c_ready"))

            for l in range(DEPTH):
                if l > 0:
                    stats(T, Y1)
                rows(5)
                rows(6)
                if l == 0:
                    stats(T, Y1)
                columns(5)
                pe.wait_ge(S("x_split"), me.nth("x_split", KS))
                tm(TT, 512)
                columns(6)

                def rotate(g):
                    k, b = 2 if g < 5 else 1, 4 + g % 2
                    if b in held:
                        pe.wait_ge(*held[b])
                    ins = nc.tensor.matmul(bank[b][:, 0:k * T], c1v("perm"),
                                           Z[:, 2 * g:2 * g + k, :].rearrange("p a t -> p (a t)"), start=True, stop=True)
                    ins.then_inc(S("rot_ready"), 1)
                    read_by(b, "rot_freed")

                def index(i):
                    qt, h, b = i // IDXH, i % IDXH, 6 + i % 2
                    nk = P * (qt + 1)
                    if b in held:
                        pe.wait_ge(*held[b])
                    ins = nc.tensor.matmul(bank[b][:, 0:nk], Z[half(h), Z1["qi"] + h // 2, qt * P:(qt + 1) * P],
                                           Z[half(h), Z1["ki"], 0:nk], start=True, stop=True)
                    ins.then_inc(S("idx_ready"), 1)
                    read_by(b, "idx_freed")

                for t in range(NZ1):
                    fm(KS, T, x_lat, "z_freed")
                    if t == 12:
                        pe.wait_ge(S("ld_c1"), 16)
                        pe.wait_ge(S("z_freed"), me.nth("z_freed", 12))
                        rotate(4)
                        rotate(5)
                        for qt in range(TT):
                            if 6 + qt in held:
                                pe.wait_ge(*held[6 + qt])
                            ins = nc.tensor.transpose(bank[6 + qt][:, 0:P], Z[:, Z1["wi"], qt * P:(qt + 1) * P], cst("ident"))
                            ins.then_inc(S("wi_ready"), 1)
                            read_by(6 + qt, "wi_freed")
                    if t in (13, 14):
                        rotate(t - 13)
                    if t == 15:
                        pe.wait_ge(S("qi_roped"), me.nth("qi_roped"))
                    if 15 <= t < 19:
                        index(2 * (t - 15))
                        index(2 * (t - 15) + 1)
                    if t in (21, 22):
                        rotate(t - 19)
                pe.wait_ge(S("ld_p1"), 16 * (3 * l + 3))
                pe.wait_ge(S("z_freed"), me.nth("z_freed", NZ1 - 12))
                pe.wait_ge(S("rope_done"), me.nth("rope_done"))

                def score1(it, bk):
                    h, qt, nk, _ = it
                    return nc.tensor.matmul(bk[:, 0:nk], Z[half(h), Z1["q"] + h // 2, qt * P:(qt + 1) * P],
                                            Z[half(h), Z1["k"] + h // 2, 0:nk], start=True, stop=True)

                def pv1(j, it, bk):
                    h, qt, nk, _ = it
                    for kt in range(nk // P):
                        ins = nc.tensor.matmul(bk[half(h), qt * P:(qt + 1) * P], V1[:, kt, h * HD:(h + 1) * HD],
                                               PT1[:, j % 2, kt * P:(kt + 1) * P], start=(kt == 0), stop=(kt == nk // P - 1))
                    return ins

                def mod1(i):
                    if i < 2 * KS:
                        rows(4 + i // KS, i % KS, i % KS + 1)
                    if i == 2 * KS:
                        columns(4)

                attention(ITEMS1, score1, P1, pv1, between=mod1)
                pe.wait_ge(S("pool_ready"), me.nth("pool_ready"))
                for m in range(2):
                    if 2 + m in held:
                        pe.wait_ge(*held[2 + m])
                    ins = nc.tensor.matmul(bank[2 + m][:, 0:T], M1[:, 512 + m * P:512 + (m + 1) * P], PD[:, m, :],
                                           start=True, stop=True)
                    ins.then_inc(S("pw_ready"), 1)
                    read_by(2 + m, "pw_freed")
                for src, given, freed in ((CV, "conv_ready", "xc_ready"), (CT, "conv_sq", "cvar_eps")):
                    pe.wait_ge(S(given), me.nth(given))
                    if 4 in held:
                        pe.wait_ge(*held[4])
                    for k in range(2):
                        ins = nc.tensor.matmul(bank[4][:, 0:T], cst("ones256"), src[:, k, :], start=(k == 0), stop=(k == 1))
                    ins.then_inc(S("cstat_ready"), 1)
                    read_by(4, freed)
                    if src is CV:
                        columns(5)
                rows(6)
                pe.wait_ge(S("conv_silu"), me.nth("conv_silu"))
                for m in range(2):
                    if m in held:
                        pe.wait_ge(*held[m])
                    for k in range(2):
                        ins = nc.tensor.matmul(bank[m][:, 0:T], M1[:, k * T + m * P:k * T + (m + 1) * P], CV[:, k, :],
                                               start=(k == 0), stop=(k == 1))
                    ins.then_inc(S("pw_ready"), 1)
                    read_by(m, "pw_freed")
                columns(6)
                pe.wait_ge(S("y_split"), me.nth("y_split", KS))
                for m in range(KS):
                    fm(KS, T, x_lat, "wo_freed")
                pe.wait_ge(S("ple_split"), me.nth("ple_split"))
                for u in range(2):
                    hi, lo = unit()
                    for j in range(4):
                        b = me.next_tile()
                        if b in held:
                            pe.wait_ge(*held[b])
                        for k in range(2):
                            w = slice((2 * j + k) * P, (2 * j + k + 1) * P)
                            nc.tensor.matmul(bank[b][:, 0:T], hi[:, w], PLEH[:, 0, k, :], start=(k == 0), stop=False)
                            nc.tensor.matmul(bank[b][:, 0:T], hi[:, w], PLEH[:, 1, k, :], start=False, stop=False)
                            ins = nc.tensor.matmul(bank[b][:, 0:T], lo[:, w], PLEH[:, 0, k, :], start=False, stop=(k == 1))
                        ins.then_inc(S("unit_done" if j == 3 else "ple_ready"), 1)
                        read_by(b, "ple_freed")
                rows(5)
                pe.wait_ge(S("h_split"), me.nth("h_split", KS))
                for m in range(KS):
                    fm(KS, T, lambda s: (NHI[:, s, T:TC], NLO[:, s, T:TC]), "gate_freed")
                    if m == 0:
                        columns(5)
            stats(T, Y1)
            rows(5)

            for l in range(DEPTH):
                uc = l < DEPTH - 1
                n, rhs = (TC, x_all) if uc else (T, x_lat)
                stats(TC, SQ2)
                if l == 0:
                    columns(5)
                    rows(6)
                    rows(7)
                    columns(6)
                pe.wait_ge(S("x_split"), me.nth("x_split", KS))
                for v in range(2):
                    tm(4, VW)
                    if l == 0 and v == 0:
                        columns(7)
                for name in TILES2:
                    lat = name in LAT_ONLY and not uc
                    fm(KS, T if lat else TC, x_lat if lat else x_all, "z_freed")
                pe.wait_ge(S("ld_c2"), 16 * 2 * (l + 1))
                pe.wait_ge(S("z_freed"), me.nth("z_freed", NZ2))
                for t in range(3):
                    if t % 2 in held:
                        pe.wait_ge(*held[t % 2])
                    ins = nc.tensor.matmul(bank[t % 2][:, 0:T], c2v("perm"), ZB[:, t, 0:T], start=True, stop=True)
                    ins.then_inc(S("rot_ready"), 1)
                    read_by(t % 2, "rot_freed")
                for i in range(4):
                    s, d = i // 2, i % 2
                    if 2 + d in held:
                        pe.wait_ge(*held[2 + d])
                    r = slice(32 * d, 32 * d + 17)
                    for t in range(2):
                        ins = nc.tensor.matmul(bank[2 + d][:, t * 192:(t + 1) * 192],
                                               ZB[r, Z2["glr"], (2 * s + t) * P:(2 * s + t + 1) * P], WG[r, :],
                                               start=True, stop=True)
                    ins.then_inc(S("gate_ready"), 1)
                    read_by(2 + d, "g_ready")
                if uc:
                    rows(5)
                pe.wait_ge(S("rope_done"), me.nth("rope_done"))
                pe.wait_ge(S("g_ready"), me.nth("g_ready", 4))
                for h in range(GH):
                    for d in range(2):
                        pe.wait_ge(S("g4_ready"), me.nth("g4_ready"))
                        if 2 + d in held:
                            pe.wait_ge(*held[2 + d])
                        u = c2v("uf") if d == 0 else c2v("ub")
                        for s in range(2):
                            for k in range(2):
                                t = k if d == 0 else 1 - k
                                lhs = gates4(2 * h + d)[:, 2 * s + t, :, :].rearrange("p c k -> p (c k)")
                                if k == 0:
                                    o, r = bank[2 + d][:, s * T:(s + 1) * T], u
                                elif d == 0:
                                    o, r = bank[2 + d][:, s * T + P:(s + 1) * T], u[:, 0:P]
                                else:
                                    o, r = bank[2 + d][:, s * T:s * T + P], u[:, P:T]
                                ins = nc.tensor.matmul(o, lhs, r, start=(k == 0), stop=(k == 1))
                        ins.then_inc(S("b_ready"), 1)
                        read_by(2 + d, "b_copied")
                    for w in range(2):
                        if h < 4:
                            t, r0 = 1 - w, 32 * h
                        else:
                            t, r0 = 2, 32 * (h - 4) + (64 if w == 0 else 0)
                        if w in held:
                            pe.wait_ge(*held[w])
                        ins = nc.tensor.matmul(bank[w][:], c2v("rep")[r0:r0 + 32, :], ZB[r0:r0 + 32, t, :], start=True, stop=True)
                        ins.then_inc(S("kq_ready"), 1)
                        read_by(w, "kq_freed")
                    other = 6 + (h // 2 + 1) % 2
                    if uc:
                        if h == 0:
                            columns(5)
                        rows(other)
                    pe.wait_ge(S("dec_ready"), me.nth("dec_ready", 2))
                    seqs = 2 if uc else 1
                    for s in range(seqs):
                        if 4 + s in held:
                            pe.wait_ge(*held[4 + s])
                        for d in range(2):
                            for t in range(2):
                                i = 2 * s + t
                                ins = nc.tensor.matmul(bank[4 + s][:, (2 * d + t) * P:(2 * d + t + 1) * P],
                                                       EY[:, d, 512 + i * P:512 + (i + 1) * P], EY[:, d, i * P:(i + 1) * P],
                                                       start=True, stop=True)
                        ins.then_inc(S("a_ready"), 1)
                        read_by(4 + s, "am_read")
                    if 0 in held:
                        pe.wait_ge(*held[0])
                    for s in range(seqs):
                        for d in range(2):
                            i = 2 * s + (1 - d)
                            ins = nc.tensor.matmul(bank[0][:, (2 * s + d) * P:(2 * s + d + 1) * P],
                                                   EY[:, d, 1024 + s * P:1024 + (s + 1) * P], EY[:, d, i * P:(i + 1) * P],
                                                   start=True, stop=True)
                    ins.then_inc(S("ax_ready"), 1)
                    read_by(0, "ax_freed")
                    if 1 in held:
                        pe.wait_ge(*held[1])
                    for t in range(2):
                        ins = nc.tensor.matmul(bank[1][:, t * T:(t + 1) * T], E0[:, T + t * P:T + (t + 1) * P],
                                               E0[:, 0:T], start=True, stop=True)
                    ins.then_inc(S("ax_ready"), 1)
                    read_by(1, "ax_freed")
                    if uc:
                        columns(other)
                    pe.wait_ge(S("af_ready"), me.nth("af_ready", seqs))
                    pe.wait_ge(S("ax_freed"), me.nth("ax_freed", 2))
                    b, r, vh = 6 + (h // 2) % 2, half(h), slice(h * GDV, (h + 1) * GDV)
                    if h % 2 == 0:
                        if b in held:
                            pe.wait_ge(*held[b])
                    for t in range(2):
                        nc.tensor.matmul(bank[b][r, 0:T], V2[:, t, vh], AF[:, 0, t, :], start=(t == 0), stop=False)
                    for t in range(2):
                        ins = nc.tensor.matmul(bank[b][r, 0:T], V2[:, 2 + t, vh], A0[:, t, :], start=False, stop=(t == 1))
                    if uc:
                        for t in range(2):
                            ins = nc.tensor.matmul(bank[b][r, T:TC], V2[:, 2 + t, vh], AF[:, 1, t, :],
                                                   start=(t == 0), stop=(t == 1))
                    if h % 2 == 0:
                        ins.then_inc(S("gpv_done"), 1)
                    else:
                        ins.then_inc(S("gpv_done"), 1)
                        read_by(b, "og_read")
                        pe.wait_ge(S("osq_ready"), me.nth("osq_ready"))
                        if 5 in held:
                            pe.wait_ge(*held[5])
                        ins = nc.tensor.matmul(bank[5][:, 0:n], cst("blk"), OM[:, 0, 0:n], start=True, stop=True)
                        ins.then_inc(S("oms_ready"), 1)
                        read_by(5, "oms_eps")

                def score2(it, bk):
                    h, qt, nk, own = it
                    o = T if own else 0
                    return nc.tensor.matmul(bk[:, 0:nk], ZB[half(h), Z2["nq"] + h // 2, o + qt * P:o + (qt + 1) * P],
                                            ZB[half(h), Z2["nk"] + h // 2, o:TC], start=True, stop=True)

                def pv2(j, it, bk):
                    h, qt, nk, own = it
                    o, k0 = (T, 2) if own else (0, 0)
                    for kt in range(nk // P):
                        ins = nc.tensor.matmul(bk[half(h), o + qt * P:o + (qt + 1) * P],
                                               V2[:, k0 + kt, VW + h * 64:VW + (h + 1) * 64],
                                               PT2[:, j % 2, kt * P:(kt + 1) * P], start=(kt == 0), stop=(kt == nk // P - 1))
                    return ins

                attention(items2(uc), score2, P2, pv2, uc)
                pe.wait_ge(S("y_split"), me.nth("y_split", KS))
                for m in range(KS):
                    fm(KS, n, rhs, "wo_freed")
                stats(n, SQ2)
                if uc:
                    rows(5)
                    rows(6)
                    columns(5)
                pe.wait_ge(S("x_split"), me.nth("x_split", KS))
                for m in range(2 * FT):
                    fm(KS, n, rhs, "up_freed")
                    if uc and m == 1:
                        columns(6)
                pe.wait_ge(S("hid_split"), me.nth("hid_split", FT))
                for m in range(KS):
                    fm(FT, n, lambda s: (HHI[:, s, 0:n], HLO[:, s, 0:n]), "wo_freed")
            stats(T, SQ2)

        @block.scalar
        def _(act):
            me = Side(act, "act")
            split = 0

            def A(out, in_, func=ACT.Copy, **kw):
                return nc.scalar.activation(out, in_, func, **kw)

            def split_to(n):
                nonlocal split
                while split < min(n, NU):
                    u, k = split, SPLIT_NO[split]
                    split += 1
                    if PLAIN[u]:
                        continue
                    act.wait_ge(S(f"raw{u % RAW}"), 16 * (u // RAW + 1))
                    if k >= SPL:
                        act.wait_ge(S("unit_done"), SPLIT_UNITS[k - SPL] + 1)
                    w = WIDTHS[u]
                    A(WHI[:, k % SPL, 0:w], RAWB[:, u % RAW, 0:w]).then_inc(S("hi_ready"), 1)

            def rest(n=1):
                for _ in range(n):
                    me.u += 1
                    split_to(me.u + AHEAD)

            def plain(n):
                me.u += n

            def ahead():
                split_to(me.u + AHEAD)

            def unit(n=1):
                rest(n)
                act.wait_ge(S("unit_done"), me.u)

            def copy_rows(b, u):
                act.wait_ge(S("unit_done"), u)
                if made_rows[0] > 0:
                    act.wait_ge(S("cols_ready"), me.nth("cols_ready"))
                made_rows[0] += 1
                A(ROWS[:], bank[b][0:2, :]).then_inc(S("rows_copied"), 1)

            made_rows = [0]

            def stats(n, ms, sq):
                for s in range(0, KS, 2):
                    A(sq[:, s:s + 2, 0:n], X[:, s:s + 2, 0:n], ACT.Square).then_inc(S("sq_ready"), 1)
                act.wait_ge(S("ms_eps"), me.nth("ms_eps"))
                A(ms[:, 1, 0:n], ms[:, 0, 0:n], ACT.Ln).then_inc(S("act_chain"), 1)
                act.wait_ge(S("act_chain"), me.nth("act_chain"))
                A(ms[:, 2, 0:n], ms[:, 1, 0:n], ACT.Exp, scale=-0.5).then_inc(S("rs_guess"), 1)

            def split_hi(n, src, o, given, slabs=range(KS)):
                for s in slabs:
                    act.wait_ge(S(given), me.nth(given))
                    A(NHI[:, s, o:o + n], src[:, s, 0:n]).then_inc(S("xh_ready"), 1)

            def softmax(items, lbuf, pbuf, ptbuf, stb, scale, done, between=None):
                n = len(items)
                for i in range(n + 2):
                    if i < n:
                        k, nk = i % 3, items[i][2]
                        act.wait_ge(S("l_ready"), me.nth("l_ready"))
                        A(pbuf[:, k, 0:nk], lbuf[:, k, 0:nk], ACT.Exp, bias=stb[:, k, 1:2], scale=scale,
                          accum_out=stb[:, k, 2:3]).then_inc(S("e_ready"), 1)
                    if between is not None:
                        between(i)
                    if i >= 2:
                        j = i - 2
                        act.wait_ge(S("pt_ready"), me.nth("pt_ready"))
                        if j >= 2:
                            act.wait_ge(S("pv_done"), me.nth("pv_done"))
                            done(items[j - 2])
                        A(ptbuf[:, j % 2, 0:items[j][2]], bank[2 + j % 2][:, 0:items[j][2]]).then_inc(S("pt_freed"), 1)
                for j in (n - 2, n - 1):
                    act.wait_ge(S("pv_done"), me.nth("pv_done"))
                    done(items[j])

            act.dma_start(X[:, :, 0:T], xt[:, :, 0:T]).then_inc(S("ld_x"), 16)
            act.wait_ge(S("ld_prm"), 16)
            A(CV2[:], prm_col("cvec", 0, 2 * KS).rearrange("p (s c) -> p s c", c=2), ACT.Silu).then_inc(S("c_ready"), 1)

            act.wait_ge(S("ld_x"), 16)
            for l in range(DEPTH):
                stats(T, MS1, Y1)
                plain(2 * ROW_U)
                first_u = me.u
                copy_rows(5, first_u - ROW_U)
                ahead()
                split_hi(T, Y1, 0, "t_ready")
                copy_rows(6, first_u)
                rest(4)
                for t in range(NZ1):
                    unit()
                    A(Z[:, t, :], bank[me.next_tile()][:, 0:T], ACT.Identity, bias=prm_col(f"bin{l}", t)).then_inc(S("z_freed"), 1)
                    if t == 12:
                        for qt in range(TT):
                            act.wait_ge(S("wi_ready"), me.nth("wi_ready"))
                            A(WI[:, qt, :], bank[6 + qt][:, 0:IDXH]).then_inc(S("wi_freed"), 1)
                    if 15 <= t < 19:
                        for i in (2 * (t - 15), 2 * (t - 15) + 1):
                            nk = P * (i // IDXH + 1)
                            act.wait_ge(S("idx_ready"), me.nth("idx_ready"))
                            if i >= 2:
                                act.wait_ge(S("rl_used"), me.nth("rl_used"))
                            A(RL[:, i % 2, 0:nk], bank[6 + i % 2][:, 0:nk], ACT.Relu, scale=HD ** -0.5).then_inc(S("idx_freed"), 1)
                    if t == 19:
                        act.wait_ge(S("rl_used"), me.nth("rl_used", 2))
                        act.wait_ge(S("z_freed"), me.nth("z_freed", 20))
                        A(SG[:], Z[:, Z1["glu"]:Z1["glu"] + 2, :], ACT.Sigmoid).then_inc(S("glu_ready"), 1)
                act.wait_ge(S("z_freed"), me.nth("z_freed", NZ1 - 20))
                A(GT1[:, 0:2, :], Z[:, Z1["cgate"]:Z1["cgate"] + 2, :], ACT.Silu)
                A(GT1[:, 2:4, :], Z[:, Z1["pgate"]:Z1["pgate"] + 2, :], ACT.Silu)
                A(GT1[:, 4:8, :], Z[:, Z1["agate"]:Z1["agate"] + 4, :], ACT.Silu).then_inc(S("silu_ready"), 1)

                def done1(it):
                    if ends_pair(it):
                        A(OB[:, it[0] // 2, :], bank[6 + (it[0] // 2) % 2][:, 0:T]).then_inc(S("o_freed"), 1)

                def mod1(i):
                    if i == len(ITEMS1) - 2:
                        copy_rows(4, me.u + ROW_U)

                softmax(ITEMS1, L1, P1, PT1, ST1, HD ** -0.5, done1, mod1)
                copy_rows(5, me.u + 2 * ROW_U)
                for m in range(2):
                    act.wait_ge(S("pw_ready"), me.nth("pw_ready"))
                    A(Y1[:, 2 + m, :], bank[2 + m][:, 0:T], ACT.Identity, bias=PB[:, m:m + 1],
                      scale=prm_col(f"pools{l}", m)).then_inc(S("pw_freed"), 1)
                act.wait_ge(S("xc_ready"), me.nth("xc_ready"))
                A(CT[:], CV[:], ACT.Square).then_inc(S("conv_sq"), 1)
                act.wait_ge(S("cvar_eps"), me.nth("cvar_eps"))
                A(MS1[:, 1, :], MS1[:, 0, :], ACT.Ln).then_inc(S("act_chain"), 1)
                act.wait_ge(S("act_chain"), me.nth("act_chain"))
                A(MS1[:, 2, :], MS1[:, 1, :], ACT.Exp, scale=-0.5).then_inc(S("rs_guess"), 1)
                split_hi(T, Y1, 0, "y_ready", range(2, KS))
                act.wait_ge(S("cn_ready"), me.nth("cn_ready"))
                for k in range(2):
                    ins = A(CV[:, k, :], CV[:, k, :], ACT.Silu, bias=prm_col(f"lnb{l}", k), scale=prm_col(f"lng{l}", k))
                ins.then_inc(S("conv_silu"), 1)
                plain(3 * ROW_U)
                copy_rows(6, me.u)
                for m in range(2):
                    act.wait_ge(S("pw_ready"), me.nth("pw_ready"))
                    A(Y1[:, m, :], bank[m][:, 0:T], ACT.Identity, bias=prm_col(f"pwb{l}", m)).then_inc(S("pw_freed"), 1)
                ahead()
                split_hi(T, Y1, 0, "y_ready", range(2))
                act.wait_ge(S("ld_p1"), 16 * 3 * (l + 1))
                A(PLEH[:, 0, :, :], PIN[:]).then_inc(S("ple_hi"), 1)
                rest(KS)
                me.tile += KS
                split_hi(T, X, T, "wo_freed")
                for u in range(2):
                    for j in range(4):
                        if j == 3:
                            unit()
                        else:
                            act.wait_ge(S("ple_ready"), me.nth("ple_ready"))
                        A(Y1[:, 4 * u + j, :], bank[me.next_tile()][:, 0:T]).then_inc(S("ple_freed"), 1)
                plain(ROW_U)
                copy_rows(5, me.u)
                ahead()
                for m in range(KS):
                    unit()
                    if m >= 2:
                        act.wait_ge(S("x_new"), me.nth("x_new"))
                    A(SG[:, m % 2, :], bank[me.next_tile()][:, 0:T], ACT.Sigmoid).then_inc(S("gate_freed"), 1)
                act.wait_ge(S("x_new"), me.nth("x_new", 2))
            stats(T, MS1, Y1)
            plain(ROW_U)
            copy_rows(5, me.u)
            act.wait_ge(S("x_new"), me.nth("x_new", KS))

            act.wait_ge(S("x_split"), me.nth("x_split", KS * DEPTH))
            act.wait_ge(S("y_split"), me.nth("y_split", KS * DEPTH))
            act.wait_ge(S("pw_freed"), me.nth("pw_freed", 4 * DEPTH))
            for l in range(DEPTH):
                uc = l < DEPTH - 1
                n = TC if uc else T
                if l == 0:
                    act.wait_ge(S("ld_ctx"), 16)
                stats(TC, MS2, SQ2)
                if uc:
                    plain(2 * ROW_U)
                    first_u = me.u
                    copy_rows(6, first_u - ROW_U)
                ahead()
                split_hi(TC, TB2, 0, "t_ready")
                if uc:
                    copy_rows(7, first_u)
                act.wait_ge(S("x_split"), me.nth("x_split", KS))
                for v in range(2):
                    unit(4)
                    for t in range(4):
                        A(V2[:, t, v * VW:(v + 1) * VW], bank[t][:, 0:VW]).then_inc(S("v_freed"), 1)
                for i, name in enumerate(TILES2):
                    unit()
                    w = T if name in LAT_ONLY and not uc else TC
                    z, g = ZB[:, i, 0:w], bank[me.next_tile()][:, 0:w]
                    if name == "glr":
                        ins = A(z, g, ACT.Identity, bias=cst("glrone"))
                    elif name == "nq":
                        ins = A(z, g, scale=64 ** -0.5)
                    else:
                        ins = A(z, g)
                    ins.then_inc(S("z_freed"), 1)
                for i in range(4):
                    act.wait_ge(S("gate_ready"), me.nth("gate_ready"))
                    g = gate_part(GTA, i)
                    A(g, bank[2 + i % 2][:, 0:VW].rearrange("p (t k) -> p t k", t=2), ACT.Abs).then_inc(S("act_chain"), 1)
                    act.wait_ge(S("act_chain"), me.nth("act_chain"))
                    A(g, g, ACT.Exp, scale=-1.0).then_inc(S("act_chain"), 1)
                    act.wait_ge(S("act_chain"), me.nth("act_chain"))
                    A(g, g, ACT.Ln, bias=1.0).then_inc(S("gln_ready"), 1)
                if uc:
                    plain(ROW_U)
                    copy_rows(5, me.u)
                for h in range(GH):
                    for d in range(2):
                        act.wait_ge(S("b_ready"), me.nth("b_ready"))
                        A(EY[:, d, 0:512], bank[2 + d][:]).then_inc(S("b_copied"), 1)
                    if h > 0:
                        act.wait_ge(S("dec_ready"), me.nth("dec_ready", 2))
                    for w in range(2):
                        act.wait_ge(S("kq_ready"), me.nth("kq_ready"))
                        A(KQ[:, w, :], bank[w][:], scale=1.0 if w == 0 else GDK ** -0.5).then_inc(S("kq_freed"), 1)
                    for d in range(2):
                        act.wait_ge(S("bm_ready"), me.nth("bm_ready"))
                        r = slice(32 * d, 32 * d + 32)
                        A(E0[r, 0:T], EY[r, d, 0:T], ACT.Exp)
                        A(E0[r, T:TC], EY[r, d, T:TC], ACT.Exp, scale=-1.0, bias=BM[r, d, 4:5]).then_inc(S("e0_ready"), 1)
                        act.wait_ge(S("e0_ready"), me.nth("e0_ready"))
                        act.wait_ge(S("ex_ready"), me.nth("ex_ready"))
                        A(EY[:, d, :], EX[:], ACT.Exp).then_inc(S("ey_ready"), 1)
                    if uc:
                        plain(ROW_U)
                        copy_rows(6 + (h // 2 + 1) % 2, me.u)
                    act.wait_ge(S("ax_ready"), me.nth("ax_ready"))
                    for s in range(2 if uc else 1):
                        ins = A(AF[:, s, :, :].rearrange("p a t -> p (a t)")[:, P:3 * P], bank[0][:, 2 * s * P:(2 * s + 2) * P])
                    ins.then_inc(S("ax_freed"), 1)
                    act.wait_ge(S("ax_ready"), me.nth("ax_ready"))
                    A(A0[:].rearrange("p a t -> p (a t)"), bank[1][:]).then_inc(S("ax_freed"), 1)
                    act.wait_ge(S("gpv_done"), me.nth("gpv_done"))
                    if h % 2 == 1:
                        A(OM[:, 0, 0:n], bank[6 + (h // 2) % 2][:, 0:n], ACT.Square).then_inc(S("osq_ready"), 1)
                        act.wait_ge(S("oms_eps"), me.nth("oms_eps"))
                        A(OM[:, 3, 0:n], OM[:, 1, 0:n], ACT.Ln).then_inc(S("act_chain"), 1)
                        act.wait_ge(S("act_chain"), me.nth("act_chain"))
                        A(OM[:, 3, 0:n], OM[:, 3, 0:n], ACT.Exp, scale=-0.5).then_inc(S("rs_guess"), 1)
                        A(OM[:, 2, 0:n], ZB[:, Z2["r"] + h // 2, 0:n], ACT.Silu).then_inc(S("rsilu_ready"), 1)
                        act.wait_ge(S("yo_ready"), me.nth("yo_ready"))
                        A(NHI[:, h // 2, 0:n], OG[:, 0:n]).then_inc(S("xh_ready"), 1)
                act.wait_ge(S("dec_ready"), me.nth("dec_ready", 2))
                for k in range(2):
                    act.wait_ge(S("yo_ready"), me.nth("yo_ready"))
                    A(NHI[:, 3 + k, 0:n], ZB[:, Z2["scx"] + k, 0:n]).then_inc(S("xh_ready"), 1)
                act.wait_ge(S("y_split"), me.nth("y_split", 5))

                def done2(it):
                    if ends_pair(it, uc):
                        k = it[0] // 2
                        A(OY[:, k, 0:n], bank[6 + k % 2][:, 0:n]).then_inc(S("o_freed"), 1)
                        act.wait_ge(S("o_freed"), me.nth("o_freed"))
                        A(NHI[:, 5 + k, 0:n], OY[:, k, 0:n]).then_inc(S("xh_ready"), 1)

                if l == 0:
                    act.wait_ge(S("o_freed"), me.nth("o_freed", 4 * DEPTH))
                softmax(items2(uc), L2, P2, PT2, ST2, 1.0, done2)
                ahead()
                act.wait_ge(S("y_split"), me.nth("y_split", 3))
                rest(KS)
                me.tile += KS
                act.wait_ge(S("wo_freed"), me.nth("wo_freed", KS))
                stats(n, MS2, SQ2)
                if uc:
                    plain(2 * ROW_U)
                    first_u = me.u
                    copy_rows(5, first_u - ROW_U)
                ahead()
                split_hi(n, TB2, 0, "t_ready")
                if uc:
                    copy_rows(6, first_u)
                act.wait_ge(S("x_split"), me.nth("x_split", KS))
                for p in range(FT + 2):
                    if p < FT:
                        for w in range(2):
                            unit()
                            j = w * FT + p
                            if w == 0 and p >= 3:
                                act.wait_ge(S("hid_split"), me.nth("hid_split"))
                            A(CF[:, w, p % 3, 0:n], bank[me.next_tile()][:, 0:n], ACT.Identity,
                              bias=prm_col(f"fb{l}", j), scale=prm_col(f"fw{l}", 2 * FT + j)).then_inc(S("centre_ready"), 1)
                    if 1 <= p < FT + 1:
                        act.wait_ge(S("up_freed"), me.nth("up_freed", 2))
                        A(CF[:, 0, (p - 1) % 3, 0:n], CF[:, 0, (p - 1) % 3, 0:n], ACT.Silu).then_inc(S("fsilu_ready"), 1)
                    if p >= 2:
                        act.wait_ge(S("hid_ready"), me.nth("hid_ready"))
                        A(HHI[:, p - 2, 0:n], CF[:, 1, (p - 2) % 3, 0:n]).then_inc(S("hh_ready"), 1)
                act.wait_ge(S("hid_split"), me.nth("hid_split", 3))
                rest(3 * KS)
                me.tile += KS
                act.wait_ge(S("wo_freed"), me.nth("wo_freed", KS))
            stats(T, MS2, SQ2)

        @block.vector
        def _(dve):
            me = Side(dve, "dve")
            V = nc.vector
            split = 0

            def split_to(n):
                nonlocal split
                while split < min(n, NU):
                    u, k = split, SPLIT_NO[split]
                    split += 1
                    if PLAIN[u]:
                        continue
                    dve.wait_ge(S("hi_ready"), k + 1)
                    w = WIDTHS[u]
                    V.tensor_tensor(WLO[:, k % SPL, 0:w], RAWB[:, u % RAW, 0:w], WHI[:, k % SPL, 0:w].bitcast(F32),
                                    ALU.subtract).then_inc(S("lo_ready"), 1)

            def rest(n=1):
                for _ in range(n):
                    me.u += 1
                    split_to(me.u + AHEAD)

            def plain(n):
                me.u += n

            def ahead():
                split_to(me.u + AHEAD)

            def unit(n=1):
                rest(n)
                dve.wait_ge(S("unit_done"), me.u)

            def rsqrt(m, g, t, out):
                V.tensor_tensor(t, g, g, ALU.mult).then_inc(S("dve_chain"), 1)
                dve.wait_ge(S("dve_chain"), me.nth("dve_chain"))
                V.tensor_tensor(t, t, m, ALU.mult).then_inc(S("dve_chain"), 1)
                dve.wait_ge(S("dve_chain"), me.nth("dve_chain"))
                V.tensor_scalar(t, t, -0.5, 1.5, ALU.mult, ALU.add).then_inc(S("dve_chain"), 1)
                dve.wait_ge(S("dve_chain"), me.nth("dve_chain"))
                V.tensor_tensor(out, g, t, ALU.mult).then_inc(S("dve_chain"), 1)
                dve.wait_ge(S("dve_chain"), me.nth("dve_chain"))

            def stats(n, ms):
                dve.wait_ge(S("ms_ready"), me.nth("ms_ready"))
                V.tensor_scalar(ms[:, 0, 0:n], bank[4][:, 0:n], EPS, None, ALU.add).then_inc(S("ms_eps"), 1)
                dve.wait_ge(S("rs_guess"), me.nth("rs_guess"))
                rsqrt(ms[:, 0, 0:n], ms[:, 2, 0:n], ms[:, 1, 0:n], ms[:, 3, 0:n])

            def split_lo(n, src, o, done, slabs=range(KS)):
                for s in slabs:
                    dve.wait_ge(S("xh_ready"), me.nth("xh_ready"))
                    V.tensor_tensor(NLO[:, s, o:o + n], src[:, s, 0:n], NHI[:, s, o:o + n].bitcast(F32), ALU.subtract).then_inc(S(done), 1)

            def modulation(b):
                l, first = taken[0] // ROW_TILES, 4 * (taken[0] % ROW_TILES)
                taken[0] += 1
                dve.wait_ge(S("cols_ready"), me.nth("cols_ready"))
                V.tensor_tensor(MOD[:, l, first:first + 4, :], bank[b][:, 0:8].rearrange("p (j c) -> p j c", c=2),
                                bl(prm_col(f"bada{l}", first, 4), 2), ALU.add).then_inc(S("mod_done"), 1)

            taken = [0]

            def softmax(items, bias, lbuf, pbuf, stb, scale, between=None):
                n = len(items)
                for i in range(n + 1):
                    if i < n:
                        k, nk = i % 3, items[i][2]
                        b = bias(items[i])
                        dve.wait_ge(S("s_ready"), me.nth("s_ready"))
                        if b is None:
                            V.tensor_copy(lbuf[:, k, 0:nk], bank[i % 2][:, 0:nk])
                            V.reduce_max(stb[:, k, 0:1], bank[i % 2][:, 0:nk], AX_X).then_inc(S("s_freed"), 1)
                        else:
                            V.tensor_tensor_reduce(out=lbuf[:, k, 0:nk], in0=bank[i % 2][:, 0:nk], in1=b, scale=1.0,
                                                   scalar=-3.0e38, op0=ALU.add, op1=ALU.max,
                                                   accum_out=stb[:, k, 0:1]).then_inc(S("s_freed"), 1)
                        dve.wait_ge(S("s_freed"), me.nth("s_freed"))
                        V.tensor_scalar(stb[:, k, 1:2], stb[:, k, 0:1], -scale, None, ALU.mult).then_inc(S("l_ready"), 1)
                        if between is not None:
                            between(i)
                    if i >= 1:
                        k, nk = (i - 1) % 3, items[i - 1][2]
                        dve.wait_ge(S("e_ready"), me.nth("e_ready"))
                        V.reciprocal(stb[:, k, 3:4], stb[:, k, 2:3]).then_inc(S("dve_chain"), 1)
                        dve.wait_ge(S("dve_chain"), me.nth("dve_chain"))
                        V.tensor_scalar(pbuf[:, k, 0:nk], pbuf[:, k, 0:nk], stb[:, k, 3:4], None, ALU.mult).then_inc(S("p_ready"), 1)

            dve.wait_ge(S("ld_prm"), 16)

            dve.wait_ge(S("ld_x"), 16)
            V.memset(UP[:, :, 0:CONV_K - 1], 0.0)
            V.memset(PP[:, :, 0:16], 0.0)
            V.memset(PS[:, :, :, 0:16], 0.0).then_inc(S("dve_chain"), 1)
            dve.wait_ge(S("dve_chain"), me.nth("dve_chain"))
            dve.wait_ge(S("ld_c1"), 16)
            for l in range(DEPTH):
                dve.wait_ge(S("ld_p1"), 16 * 3 * (l + 1))
                stats(T, MS1)
                for s in range(KS):
                    V.scalar_tensor_tensor(Y1[:, s, :], X[:, s, 0:T], prm_col(f"norm{l}", s), MS1[:, 3, :],
                                           ALU.mult, ALU.mult).then_inc(S("t_ready"), 1)
                plain(2 * ROW_U)
                ahead()
                split_lo(T, Y1, 0, "x_split")
                modulation(5)
                unit(4)
                for t in range(TT):
                    V.tensor_tensor(V1[:, t, :], bank[t][:], BV[:], ALU.add).then_inc(S("v_freed"), 1)
                modulation(6)

                def rope(g, done):
                    k = 2 if g < 5 else 1
                    z = Z[:, 2 * g:2 * g + k, :]
                    rt = RT[:, 0:k * T].rearrange("p (a t) -> p a t", a=k)
                    dve.wait_ge(S("rot_ready"), me.nth("rot_ready"))
                    V.tensor_tensor(rt, bank[4 + g % 2][:, 0:k * T].rearrange("p (a t) -> p a t", a=k),
                                    bc(c1v("sin"), k), ALU.mult).then_inc(S("rot_freed"), 1)
                    V.tensor_tensor(z, z, bc(c1v("cos"), k), ALU.mult).then_inc(S("dve_chain"), 1)
                    dve.wait_ge(S("rot_freed"), me.nth("rot_freed"))
                    dve.wait_ge(S("dve_chain"), me.nth("dve_chain"))
                    V.tensor_tensor(z, z, rt, ALU.add).then_inc(S(done), 1)
                    dve.wait_ge(S(done), me.nth(done))

                def index(i):
                    qt, h = i // IDXH, i % IDXH
                    nk = P * (qt + 1)
                    dve.wait_ge(S("idx_freed"), me.nth("idx_freed"))
                    if h == 0:
                        ins = V.tensor_scalar(SC[:, qt, 0:nk], RL[:, i % 2, 0:nk], WI[:, qt, h:h + 1], None, ALU.mult)
                    else:
                        ins = V.scalar_tensor_tensor(SC[:, qt, 0:nk], RL[:, i % 2, 0:nk], WI[:, qt, h:h + 1],
                                                     SC[:, qt, 0:nk], ALU.mult, ALU.add)
                    ins.then_inc(S("rl_used"), 1)
                    dve.wait_ge(S("rl_used"), me.nth("rl_used"))

                def topk(qt, r0, r1):
                    nk = P * (qt + 1)
                    sc, causal = SC[:, qt, 0:nk], c1v("causal")[:, qt * T:qt * T + nk]
                    if r0 == 0:
                        V.tensor_tensor(sc, sc, causal, ALU.add).then_inc(S("dve_chain"), 1)
                        dve.wait_ge(S("dve_chain"), me.nth("dve_chain"))
                    for _ in range(r0, r1):
                        V.max(M8[:], sc).then_inc(S("dve_chain"), 1)
                        dve.wait_ge(S("dve_chain"), me.nth("dve_chain"))
                        V.match_replace(out=sc, in_to_replace=M8[:], in_values=sc, imm_value=-3.0e38).then_inc(S("dve_chain"), 1)
                        dve.wait_ge(S("dve_chain"), me.nth("dve_chain"))
                    if r1 == TOPK // 8:
                        V.tensor_scalar(MB[:, qt, 0:nk], sc, -2.0e38, -1.0e30, ALU.is_gt, ALU.mult).then_inc(S("dve_chain"), 1)
                        dve.wait_ge(S("dve_chain"), me.nth("dve_chain"))
                        V.tensor_tensor(MB[:, qt, 0:nk], MB[:, qt, 0:nk], causal, ALU.add).then_inc(S("dve_chain"), 1)
                        dve.wait_ge(S("dve_chain"), me.nth("dve_chain"))

                for t in range(NZ1):
                    rest()
                    if t == 12:
                        dve.wait_ge(S("z_freed"), me.nth("z_freed", 12))
                        rope(4, "dve_chain")
                        rope(5, "qi_roped")
                    if t in (13, 14):
                        rope(t - 13, "dve_chain")
                    if t == 15:
                        dve.wait_ge(S("wi_freed"), me.nth("wi_freed", TT))
                    if 15 <= t < 19:
                        index(2 * (t - 15))
                        index(2 * (t - 15) + 1)
                    if t == 17:
                        topk(0, 0, 4)
                    if t == 18:
                        topk(0, 4, 8)
                    if t == 19:
                        topk(1, 0, 4)
                    if t == 20:
                        topk(1, 4, 8)
                    if t == 22:
                        rope(2, "dve_chain")
                    if t == 23:
                        rope(3, "rope_done")
                    if t == 24:
                        dve.wait_ge(S("glu_ready"), me.nth("glu_ready"))
                        dve.wait_ge(S("z_freed"), me.nth("z_freed", 8))
                        V.tensor_tensor(UP[:, :, CONV_K - 1:], Z[:, Z1["val"]:Z1["val"] + 2, :], SG[:], ALU.mult).then_inc(S("dve_chain"), 1)
                        V.tensor_copy(PP[:, :, 16:], Z[:, Z1["pin"]:Z1["pin"] + 2, :]).then_inc(S("dve_chain"), 1)
                        dve.wait_ge(S("dve_chain"), me.nth("dve_chain", 2))
                me.tile += NZ1
                plain(3 * ROW_U)
                for j in range(4):
                    s = PP[:] if j == 0 else PS[:, j - 1, :, :]
                    V.tensor_tensor(PS[:, j, :, 16:], s[:, :, 16:], s[:, :, 16 - (1 << j):16 + T - (1 << j)], ALU.add).then_inc(S("dve_chain"), 1)
                    dve.wait_ge(S("dve_chain"), me.nth("dve_chain"))
                for g in range(4):
                    r, m = half(g), g // 2
                    ins = V.tensor_tensor(PD[r, m, :], PS[r, g, m, 16:], c1v("icnt")[r, m * T:(m + 1) * T], ALU.mult)
                V.tensor_tensor(PB[:], prm_col(f"poolb{l}", 0, 2), prm_col(f"pools{l}", 0, 2), ALU.mult).then_inc(S("dve_chain"), 1)
                dve.wait_ge(S("dve_chain"), me.nth("dve_chain"))
                V.tensor_tensor(PD[:], PD[:], PP[:, :, 16:], ALU.subtract).then_inc(S("pool_ready"), 1)

                def conv(i):
                    for k in (2 * i, 2 * i + 1):
                        if k >= CONV_K:
                            continue
                        for m in range(2):
                            w, src = prm_col(f"dww{l}", m * CONV_K + k), UP[:, m, k:k + T]
                            if k == 0:
                                ins = V.tensor_scalar(CV[:, m, :], src, w, prm_col(f"dwb{l}", m), ALU.mult, ALU.add)
                            else:
                                ins = V.scalar_tensor_tensor(CV[:, m, :], src, w, CV[:, m, :], ALU.mult, ALU.add)
                        if k < CONV_K - 1:
                            ins.then_inc(S("dve_chain"), 1)
                            dve.wait_ge(S("dve_chain"), me.nth("dve_chain"))
                        else:
                            ins.then_inc(S("conv_ready"), 1)
                            dve.wait_ge(S("conv_ready"), me.nth("conv_ready"))

                softmax(ITEMS1, lambda it: MB[:, it[1], 0:it[2]], L1, P1, ST1, HD ** -0.5, conv)
                modulation(4)
                dve.wait_ge(S("cstat_ready"), me.nth("cstat_ready"))
                V.tensor_tensor(CV[:], CV[:], bc(bank[4][:, 0:T], 2), ALU.subtract).then_inc(S("xc_ready"), 1)
                dve.wait_ge(S("xc_ready"), me.nth("xc_ready"))
                dve.wait_ge(S("silu_ready"), me.nth("silu_ready"))
                dve.wait_ge(S("o_freed"), me.nth("o_freed", 4))
                dve.wait_ge(S("pw_freed"), me.nth("pw_freed", 2))
                for m in range(2, KS):
                    V.tensor_tensor(Y1[:, m, :], Y1[:, m, :] if m < 4 else OB[:, m - 4, :], GT1[:, m, :], ALU.mult).then_inc(S("y_ready"), 1)
                dve.wait_ge(S("cstat_ready"), me.nth("cstat_ready"))
                V.tensor_scalar(MS1[:, 0, :], bank[4][:, 0:T], EPS, None, ALU.add).then_inc(S("cvar_eps"), 1)
                modulation(5)
                dve.wait_ge(S("rs_guess"), me.nth("rs_guess"))
                rsqrt(MS1[:, 0, :], MS1[:, 2, :], MS1[:, 1, :], MS1[:, 3, :])
                V.tensor_tensor(CV[:], CV[:], bc(MS1[:, 3, :], 2), ALU.mult).then_inc(S("cn_ready"), 1)
                split_lo(T, Y1, 0, "y_split", range(2, KS))
                for m in range(2):
                    dve.wait_ge(S("pw_freed"), me.nth("pw_freed"))
                    V.tensor_tensor(Y1[:, m, :], Y1[:, m, :], GT1[:, m, :], ALU.mult).then_inc(S("y_ready"), 1)
                ahead()
                split_lo(T, Y1, 0, "y_split", range(2))
                modulation(6)
                dve.wait_ge(S("ple_hi"), me.nth("ple_hi"))
                V.tensor_tensor(PLEH[:, 1, :, :], PIN[:], PLEH[:, 0, :, :].bitcast(F32), ALU.subtract).then_inc(S("ple_split"), 1)
                for m in range(KS):
                    unit()
                    V.tensor_tensor(X[:, m, 0:T], X[:, m, 0:T], bank[me.next_tile()][:, 0:T], ALU.add).then_inc(S("wo_freed"), 1)
                split_lo(T, X, T, "h_split")
                rest(2)
                dve.wait_ge(S("ple_freed"), me.nth("ple_freed", KS))
                me.tile += 2 * KS
                plain(ROW_U)
                ahead()
                for m in range(KS):
                    rest()
                    dve.wait_ge(S("gate_freed"), me.nth("gate_freed"))
                    V.tensor_tensor(Y1[:, m, :], Y1[:, m, :], SG[:, m % 2, :], ALU.mult).then_inc(S("dve_chain"), 1)
                    dve.wait_ge(S("dve_chain"), me.nth("dve_chain"))
                    V.tensor_tensor(X[:, m, 0:T], X[:, m, 0:T], Y1[:, m, :], ALU.add).then_inc(S("x_new"), 1)
                    if m == 0:
                        modulation(5)
            stats(T, MS1)
            for s in range(KS):
                V.scalar_tensor_tensor(X[:, s, 0:T], X[:, s, 0:T], prm_col("fin1", s), MS1[:, 3, :],
                                       ALU.mult, ALU.mult).then_inc(S("x_new"), 1)

            plain(ROW_U)

            def modulate(l, n, gain, shift, scale):
                V.scalar_tensor_tensor(GM[:], MOD[:, l, scale:scale + KS, :], 1.0, bl(prm_col(gain, 0, KS), 2),
                                       ALU.add, ALU.mult).then_inc(S("dve_chain"), 1)
                dve.wait_ge(S("dve_chain"), me.nth("dve_chain"))
                ahead()
                for s in range(KS):
                    for c in range(n // T):
                        w = slice(c * T, (c + 1) * T)
                        ins = V.scalar_tensor_tensor(TB2[:, s, w], X[:, s, w], GM[:, s, c:c + 1], MS2[:, 3, w], ALU.mult, ALU.mult)
                    ins.then_inc(S("dve_chain"), 1)
                    dve.wait_ge(S("dve_chain"), me.nth("dve_chain"))
                    for c in range(n // T):
                        w = slice(c * T, (c + 1) * T)
                        ins = V.tensor_scalar(TB2[:, s, w], TB2[:, s, w], MOD[:, l, shift + s, c:c + 1], None, ALU.add)
                    ins.then_inc(S("t_ready"), 1)
                split_lo(n, TB2, 0, "x_split")

            def residual(l, n, gate, units):
                for m in range(KS):
                    unit(units)
                    b = bank[me.next_tile()]
                    for c in range(n // T):
                        w = slice(c * T, (c + 1) * T)
                        ins = V.scalar_tensor_tensor(X[:, m, w], b[:, w], MOD[:, l, gate + m, c:c + 1], X[:, m, w],
                                                     ALU.mult, ALU.add)
                    ins.then_inc(S("wo_freed"), 1)

            def seq(ap, n):
                return ap.rearrange("p (s t) -> p s t", t=T)

            dve.wait_ge(S("x_new"), me.nth("x_new", KS * (DEPTH + 1)))
            dve.wait_ge(S("s_freed"), me.nth("s_freed", 0))
            for l in range(DEPTH):
                uc = l < DEPTH - 1
                n = TC if uc else T
                if uc:
                    plain(2 * ROW_U)
                    modulation(5)
                stats(TC, MS2)
                modulate(l, TC, f"nmix{l}", SH1, SC1)
                if uc:
                    modulation(6)
                rest(4)
                if uc:
                    modulation(7)
                rest(4 + NZ2)
                me.tile += NZ2
                dve.wait_ge(S("ld_c2"), 16 * 2 * (l + 1))
                dve.wait_ge(S("z_freed"), me.nth("z_freed", NZ2))
                for t in range(3):
                    z = ZB[:, t, 0:T]
                    dve.wait_ge(S("rot_ready"), me.nth("rot_ready"))
                    V.tensor_tensor(AM[:, 0:T], bank[t % 2][:, 0:T], c2v("sin"), ALU.mult).then_inc(S("rot_freed"), 1)
                    V.tensor_tensor(z, z, c2v("cos"), ALU.mult).then_inc(S("dve_chain"), 1)
                    dve.wait_ge(S("dve_chain"), me.nth("dve_chain"))
                    ins = V.tensor_tensor(z, z, AM[:, 0:T], ALU.add)
                    if t < 2:
                        ins.then_inc(S("dve_chain"), 1)
                        dve.wait_ge(S("dve_chain"), me.nth("dve_chain"))
                ins.then_inc(S("rope_done"), 1)
                for i in range(4):
                    dve.wait_ge(S("gln_ready"), me.nth("gln_ready"))
                    V.scalar_tensor_tensor(gate_part(GT, i), bank[2 + i % 2][:, 0:VW].rearrange("p (t k) -> p t k", t=2),
                                           0.0, gate_part(GTA, i), ALU.min, ALU.subtract).then_inc(S("g_ready"), 1)
                if uc:
                    plain(ROW_U)
                for h in range(GH):
                    def middles(d):
                        dve.wait_ge(S("b_copied"), me.nth("b_copied"))
                        b = EY[:, d, 0:TC]
                        for c in range(NCH):
                            r = slice(CH * c, CH * (c + 1))
                            V.tensor_copy(BM[r, d, 0:4], EY[r, d, 0:TC].rearrange("p (i t) -> p i t", t=P)[
                                :, :, CH * c + CH // 2 - 1 + d])
                        e = TC - 1 if d == 0 else T
                        V.tensor_copy(BM[:, d, 4:5], b[:, e:e + 1]).then_inc(S("bm_ready"), 1)
                        dve.wait_ge(S("bm_ready"), me.nth("bm_ready"))
                        V.tensor_tensor(AM[:].rearrange("p (i t) -> p i t", t=P),
                                        b.rearrange("p (i t) -> p i t", t=P),
                                        bl(BM[:, d, 0:4], P), ALU.subtract).then_inc(S("dve_chain"), 1)
                        dve.wait_ge(S("dve_chain"), me.nth("dve_chain"))

                    def exponents(d):
                        am = AM[:].rearrange("p (i t) -> p i t", t=P)
                        cap = c2v("capkf") if d == 0 else c2v("capkb")
                        V.tensor_tensor(EX[:, 0:512].rearrange("p (i t) -> p i t", t=P), am, bc(c2v("capq"), 4), ALU.min)
                        V.scalar_tensor_tensor(EX[:, 512:1024].rearrange("p (i t) -> p i t", t=P), am, -1.0,
                                               bc(cap, 4), ALU.mult, ALU.min)
                        V.tensor_tensor(EX[:, 1024:].rearrange("p (s t) -> p s t", t=P),
                                        bl(BM[:, d, 1 - d:4:2], P),
                                        EY[:, d, 0:TC].rearrange("p (s i t) -> p s i t", i=2, t=P)[:, :, d, :],
                                        ALU.subtract).then_inc(S("ex_ready"), 1)

                    def decay(d):
                        V.tensor_tensor(EY[:, d, 0:512], EY[:, d, 0:512], KQ[:, 1, :], ALU.mult)
                        V.tensor_tensor(EY[:, d, 512:1024], EY[:, d, 512:1024], KQ[:, 0, :], ALU.mult)
                        dve.wait_ge(S("e0_ready"), me.nth("e0_ready"))
                        if d == 1:
                            V.tensor_tensor(E0[:, 0:T], E0[:, 0:T], KQ[0:64, 1, 0:T], ALU.mult)
                            V.tensor_tensor(E0[:, T:], E0[:, T:], KQ[0:64, 0, T:], ALU.mult)
                        ey = EY[:, d, 1024:].rearrange("p (s t) -> p s t", t=P)
                        V.tensor_tensor(ey, ey, KQ[:, 0, :].rearrange("p (s i t) -> p s i t", i=2, t=P)[:, :, d, :],
                                        ALU.mult).then_inc(S("dec_ready"), 1)

                    if uc and h == 0:
                        modulation(5)
                    middles(0)
                    exponents(0)
                    middles(1)
                    dve.wait_ge(S("ey_ready"), me.nth("ey_ready"))
                    exponents(1)
                    dve.wait_ge(S("kq_freed"), me.nth("kq_freed", 2))
                    decay(0)
                    dve.wait_ge(S("ey_ready"), me.nth("ey_ready"))
                    decay(1)
                    if h > 0:
                        dve.wait_ge(S("gpv_done"), me.nth("gpv_done"))
                    for s in range(2 if uc else 1):
                        dve.wait_ge(S("a_ready"), me.nth("a_ready"))
                        V.tensor_tensor(AM[:], bank[4 + s][:], c2v("mask"), ALU.mult).then_inc(S("am_read"), 1)
                        dve.wait_ge(S("am_read"), me.nth("am_read"))
                        o = AF[:, s, :, :].rearrange("p a (b t) -> p (a b) t", t=P)[:, 0:4:3, :]
                        V.tensor_tensor(o, AM[:, 0:T].rearrange("p (a t) -> p a t", t=P),
                                        AM[:, T:].rearrange("p (a t) -> p a t", t=P), ALU.add).then_inc(S("af_ready"), 1)
                        dve.wait_ge(S("af_ready"), me.nth("af_ready"))
                    if uc:
                        plain(ROW_U)
                        modulation(6 + (h // 2 + 1) % 2)
                    if h % 2 == 1:
                        k = h // 2
                        dve.wait_ge(S("oms_ready"), me.nth("oms_ready"))
                        V.tensor_scalar(OM[:, 1, 0:n], bank[5][:, 0:n], EPS, None, ALU.add).then_inc(S("oms_eps"), 1)
                        dve.wait_ge(S("rs_guess"), me.nth("rs_guess"))
                        rsqrt(OM[:, 1, 0:n], OM[:, 3, 0:n], OM[:, 0, 0:n], OM[:, 3, 0:n])
                        V.tensor_tensor(OG[:, 0:n], bank[6 + k % 2][:, 0:n], OM[:, 3, 0:n], ALU.mult).then_inc(S("og_read"), 1)
                        dve.wait_ge(S("og_read"), me.nth("og_read"))
                        dve.wait_ge(S("rsilu_ready"), me.nth("rsilu_ready"))
                        V.scalar_tensor_tensor(OG[:, 0:n], OG[:, 0:n], prm_col(f"glag{l}"), OM[:, 2, 0:n],
                                               ALU.mult, ALU.mult).then_inc(S("yo_ready"), 1)
                        dve.wait_ge(S("yo_ready"), me.nth("yo_ready"))
                        dve.wait_ge(S("xh_ready"), me.nth("xh_ready"))
                        V.tensor_tensor(NLO[:, k, 0:n], OG[:, 0:n], NHI[:, k, 0:n].bitcast(F32), ALU.subtract).then_inc(S("y_split"), 1)
                dve.wait_ge(S("gpv_done"), me.nth("gpv_done"))
                cc_, xx = ZB[:, Z2["scc"]:Z2["scc"] + 2, 0:n], ZB[:, Z2["scx"]:Z2["scx"] + 2, 0:n]
                V.tensor_tensor(cc_, cc_, xx, ALU.mult).then_inc(S("dve_chain"), 1)
                dve.wait_ge(S("dve_chain"), me.nth("dve_chain"))
                for k in range(2):
                    a, x = ZB[:, Z2["scc"] + k, 0:n], ZB[:, Z2["scx"] + k, 0:n]
                    w = [prm_col(f"scw{l}", 2 * tap + k) for tap in range(3)]
                    V.tensor_scalar(x, a, w[1], prm_col(f"scbias{l}", k), ALU.mult, ALU.add).then_inc(S("dve_chain"), 1)
                    dve.wait_ge(S("dve_chain"), me.nth("dve_chain"))
                    a, y = seq(a, n), seq(x, n)
                    V.scalar_tensor_tensor(y[:, :, 1:], a[:, :, :-1], w[0], y[:, :, 1:], ALU.mult, ALU.add).then_inc(S("dve_chain"), 1)
                    dve.wait_ge(S("dve_chain"), me.nth("dve_chain"))
                    V.scalar_tensor_tensor(y[:, :, :-1], a[:, :, 1:], w[2], y[:, :, :-1], ALU.mult, ALU.add).then_inc(S("dve_chain"), 1)
                    dve.wait_ge(S("dve_chain"), me.nth("dve_chain"))
                    V.tensor_tensor(x, x, ZB[:, Z2["scb"] + k, 0:n], ALU.mult).then_inc(S("yo_ready"), 1)
                    dve.wait_ge(S("yo_ready"), me.nth("yo_ready"))
                for k in range(2):
                    dve.wait_ge(S("xh_ready"), me.nth("xh_ready"))
                    V.tensor_tensor(NLO[:, 3 + k, 0:n], ZB[:, Z2["scx"] + k, 0:n], NHI[:, 3 + k, 0:n].bitcast(F32),
                                    ALU.subtract).then_inc(S("y_split"), 1)
                V.memset(NB[:, :, :, T:], 0.0).then_inc(S("dve_chain"), 1)
                dve.wait_ge(S("dve_chain"), me.nth("dve_chain"))
                half_loads = [0, 0]

                def bias2(it):
                    h, qt, nk, own = it
                    if own:
                        return None
                    if qt == 0:
                        half_loads[h % 2] += 1
                        dve.wait_ge(S(f"ld_nb{h % 2}"), 16 * (NAH // 2 * l + half_loads[h % 2]))
                    return NB[:, h % 2, qt, :]

                if l == 0:
                    me.seen["s_freed"] = len(ITEMS1) * DEPTH
                softmax(items2(uc), bias2, L2, P2, ST2, 1.0)
                for k in range(3):
                    dve.wait_ge(S("xh_ready"), me.nth("xh_ready"))
                    V.tensor_tensor(NLO[:, 5 + k, 0:n], OY[:, k, 0:n], NHI[:, 5 + k, 0:n].bitcast(F32),
                                    ALU.subtract).then_inc(S("y_split"), 1)
                ahead()
                residual(l, n, G1, 1)
                dve.wait_ge(S("wo_freed"), me.nth("wo_freed", KS))
                stats(n, MS2)
                if uc:
                    plain(2 * ROW_U)
                modulate(l, n, f"nffn{l}", SH2, SC2)
                if uc:
                    modulation(5)
                for p in range(FT + 2):
                    if uc and p == 2:
                        modulation(6)
                    if p < FT:
                        for w in range(2):
                            unit()
                            dve.wait_ge(S("centre_ready"), me.nth("centre_ready"))
                            b = seq(bank[me.next_tile()][:, 0:n], n)
                            y = seq(CF[:, w, p % 3, 0:n], n)
                            j = w * FT + p
                            V.scalar_tensor_tensor(y[:, :, 1:], b[:, :, :-1], prm_col(f"fw{l}", j),
                                                   y[:, :, 1:], ALU.mult, ALU.add).then_inc(S("dve_chain"), 1)
                            dve.wait_ge(S("dve_chain"), me.nth("dve_chain"))
                            V.scalar_tensor_tensor(y[:, :, :-1], b[:, :, 1:], prm_col(f"fw{l}", 4 * FT + j),
                                                   y[:, :, :-1], ALU.mult, ALU.add).then_inc(S("up_freed"), 1)
                    if 1 <= p < FT + 1:
                        k = (p - 1) % 3
                        dve.wait_ge(S("fsilu_ready"), me.nth("fsilu_ready"))
                        V.tensor_tensor(CF[:, 1, k, 0:n], CF[:, 1, k, 0:n], CF[:, 0, k, 0:n], ALU.mult).then_inc(S("hid_ready"), 1)
                    if p >= 2:
                        dve.wait_ge(S("hh_ready"), me.nth("hh_ready"))
                        V.tensor_tensor(HLO[:, p - 2, 0:n], CF[:, 1, (p - 2) % 3, 0:n],
                                        HHI[:, p - 2, 0:n].bitcast(F32), ALU.subtract).then_inc(S("hid_split"), 1)
                dve.wait_ge(S("up_freed"), me.nth("up_freed", 2 * FT))
                dve.wait_ge(S("hid_ready"), me.nth("hid_ready", FT))
                residual(l, n, G2, 3)
                dve.wait_ge(S("wo_freed"), me.nth("wo_freed", KS))
            stats(T, MS2)
            for s in range(KS):
                V.scalar_tensor_tensor(X[:, s, 0:T], X[:, s, 0:T], prm_col("fin2", s), MS2[:, 3, 0:T],
                                       ALU.mult, ALU.mult).then_inc(S("x_new"), 1)


def fm_units(w, cols):
    cols = np.asarray(cols)
    t = np.zeros((w.shape[0], P), np.float32)
    ok = cols >= 0
    t[:, :len(cols)][:, ok] = w[:, cols[ok]]
    t = t.reshape(-1, P, P).transpose(1, 0, 2)
    return [t[:, s:s + 8].reshape(P, -1) for s in range(0, t.shape[1], 8)]


def tm_units(w):
    t = w.reshape(KS, P, -1).transpose(1, 0, 2)
    return [t[:, s:s + 2].reshape(P, -1) for s in range(0, KS, 2)]


def columns1():
    o = np.cumsum([0, 256, 256, 256, 256, 256, 512, 512, 512, 512, 256, 64, 4])
    val, glu, cg, pin, pg, q, k, v, ag, qi, ki, wi = o[:12]
    base = {"q": q, "k": k, "qi": qi, "val": val, "glu": glu, "cgate": cg, "pin": pin, "pgate": pg, "agate": ag}
    out = []
    for t, name in enumerate(TILES1):
        if name == "ki":
            out.append(np.concatenate([ki + np.arange(64)] * 2))
        elif name == "wi":
            out.append(np.concatenate([wi + np.arange(4), np.full(124, -1)]))
        else:
            out.append(base[name] + (t - Z1[name]) * P + np.arange(P))
    return out, v


def columns2():
    o = np.cumsum([0, 192, 192, 384, 16, 16, 384, 256, 256, 256, 384, 384, 384])
    q, k, v, lf, lb, r, sb_, sc_, sx, nq, nk, nv = o[:12]
    base = {"nk": nk, "nq": nq, "r": r, "scb": sb_, "scc": sc_, "scx": sx}
    pad = np.full(16, -1)
    out = []
    for t, name in enumerate(TILES2):
        if name == "gqa":
            out.append(q + np.arange(P))
        elif name == "gka":
            out.append(k + np.arange(P))
        elif name == "gqk":
            out.append(np.concatenate([q + P + np.arange(64), k + P + np.arange(64)]))
        elif name == "glr":
            out.append(np.concatenate([lf + np.arange(16), pad, lb + np.arange(16), np.full(80, -1)]))
        else:
            out.append(base[name] + (t - Z2[name]) * P + np.arange(P))
    return out, v, nv


def constants():
    f = np.float32
    cc, c1, c2 = np.zeros((P, NCC), f), np.zeros((P, NC1), f), np.zeros((P, NC2), f)

    def put(arr, table, name, value):
        a, n = table[name]
        arr[:, a:a + n] = value

    i = np.arange(P)
    put(cc, CC, "ident", np.eye(P))
    put(cc, CC, "ones", 1.0 / D)
    put(cc, CC, "ones256", 1.0 / CONV_W)
    put(cc, CC, "blk", (i[:, None] // 64 == i[None, :] // 64) / 64.0)
    put(cc, CC, "glrone", ((i == 16) | (i == 48))[:, None])

    perm = np.zeros((P, P))
    for d in range(P):
        if d % 64 < 32:
            perm[d + 32, d] = -1.0
        else:
            perm[d - 32, d] = 1.0
    put(c1, C1, "perm", perm)
    t = np.arange(T)
    inv = (f(10000.0) ** (-np.arange(32, dtype=f) / f(32))).astype(f)
    ang = (inv[i % 32][:, None] * t.astype(f)[None, :]).astype(f)
    put(c1, C1, "cos", np.cos(ang))
    put(c1, C1, "sin", np.sin(ang))
    put(c1, C1, "causal", np.concatenate([np.where(t[None, :] <= qt * P + i[:, None], 0.0, -1.0e30) for qt in range(TT)], 1))
    put(c1, C1, "icnt", np.concatenate([1.0 / np.minimum(t[None, :] + 1, np.array(POOL_WINDOWS)[2 * m + i // 64][:, None])
                                        for m in range(2)], 1))

    perm = np.zeros((P, P))
    perm[i[1::2], i[0::2]] = -1.0
    perm[i[0::2], i[1::2]] = 1.0
    put(c2, C2, "perm", perm)
    inv = (f(10000.0) ** (-np.arange(8, dtype=f) / f(8))).astype(f)
    ang = np.concatenate([(t // 64).astype(f)[:, None] * inv, (t % 64).astype(f)[:, None] * inv], 1).astype(f)
    ang = ang.T[(i % 32) // 2]
    put(c2, C2, "cos", np.cos(ang))
    put(c2, C2, "sin", np.sin(ang))
    put(c2, C2, "rep", i[:, None] % 32 == i[None, :] % 32)
    tri = (i[:, None] <= i[None, :]) / 16.0
    put(c2, C2, "uf", np.concatenate([tri, np.full((P, P), 1 / 16.0)], 1))
    put(c2, C2, "ub", np.concatenate([np.full((P, P), 1 / 16.0), tri.T], 1))
    c = i[:, None] // CH
    put(c2, C2, "capkf", np.where(i[None, :] < CH * (c + 1), CAP, -200.0))
    put(c2, C2, "capkb", np.where(i[None, :] >= CH * c, CAP, -200.0))
    put(c2, C2, "capq", np.where(i[None, :] // CH == c, CAP, -200.0))
    mf = (i[:, None] <= i[None, :]) * 1.0
    put(c2, C2, "mask", np.concatenate([mf, mf, mf.T, mf.T], 1))
    return cc, c1, c2


def bias_index():
    t = np.arange(T)
    r, c = t // 64, t % 64
    start = np.clip(c - 8, 0, 64 - 16)
    inside = (c[None, :] >= start[:, None]) & (c[None, :] < start[:, None] + 16)
    dr = r[None, :] - r[:, None] + 7
    dc = np.clip(c[None, :] - c[:, None] + 15, 0, 30)
    return dr, dc, inside


def kernel(**inp):
    import concourse.bacc as bacc
    from concourse.bass_utils import run_bass_kernel_spmd

    a = {k: np.ascontiguousarray(v) for k, v in inp.items()}
    f = np.float32
    ws = np.zeros((NU, P, UNIT), f)
    at = 0

    def put(units):
        nonlocal at
        for u in units:
            assert u.shape[1] == WIDTHS[at]
            ws[at, :, 0:u.shape[1]] = u
            at += 1

    def tiles(w, n=None):
        for m in range((w.shape[1] if n is None else n) // P):
            put(fm_units(w, m * P + np.arange(P)))

    taken = 0

    def rows(n):
        nonlocal taken
        for _ in range(n):
            l, c = taken // ROW_TILES, taken % ROW_TILES * 512
            put(tm_units(a["w_ada_2"][l][:, c:c + 512]))
            taken += 1

    cols, v = columns1()
    for l in range(DEPTH):
        w = a["w_in"][l]
        rows(2)
        put(tm_units(w[:, v:v + 512]))
        for c in cols:
            put(fm_units(w, c))
        rows(3)
        tiles(a["w_out"][l])
        pw = a["ple_w"][l].reshape(2, P, KS, P).transpose(1, 2, 0, 3)
        put([pw[:, 4 * u:4 * u + 4].reshape(P, -1) for u in range(2)])
        rows(1)
        tiles(a["ple_gate_w"][l])
    rows(1)
    cols2, v, nv = columns2()
    for l in range(DEPTH):
        w = a["w_in_2"][l]
        rows(2 if l == 0 else 0)
        put(tm_units(w[:, v:v + VW]))
        put(tm_units(w[:, nv:nv + VW]))
        for c in cols2:
            put(fm_units(w, c))
        rows(1 + GH if l == 0 else 0)
        tiles(a["w_out_2"][l])
        rows(2 if l == 0 else 0)
        for m in range(FT):
            for o in (0, FFN):
                put(fm_units(a["ffn_w_up_2"][l], o + m * P + np.arange(P)))
        tiles(a["ffn_w_down_2"][l])
    assert at == NU

    prm = np.zeros((P, NPC), f)

    def par(name, vec):
        vec = vec.reshape(-1, P).T
        prm[:, PC[name]:PC[name] + vec.shape[1]] = vec

    for l in range(DEPTH):
        par(f"norm{l}", a["norm_g"][l])
        b = a["b_in"][l]
        par(f"bin{l}", np.concatenate([np.where(c >= 0, b[c], f(0)) for c in cols]))
        prm[:, PC[f"dww{l}"]:PC[f"dww{l}"] + 62] = a["conv_dw_w"][l].reshape(CONV_K, 2, P).transpose(2, 1, 0).reshape(P, 62)
        for name, src in (("dwb", "conv_dw_b"), ("lng", "conv_ln_g"), ("lnb", "conv_ln_b"), ("pwb", "conv_pw_b"),
                          ("poolb", "pool_b"), ("pools", "pool_scale"), ("nmix", "norm_mix_g_2"), ("nffn", "norm_ffn_g_2"),
                          ("bada", "b_ada_2"), ("scbias", "sc_conv_b_2"), ("fb", "ffn_conv_b_2"), ("scw", "sc_conv_w_2"),
                          ("fw", "ffn_conv_w_2")):
            par(f"{name}{l}", a[src][l])
        par(f"glag{l}", np.concatenate([a["gla_norm_g_2"][l]] * 2))
    par("fin1", a["final_norm_g"])
    par("fin2", a["final_norm_g_2"])
    cv = np.stack([a["c_2"][0], a["c_ctx_2"]], 1)
    prm[:, PC["cvec"]:] = cv.reshape(KS, P, 2).transpose(1, 0, 2).reshape(P, 2 * KS)

    mat1 = np.zeros((DEPTH, P, 768), f)
    mat1[:, :, 0:512] = a["conv_pw_w"].reshape(DEPTH, 2, P, 256).transpose(0, 2, 1, 3).reshape(DEPTH, P, 512)
    for g in range(4):
        r, o = 64 * (g % 2), 512 + P * (g // 2) + 64 * (g % 2)
        mat1[:, r:r + 64, o:o + 64] = a["pool_w"][:, g]
    wgp = np.zeros((DEPTH, 64, 192), f)
    wgp[:, 0:16], wgp[:, 16] = a["gla_wg2_fw_2"], a["gla_bg_fw_2"]
    wgp[:, 32:48], wgp[:, 48] = a["gla_wg2_bw_2"], a["gla_bg_bw_2"]
    dr, dc, inside = bias_index()
    nab = np.where(inside, a["na_rpb_2"][:, :, dr, dc], f(-1.0e30)).astype(f)
    nab = np.ascontiguousarray(nab.reshape(DEPTH, NAH, TT, P, T).transpose(0, 1, 3, 2, 4))

    def slabs(x):
        return x.T.reshape(-1, P, x.shape[0]).transpose(1, 0, 2)

    xt = np.ascontiguousarray(np.concatenate([slabs(a["x"][0]), slabs(a["ctx_2"][0])], 2))
    ptin = np.ascontiguousarray(np.stack([slabs(a["p"][l, 0]) for l in range(DEPTH)]))
    bv1 = np.ascontiguousarray(a["b_in"][:, columns1()[1]:columns1()[1] + 512])
    cc, c1, c2 = constants()

    nc = bacc.Bacc("TRN2", target_bir_lowering=False, num_devices=1)
    arrays = dict(ws=ws, prm=prm, cc=cc, c1=c1, c2=c2, xt=xt, ptin=ptin, mat1=mat1, bv1=bv1, wgp=wgp, nab=nab)
    aps = {k: nc.dram_tensor(f"in_{k}", v.shape, F32, kind="ExternalInput").ap() for k, v in arrays.items()}
    out = nc.dram_tensor("out_x", (P, KS, T), F32, kind="ExternalOutput").ap()
    build(nc, out=out, **aps)
    r = run_bass_kernel_spmd(nc, [{f"in_{k}": v for k, v in arrays.items()}], core_ids=[0])
    y = r.results[0]["out_x"]
    return np.ascontiguousarray(y.transpose(2, 1, 0).reshape(1, T, D))
```

```python
from contextlib import ExitStack

import numpy as np

import concourse.bass as bass
from concourse import mybir

F32 = mybir.dt.float32
F32R = mybir.dt.float32r
ALU = mybir.AluOpType
ACT = mybir.ActivationFunctionType
AX_X = mybir.AxisListType.X

P = 128
T = 256
TC = 512
TT = T // P
D = 1024
KS = D // P
DEPTH = 2
UNIT = 1024
EPS = 1e-6

CONV_W, CONV_K, POOL_W = 256, 31, 256
POOL_WINDOWS = (2, 4, 8, 16)
HD, NH1 = 64, 8
IDXH = 4
TOPK = T // 4
PLE = 256
TILES1 = ["val"] * 2 + ["glu"] * 2 + ["q"] * 4 + ["k"] * 4 + ["qi"] * 2 + ["ki", "wi"] + \
    ["pin"] * 2 + ["pgate"] * 2 + ["cgate"] * 2 + ["agate"] * 4
Z1 = {n: TILES1.index(n) for n in TILES1}
NZ1 = len(TILES1)
TAPS_AT = {6: (0, 3), 7: (3, 6), 10: (6, 8), 11: (8, 10), 14: (10, 12), 15: (12, 14), 24: (14, 16),
           25: (16, 17)}
TAPS_LEFT = max(hi for _, hi in TAPS_AT.values())
ROPE_AT = {7: 0, 8: 1, 11: 2, 12: 3}

GH, GDK, GDV = 6, 32, 64
NAH = 6
FFN = 2816
FT = FFN // P
CH = 32
NCH = P // CH
CAP = 80.0
TILES2 = ["gqa", "gka", "gqk", "glr"] + ["scb"] * 2 + ["scc"] * 2 + ["scx"] * 2 + ["r"] * 3 + \
    ["nk"] * 3 + ["nq"] * 3
Z2 = {n: TILES2.index(n) for n in TILES2}
NZ2 = len(TILES2)
LAT_ONLY = ("nq", "r", "scb", "scc", "scx")
VW = 384

def param_columns():
    cols, at = {}, 0
    def add(name, n):
        nonlocal at
        cols[name] = at
        at += n
    for l in range(DEPTH):
        for name, n in (("norm", KS), ("bin", NZ1), ("dww", 2 * CONV_K), ("dwb", 2), ("lng", 2), ("lnb", 2),
                        ("pwb", 2), ("poolb", 2), ("pools", 2)):
            add(f"{name}{l}", n)
    add("fin1", KS)
    for l in range(DEPTH):
        for name, n in (("nmix", KS), ("nffn", KS), ("bada", 48), ("glag", 1), ("scw", 6), ("scbias", 2),
                        ("fw", 3 * 2 * FT), ("fb", 2 * FT)):
            add(f"{name}{l}", n)
    add("fin2", KS)
    add("cvec", 2 * KS)
    return cols, at


PC, NPC = param_columns()

ROW_U = 4
ROW_TILES = 12


def unit_widths():
    w, plain = [], []

    def add(widths):
        w.extend(widths)
        plain.extend([False] * len(widths))

    def rows(n):
        w.extend([UNIT] * (n * ROW_U))
        plain.extend([True] * (n * ROW_U))

    for _ in range(DEPTH):
        rows(2)
        add([UNIT] * (4 + NZ1))
        rows(3)
        add([UNIT] * (KS + 2))
        rows(1)
        add([UNIT] * KS)
    rows(1)
    for l in range(DEPTH):
        rows(2 if l == 0 else 0)
        add([2 * VW] * 8 + [UNIT] * NZ2)
        rows(1 + GH if l == 0 else 0)
        add([UNIT] * KS)
        rows(2 if l == 0 else 0)
        add([UNIT] * 2 * FT + [UNIT, UNIT, 6 * P] * KS)
    return w, plain


WIDTHS, PLAIN = unit_widths()
NU = len(WIDTHS)
SPLIT_UNITS = [u for u in range(NU) if not PLAIN[u]]
SPLIT_NO = [sum(not p for p in PLAIN[:u]) for u in range(NU)]
RAW, SPL, AHEAD = 4, 3, 2

def layout(names):
    out, at = {}, 0
    for name, n in names:
        out[name] = (at, n)
        at += n
    return out, at


CC, NCC = layout([("ident", P), ("ones", P), ("ones256", P), ("blk", P), ("glrone", 1)])
C1, NC1 = layout([("perm", P), ("cos", T), ("sin", T), ("causal", 2 * T), ("icnt", 2 * T)])
C2, NC2 = layout([("perm", P), ("cos", T), ("sin", T), ("rep", P), ("uf", T), ("ub", T),
                  ("capkf", P), ("capkb", P), ("capq", P), ("mask", 4 * P)])


def build(nc, ws, prm, cc, c1, c2, xt, ptin, mat1, bv1, wgp, nab, out):
    with ExitStack() as ctx:
        sems = {}

        def S(name):
            if name not in sems:
                sems[name] = ctx.enter_context(nc.semaphore(name))
            return sems[name]

        def sb(stack, name, shape, dt=F32):
            return stack.enter_context(nc.sbuf_tensor(name, shape, dt))

        X = sb(ctx, "X", [P, KS, TC])
        NHI = sb(ctx, "NHI", [P, KS, TC], F32R)
        NLO = sb(ctx, "NLO", [P, KS, TC], F32R)
        RAWB = sb(ctx, "RAWB", [P, RAW, UNIT])
        WHI = sb(ctx, "WHI", [P, SPL, UNIT], F32R)
        WLO = sb(ctx, "WLO", [P, SPL, UNIT], F32R)
        CST = sb(ctx, "CST", [P, NCC])
        PRM = sb(ctx, "PRM", [P, NPC])
        MOD = sb(ctx, "MOD", [P, DEPTH, 48, 2])
        GM = sb(ctx, "GM", [P, KS, 2])
        CV2 = sb(ctx, "CV2", [P, KS, 2])
        ROWS = sb(ctx, "ROWS", [2, 512])

        def cst(name):
            a, n = CC[name]
            return CST[:, a:a + n]

        def prm_col(name, i=0, n=1):
            a = PC[name] + i
            return PRM[:, a:a + n]

        st = ExitStack()
        K1 = sb(st, "K1", [P, NC1])
        Z = sb(st, "Z", [P, NZ1, T])
        V1 = sb(st, "V1", [P, TT, 512])
        BV = sb(st, "BV", [P, 512])
        M1 = sb(st, "M1", [P, 768])
        PLEH = sb(st, "PLEH", [P, 2, 2, T], F32R)
        PIN = sb(st, "PIN", [P, 2, T])
        RT = sb(st, "RT", [P, 512])
        WI = sb(st, "WI", [P, TT, IDXH])
        RL = sb(st, "RL", [P, 2, T])
        SC = sb(st, "SC", [P, TT, T])
        MB = sb(st, "MB", [P, TT, T])
        M8 = sb(st, "M8", [P, 8])
        L1 = sb(st, "L1", [P, 3, T])
        P1 = sb(st, "P1", [P, 3, T])
        PT1 = sb(st, "PT1", [P, 2, T])
        ST1 = sb(st, "ST1", [P, 3, 4])
        OB = sb(st, "OB", [P, 4, T])
        UP = sb(st, "UP", [P, 2, CONV_K - 1 + T])
        CV = sb(st, "CV", [P, 2, T])
        CT = sb(st, "CT", [P, 2, T])
        PD = sb(st, "PD", [P, 2, T])
        PP = sb(st, "PP", [P, 2, 16 + T])
        PS = sb(st, "PS", [P, 4, 2, 16 + T])
        PB = sb(st, "PB", [P, 2])
        GT1 = sb(st, "GT1", [P, 8, T])
        SG = sb(st, "SG", [P, 2, T])
        Y1 = sb(st, "Y1", [P, KS, T])
        MS1 = sb(st, "MS1", [P, 4, T])
        st.close()

        mix = ExitStack()
        K2 = sb(mix, "K2", [P, NC2])
        ZB = sb(mix, "ZB", [P, NZ2, TC])
        V2 = sb(mix, "V2", [P, 4, 2 * VW])
        st = ExitStack()
        WG = sb(st, "WG", [64, 192])
        GT = sb(st, "GT", [P, 4, VW])
        GTA = sb(st, "GTA", [P, 4, VW])
        KQ = sb(st, "KQ", [P, 2, TC])
        BM = sb(st, "BM", [P, 2, 6])
        BC = sb(st, "BC", [P, 2, TC])
        EX = sb(st, "EX", [P, 1280])
        EY = sb(st, "EY", [P, 2, 1280])
        E0 = sb(st, "E0", [64, TC])
        AM = sb(st, "AM", [P, TC])
        AF = sb(st, "AF", [P, 2, 2, T])
        A0 = sb(st, "A0", [P, 2, T])
        OM = sb(st, "OM", [P, 3, TC])
        st.close()
        st = ExitStack()
        NB = sb(st, "NB", [P, 2, TT, TC])
        L2 = sb(st, "L2", [P, 3, TC])
        P2 = sb(st, "P2", [P, 3, TC])
        PT2 = sb(st, "PT2", [P, 2, TC])
        ST2 = sb(st, "ST2", [P, 3, 4])
        OY = sb(st, "OY", [P, 3, TC])
        st.close()
        mix.close()
        st = ExitStack()
        SQ2 = sb(st, "SQ2", [P, KS, TC])
        TB2 = sb(st, "TB2", [P, KS, TC])
        MS2 = sb(st, "MS2", [P, 4, TC])
        st.close()
        st = ExitStack()
        HHI = sb(st, "HHI", [P, FT, TC], F32R)
        HLO = sb(st, "HLO", [P, FT, TC], F32R)
        CF = sb(st, "CF", [P, 2, 3, TC])
        SQF = sb(st, "SQF", [P, 4, TC])
        st.close()

        bank = [ctx.enter_context(nc.psum_tensor(f"bank{i}", [P, 512], F32)) for i in range(8)]

        def c1v(name):
            a, n = C1[name]
            return K1[:, a:a + n]

        def c2v(name):
            a, n = C2[name]
            return K2[:, a:a + n]

        def bc(ap, n):
            return ap.unsqueeze(1).broadcast_to([ap.shape[0], n, ap.shape[1]])

        def bl(ap, n):
            return ap.unsqueeze(2).broadcast_to([ap.shape[0], ap.shape[1], n])

        def half(h):
            return slice(64 * (h % 2), 64 * (h % 2) + 64)

        def gates4(i):
            g = GTA[:].rearrange("p a b -> p (a b)")[:, (i % 3) * 512:(i % 3 + 1) * 512]
            return g.rearrange("p (i c k) -> p i c k", i=4, c=NCH)

        def exps(d):
            if d == 0:
                return EX[:]
            return ZB[:, Z2["scb"]:Z2["scb"] + 4, :].rearrange("p a t -> p (a t)")[:, 0:1280]

        def gate_part(g, i):
            s, d = i // 2, i % 2
            return g[:, 2 * s:2 * s + 2, d * 192:(d + 1) * 192]

        class Side:

            def __init__(self, eng, name):
                self.eng, self.name, self.seen, self.u, self.tile = eng, name, {}, 0, 0

            def nth(self, name, k=1):
                self.seen[name] = self.seen.get(name, 0) + k
                return self.seen[name]

            def next_tile(self):
                self.tile += 1
                return (self.tile - 1) % 4

        ITEMS1 = [(h, qt, P * (qt + 1), False) for h in range(NH1) for qt in range(TT)]

        def items2(uc):
            return [(h, qt, T if own else TC, own) for h in range(NAH) for own in ((False, True) if uc else (False,))
                    for qt in range(TT)]

        def ends_pair(it, uc=False):
            return it[0] % 2 == 1 and it[1] == TT - 1 and it[3] == uc

        SH1, SC1, G1, SH2, SC2, G2 = (KS * i for i in range(6))

        block = ctx.enter_context(nc.Block())

        @block.sync
        def _(sp):
            for u in range(NU):
                if u >= RAW:
                    if PLAIN[u - RAW]:
                        sp.wait_ge(S("unit_done"), u - RAW + 1)
                    else:
                        sp.wait_ge(S("lo_ready"), SPLIT_NO[u - RAW] + 1)
                w = WIDTHS[u]
                sp.dma_start(RAWB[:, u % RAW, 0:w], ws[u, :, 0:w]).then_inc(S(f"raw{u % RAW}"), 16)
            sp.wait_ge(S("x_new"), KS * (DEPTH + 2))
            sp.dma_start(out, X[:, :, 0:T]).then_inc(S("stored"), 16)
            sp.wait_ge(S("stored"), 16)

        @block.gpsimd
        def _(pool):
            me = Side(pool, "pool")

            pool.dma_start(CST[:], cc).then_inc(S("ld_cst"), 16)
            pool.dma_start(K1[:], c1).then_inc(S("ld_c1"), 16)
            nc.gpsimd.memset(PP[:, :, 0:16], 0.0)
            nc.gpsimd.memset(PS[:, :, :, 0:16], 0.0).then_inc(S("pool_chain"), 1)
            pool.wait_ge(S("pool_chain"), me.nth("pool_chain"))
            pool.wait_ge(S("ld_prm"), 16)
            pool.wait_ge(S("ld_c1"), 16)
            for l in range(DEPTH):
                if l > 0:
                    pool.wait_ge(S("x_new"), me.nth("x_new", KS))
                pool.dma_start(BV[:], bv1[l:l + 1, :].broadcast_to([P, 512])).then_inc(S("ld_p1"), 16)
                pool.dma_start(M1[:], mat1[l]).then_inc(S("ld_p1"), 16)
                pool.dma_start(PIN[:], ptin[l]).then_inc(S("ld_p1"), 16)
                if l == 0:
                    pool.dma_start(X[:, :, T:TC], xt[:, :, T:TC]).then_inc(S("ld_ctx"), 16)
                pool.wait_ge(S("z_freed"), me.nth("z_freed", 18))
                nc.gpsimd.tensor_copy(PP[:, :, 16:], Z[:, Z1["pin"]:Z1["pin"] + 2, :]).then_inc(S("pool_chain"), 1)
                pool.wait_ge(S("pool_chain"), me.nth("pool_chain"))
                for j in range(4):
                    s = PP[:] if j == 0 else PS[:, j - 1, :, :]
                    nc.gpsimd.tensor_tensor(PS[:, j, :, 16:], s[:, :, 16:], s[:, :, 16 - (1 << j):16 + T - (1 << j)],
                                            ALU.add).then_inc(S("pool_chain"), 1)
                    pool.wait_ge(S("pool_chain"), me.nth("pool_chain"))
                for g in range(4):
                    r, m = half(g), g // 2
                    nc.gpsimd.tensor_tensor(PD[r, m, :], PS[r, g, m, 16:], c1v("icnt")[r, m * T:(m + 1) * T],
                                            ALU.mult).then_inc(S("pool_chain"), 1)
                    pool.wait_ge(S("pool_chain"), me.nth("pool_chain"))
                nc.gpsimd.tensor_tensor(PB[:], prm_col(f"poolb{l}", 0, 2), prm_col(f"pools{l}", 0, 2), ALU.mult).then_inc(S("pool_chain"), 1)
                pool.wait_ge(S("pool_chain"), me.nth("pool_chain"))
                nc.gpsimd.tensor_tensor(PD[:], PD[:], PP[:, :, 16:], ALU.subtract).then_inc(S("pool_ready"), 1)
                pool.wait_ge(S("pool_ready"), me.nth("pool_ready"))
                pool.wait_ge(S("z_freed"), me.nth("z_freed", NZ1 - 18))
            pool.wait_ge(S("x_split"), me.nth("x_split", KS * DEPTH))
            pool.wait_ge(S("s_freed"), me.nth("s_freed", len(ITEMS1) * DEPTH))
            pool.wait_ge(S("y_split"), me.nth("y_split", KS * DEPTH))
            for l in range(DEPTH):
                pool.wait_ge(S("x_split"), me.nth("x_split", KS))
                pool.dma_start(K2[:], c2).then_inc(S("ld_c2"), 16)
                pool.dma_start(WG[:], wgp[l]).then_inc(S("ld_c2"), 16)
                pool.wait_ge(S("g_ready"), me.nth("g_ready", 4))
                for i in range(2 * GH):
                    h, d = i // 2, i % 2
                    if i >= 3:
                        pool.wait_ge(S("b_ready"), me.nth("b_ready"))
                    g = GT[:, :, d * 192 + h * GDK:d * 192 + (h + 1) * GDK]
                    nc.gpsimd.tensor_copy(gates4(i), g.unsqueeze(2).broadcast_to([P, 4, NCH, GDK])).then_inc(S("g4_ready"), 1)
                pool.wait_ge(S("b_ready"), me.nth("b_ready", 3))
                pool.wait_ge(S("gpv_done"), me.nth("gpv_done", GH))
                per_head = TT * (2 if l < DEPTH - 1 else 1)
                for h in range(NAH):
                    if h >= 2:
                        pool.wait_ge(S("s_freed"), me.nth("s_freed", per_head))
                    pool.dma_start(NB[:, h % 2, :, 0:T], nab[l, h]).then_inc(S(f"ld_nb{h % 2}"), 16)
                pool.wait_ge(S("s_freed"), me.nth("s_freed", 2 * per_head))
                pool.wait_ge(S("y_split"), me.nth("y_split", KS))
                pool.wait_ge(S("x_split"), me.nth("x_split", KS))

        @block.tensor
        def _(pe):
            me = Side(pe, "pe")
            held, made = {}, {}

            def read_by(b, freed):
                made[freed] = made.get(freed, 0) + 1
                held[b] = (S(freed), made[freed])

            def unit():
                u = me.u
                me.u += 1
                k = SPLIT_NO[u]
                pe.wait_ge(S("lo_ready"), k + 1)
                return WHI[:, k % SPL, :], WLO[:, k % SPL, :]

            def rows(b, s0=0, s1=KS):
                if s0 == 0 and b in held:
                    pe.wait_ge(*held[b])
                for s in range(s0, s1):
                    u = me.u
                    if s % 2 == 0:
                        pe.wait_ge(S(f"raw{u % RAW}"), 16 * (u // RAW + 1))
                    ins = nc.tensor.matmul(bank[b][0:2, :], CV2[:, s, :], RAWB[:, u % RAW, (s % 2) * 512:(s % 2 + 1) * 512],
                                           start=(s == 0), stop=(s == KS - 1))
                    if s % 2 == 1:
                        ins.then_inc(S("unit_done"), 1)
                        me.u += 1

            def columns(b):
                pe.wait_ge(S("rows_copied"), me.nth("rows_copied"))
                for j in range(4):
                    ins = nc.tensor.matmul(bank[b][:, 2 * j:2 * j + 2], ROWS[:, j * P:(j + 1) * P], cst("ident")[0:2, 0:2],
                                           start=True, stop=True)
                ins.then_inc(S("cols_ready"), 1)
                read_by(b, "mod_done")

            def fm(slabs, n, rhs, freed, given=None, given_from=0, order=None):
                b = me.next_tile()
                if b in held:
                    pe.wait_ge(*held[b])
                o = bank[b][:, 0:n]
                order = list(order or range(slabs))
                for i, s in enumerate(order):
                    if i % 8 == 0:
                        hi, lo = unit()
                    if given is not None and i >= given_from:
                        pe.wait_ge(S(given), me.nth(given))
                    w = slice((s % 8) * P, (s % 8 + 1) * P)
                    xh, xl = rhs(s)
                    nc.tensor.matmul(o, hi[:, w], xh, start=(i == 0), stop=False)
                    nc.tensor.matmul(o, hi[:, w], xl, start=False, stop=False)
                    ins = nc.tensor.matmul(o, lo[:, w], xh, start=False, stop=(i == slabs - 1))
                    if i % 8 == 7 and i != slabs - 1:
                        ins.then_inc(S("unit_done"), 1)
                ins.then_inc(S("unit_done"), 1)
                read_by(b, freed)

            def tm(tts, w, given=None):
                for b in range(tts):
                    if b in held:
                        pe.wait_ge(*held[b])
                for u in range(4):
                    hi, lo = unit()
                    for k in range(2):
                        s, c = 2 * u + k, slice(k * w, (k + 1) * w)
                        if given is not None:
                            pe.wait_ge(S(given), me.nth(given))
                        for t in range(tts):
                            o = bank[t][:, 0:w]
                            xh, xl = NHI[:, s, t * P:(t + 1) * P], NLO[:, s, t * P:(t + 1) * P]
                            nc.tensor.matmul(o, xh, hi[:, c], start=(s == 0), stop=False)
                            nc.tensor.matmul(o, xl, hi[:, c], start=False, stop=False)
                            ins = nc.tensor.matmul(o, xh, lo[:, c], start=False, stop=(s == 7))
                    ins.then_inc(S("unit_done"), 1)
                for b in range(tts):
                    read_by(b, "v_freed")

            def x_lat(s):
                return NHI[:, s, 0:T], NLO[:, s, 0:T]

            def x_all(s):
                return NHI[:, s, :], NLO[:, s, :]

            def stats(n, sq, p0=0, p1=KS // 2):
                if p0 == 0 and 4 in held:
                    pe.wait_ge(*held[4])
                for p in range(p0, p1):
                    pe.wait_ge(S("sq_ready"), me.nth("sq_ready"))
                    for s in (2 * p, 2 * p + 1):
                        ins = nc.tensor.matmul(bank[4][:, 0:n], cst("ones"), sq[:, s % sq.shape[1], 0:n], start=(s == 0), stop=(s == KS - 1))
                    if p < KS // 2 - 1:
                        ins.then_inc(S("sq_used"), 1)
                    else:
                        ins.then_inc(S("ms_ready"), 1)
                        read_by(4, "ms_eps")

            def stats_behind(m, n, sq):
                if m in (5, 7):
                    stats(n, sq, (m - 5) // 2, (m - 3) // 2)
                if m == 7:
                    stats(n, sq, 2)

            def attention(items, score, p, out, uc=False, between=None):
                n = len(items)
                for i in range(n + 3):
                    if i < n:
                        if i % 2 in held:
                            pe.wait_ge(*held[i % 2])
                        score(items[i], bank[i % 2]).then_inc(S("s_ready"), 1)
                        read_by(i % 2, "s_freed")
                    if between is not None:
                        between(i)
                    if 2 <= i < n + 2:
                        j = i - 2
                        b = 2 + j % 2
                        pe.wait_ge(S("p_ready"), me.nth("p_ready"))
                        if b in held:
                            pe.wait_ge(*held[b])
                        for k in range(items[j][2] // P):
                            ins = nc.tensor.transpose(bank[b][:, k * P:(k + 1) * P], p[:, j % 3, k * P:(k + 1) * P], cst("ident"))
                        ins.then_inc(S("pt_ready"), 1)
                        read_by(b, "pt_freed")
                    if i >= 3:
                        j = i - 3
                        h, qt, nk, own = it = items[j]
                        b = 6 + (h // 2) % 2
                        pe.wait_ge(S("pt_freed"), me.nth("pt_freed"))
                        if h % 2 == 0 and qt == 0 and not own:
                            if b in held:
                                pe.wait_ge(*held[b])
                        ins = out(j, it, bank[b])
                        if ends_pair(it, uc):
                            ins.then_inc(S("pv_done"), 1)
                            read_by(b, "o_freed")
                        else:
                            ins.then_inc(S("pv_done"), 1)

            pe.wait_ge(S("ld_cst"), 16)
            pe.wait_ge(S("c_ready"), me.nth("c_ready"))

            for l in range(DEPTH):
                rows(5)
                if l == 0:
                    stats(T, Y1)
                rows(6)
                columns(5)
                tm(TT, 512, "x_split")
                columns(6)

                def rotate(g):
                    k, b = 2 if g < 5 else 1, 4 + g % 2
                    if b in held:
                        pe.wait_ge(*held[b])
                    ins = nc.tensor.matmul(bank[b][:, 0:k * T], c1v("perm"),
                                           Z[:, Z1["q"] + 2 * g:Z1["q"] + 2 * g + k, :].rearrange("p a t -> p (a t)"), start=True, stop=True)
                    ins.then_inc(S("rot_ready"), 1)
                    read_by(b, "rot_freed")

                def index(i):
                    qt, h, b = i // IDXH, i % IDXH, 6 + i % 2
                    nk = P * (qt + 1)
                    if b in held:
                        pe.wait_ge(*held[b])
                    ins = nc.tensor.matmul(bank[b][:, 0:nk], Z[half(h), Z1["qi"] + h // 2, qt * P:(qt + 1) * P],
                                           Z[half(h), Z1["ki"], 0:nk], start=True, stop=True)
                    ins.then_inc(S("idx_ready"), 1)
                    read_by(b, "idx_freed")

                for t in range(NZ1):
                    fm(KS, T, x_lat, "z_freed")
                    if t == 7:
                        pe.wait_ge(S("ld_c1"), 16)
                    if t in ROPE_AT:
                        pe.wait_ge(S("z_freed"), me.nth("z_freed", 6 if t == 7 else 2))
                        rotate(ROPE_AT[t])
                    if t == 16:
                        pe.wait_ge(S("z_freed"), me.nth("z_freed", 4))
                        rotate(4)
                        rotate(5)
                        for qt in range(TT):
                            if 6 + qt in held:
                                pe.wait_ge(*held[6 + qt])
                            ins = nc.tensor.transpose(bank[6 + qt][:, 0:P], Z[:, Z1["wi"], qt * P:(qt + 1) * P], cst("ident"))
                            ins.then_inc(S("wi_ready"), 1)
                            read_by(6 + qt, "wi_freed")
                    if t == 17:
                        pe.wait_ge(S("qi_roped"), me.nth("qi_roped"))
                    if 17 <= t < 21:
                        index(2 * (t - 17))
                        index(2 * (t - 17) + 1)
                pe.wait_ge(S("ld_p1"), 16 * (3 * l + 3))
                pe.wait_ge(S("z_freed"), me.nth("z_freed", NZ1 - 16))
                pe.wait_ge(S("rope_done"), me.nth("rope_done"))

                def score1(it, bk):
                    h, qt, nk, _ = it
                    return nc.tensor.matmul(bk[:, 0:nk], Z[half(h), Z1["q"] + h // 2, qt * P:(qt + 1) * P],
                                            Z[half(h), Z1["k"] + h // 2, 0:nk], start=True, stop=True)

                def pv1(j, it, bk):
                    h, qt, nk, _ = it
                    for kt in range(nk // P):
                        ins = nc.tensor.matmul(bk[half(h), qt * P:(qt + 1) * P], V1[:, kt, h * HD:(h + 1) * HD],
                                               PT1[:, j % 2, kt * P:(kt + 1) * P], start=(kt == 0), stop=(kt == nk // P - 1))
                    return ins

                def channel_mean(src, given, freed):
                    pe.wait_ge(S(given), me.nth(given))
                    if 5 in held:
                        pe.wait_ge(*held[5])
                    for k in range(2):
                        ins = nc.tensor.matmul(bank[5][:, 0:T], cst("ones256"), src[:, k, :], start=(k == 0), stop=(k == 1))
                    ins.then_inc(S("cstat_ready"), 1)
                    read_by(5, freed)

                def beside(i):
                    if i < 2 * KS:
                        rows(5 - i // KS, i % KS, i % KS + 1)
                    if i == 10:
                        columns(5)
                    if i == 12:
                        channel_mean(CV, "conv_ready", "xc_ready")
                    if i == 15:
                        channel_mean(CT, "conv_sq", "cvar_eps")

                attention(ITEMS1, score1, P1, pv1, between=beside)
                pe.wait_ge(S("pool_ready"), me.nth("pool_ready"))
                for m in range(2):
                    if 2 + m in held:
                        pe.wait_ge(*held[2 + m])
                    ins = nc.tensor.matmul(bank[2 + m][:, 0:T], M1[:, 512 + m * P:512 + (m + 1) * P], PD[:, m, :],
                                           start=True, stop=True)
                    ins.then_inc(S("pw_ready"), 1)
                    read_by(2 + m, "pw_freed")
                rows(5)
                columns(4)
                pe.wait_ge(S("conv_silu"), me.nth("conv_silu"))
                for m in range(2):
                    if m in held:
                        pe.wait_ge(*held[m])
                    for k in range(2):
                        ins = nc.tensor.matmul(bank[m][:, 0:T], M1[:, k * T + m * P:k * T + (m + 1) * P], CV[:, k, :],
                                               start=(k == 0), stop=(k == 1))
                    ins.then_inc(S("pw_ready"), 1)
                    read_by(m, "pw_freed")
                for m in range(KS):
                    if m == 0:
                        fm(KS, T, x_lat, "wo_freed", "y_split", order=[2, 3, 4, 5, 6, 7, 0, 1])
                    else:
                        fm(KS, T, x_lat, "wo_freed")
                    if m == 0:
                        columns(5)
                pe.wait_ge(S("ple_split"), me.nth("ple_split"))
                for u in range(2):
                    hi, lo = unit()
                    for j in range(4):
                        b = me.next_tile()
                        if b in held:
                            pe.wait_ge(*held[b])
                        for k in range(2):
                            w = slice((2 * j + k) * P, (2 * j + k + 1) * P)
                            nc.tensor.matmul(bank[b][:, 0:T], hi[:, w], PLEH[:, 0, k, :], start=(k == 0), stop=False)
                            nc.tensor.matmul(bank[b][:, 0:T], hi[:, w], PLEH[:, 1, k, :], start=False, stop=False)
                            ins = nc.tensor.matmul(bank[b][:, 0:T], lo[:, w], PLEH[:, 0, k, :], start=False, stop=(k == 1))
                        ins.then_inc(S("unit_done" if j == 3 else "ple_ready"), 1)
                        read_by(b, "ple_freed")
                rows(5)
                for m in range(KS):
                    fm(KS, T, lambda s: (NHI[:, s, T:TC], NLO[:, s, T:TC]), "gate_freed", "h_split" if m == 0 else None)
                    if m == 0:
                        columns(5)
                    stats_behind(m, T, Y1)
            rows(5)

            for l in range(DEPTH):
                uc = l < DEPTH - 1
                n, rhs = (TC, x_all) if uc else (T, x_lat)
                if l == 0:
                    stats(TC, SQ2)
                    columns(5)
                    rows(6)
                    rows(7)
                    columns(6)
                for v in range(2):
                    tm(4, VW, "x_split" if v == 0 else None)
                    if l == 0 and v == 0:
                        columns(7)

                def gates(i):
                    q, d, b = i // 2, i % 2, (6, 7, 4, 5)[i]
                    if b in held:
                        pe.wait_ge(*held[b])
                    r = slice(32 * d, 32 * d + 17)
                    for t in range(2):
                        ins = nc.tensor.matmul(bank[b][:, t * 192:(t + 1) * 192],
                                               ZB[r, Z2["glr"], (2 * q + t) * P:(2 * q + t + 1) * P], WG[r, :],
                                               start=True, stop=True)
                    ins.then_inc(S("gate_ready"), 1)
                    read_by(b, "g_ready")

                def sums(h):
                    for d in range(2):
                        pe.wait_ge(S("g4_ready"), me.nth("g4_ready"))
                        b = (6 if h == 0 else 2) + d
                        if b in held:
                            pe.wait_ge(*held[b])
                        u = c2v("uf") if d == 0 else c2v("ub")
                        for q in range(2):
                            for k in range(2):
                                t = k if d == 0 else 1 - k
                                lhs = gates4(2 * h + d)[:, 2 * q + t, :, :].rearrange("p c k -> p (c k)")
                                if k == 0:
                                    o, r = bank[b][:, q * T:(q + 1) * T], u
                                elif d == 0:
                                    o, r = bank[b][:, q * T + P:(q + 1) * T], u[:, 0:P]
                                else:
                                    o, r = bank[b][:, q * T:q * T + P], u[:, P:T]
                                ins = nc.tensor.matmul(o, lhs, r, start=(k == 0), stop=(k == 1))
                        ins.then_inc(S("b_ready"), 1)
                        read_by(b, "b_copied")

                def keys_queries(h):
                    for w in range(2):
                        if h < 4:
                            t, r0 = 1 - w, 32 * h
                        else:
                            t, r0 = 2, 32 * (h - 4) + (64 if w == 0 else 0)
                        b = (4 if h == 0 else 0) + w
                        if b in held:
                            pe.wait_ge(*held[b])
                        ins = nc.tensor.matmul(bank[b][:], c2v("rep")[r0:r0 + 32, :], ZB[r0:r0 + 32, t, :], start=True, stop=True)
                        ins.then_inc(S("kq_ready"), 1)
                        read_by(b, "kq_freed")

                def output_mean():
                    pe.wait_ge(S("osq_ready"), me.nth("osq_ready"))
                    if 5 in held:
                        pe.wait_ge(*held[5])
                    ins = nc.tensor.matmul(bank[5][:, 0:n], cst("blk"), OM[:, 0, 0:n], start=True, stop=True)
                    ins.then_inc(S("oms_ready"), 1)
                    read_by(5, "oms_eps")

                for i, name in enumerate(TILES2):
                    lat = name in LAT_ONLY and not uc
                    fm(KS, T if lat else TC, x_lat if lat else x_all, "z_freed")
                    if i == 5:
                        pe.wait_ge(S("ld_c2"), 16 * 2 * (l + 1))
                        pe.wait_ge(S("z_freed"), me.nth("z_freed", 4))
                        for t in range(3):
                            if 4 + t % 2 in held:
                                pe.wait_ge(*held[4 + t % 2])
                            ins = nc.tensor.matmul(bank[4 + t % 2][:, 0:T], c2v("perm"), ZB[:, t, 0:T], start=True, stop=True)
                            ins.then_inc(S("rot_ready"), 1)
                            read_by(4 + t % 2, "rot_freed")
                    if i in (6, 7):
                        gates(2 * i - 12)
                        gates(2 * i - 11)
                    if i == 14:
                        pe.wait_ge(S("rope_done"), me.nth("rope_done", 3))
                        sums(0)
                        keys_queries(0)
                pe.wait_ge(S("z_freed"), me.nth("z_freed", NZ2 - 4))
                if uc:
                    rows(5)
                for h in range(GH):
                    if h < GH - 1:
                        sums(h + 1)
                    other = 6 + (h // 2 + 1) % 2
                    if uc:
                        rows(other)
                    pe.wait_ge(S("dec_ready"), me.nth("dec_ready", 2))
                    if uc and h == 0:
                        columns(5)
                    seqs = 2 if uc else 1
                    for q in range(seqs):
                        if 4 + q in held:
                            pe.wait_ge(*held[4 + q])
                        for d in range(2):
                            for t in range(2):
                                i = 2 * q + t
                                ins = nc.tensor.matmul(bank[4 + q][:, (2 * d + t) * P:(2 * d + t + 1) * P],
                                                       EY[:, d, 512 + i * P:512 + (i + 1) * P], EY[:, d, i * P:(i + 1) * P],
                                                       start=True, stop=True)
                        ins.then_inc(S("a_ready"), 1)
                        read_by(4 + q, "am_read")
                    if 0 in held:
                        pe.wait_ge(*held[0])
                    for q in range(seqs):
                        for d in range(2):
                            i = 2 * q + (1 - d)
                            ins = nc.tensor.matmul(bank[0][:, (2 * q + d) * P:(2 * q + d + 1) * P],
                                                   EY[:, d, 1024 + q * P:1024 + (q + 1) * P], EY[:, d, i * P:(i + 1) * P],
                                                   start=True, stop=True)
                    ins.then_inc(S("ax_ready"), 1)
                    read_by(0, "ax_freed")
                    if 1 in held:
                        pe.wait_ge(*held[1])
                    for t in range(2):
                        ins = nc.tensor.matmul(bank[1][:, t * T:(t + 1) * T], E0[:, T + t * P:T + (t + 1) * P],
                                               E0[:, 0:T], start=True, stop=True)
                    ins.then_inc(S("ax_ready"), 1)
                    read_by(1, "ax_freed")
                    if uc:
                        columns(other)
                    pe.wait_ge(S("ax_freed"), me.nth("ax_freed", 2))
                    if h < GH - 1:
                        keys_queries(h + 1)
                    pe.wait_ge(S("af_ready"), me.nth("af_ready", seqs))
                    b, r, vh = 6 + (h // 2) % 2, half(h), slice(h * GDV, (h + 1) * GDV)
                    if h % 2 == 0:
                        if b in held:
                            pe.wait_ge(*held[b])
                    for t in range(2):
                        nc.tensor.matmul(bank[b][r, 0:T], V2[:, t, vh], AF[:, 0, t, :], start=(t == 0), stop=False)
                    for t in range(2):
                        ins = nc.tensor.matmul(bank[b][r, 0:T], V2[:, 2 + t, vh], A0[:, t, :], start=False, stop=(t == 1))
                    if uc:
                        for t in range(2):
                            ins = nc.tensor.matmul(bank[b][r, T:TC], V2[:, 2 + t, vh], AF[:, 1, t, :],
                                                   start=(t == 0), stop=(t == 1))
                    ins.then_inc(S("gpv_done"), 1)
                    if h % 2 == 1:
                        read_by(b, "og_read")
                    elif h > 0:
                        output_mean()
                output_mean()

                def score2(it, bk):
                    h, qt, nk, own = it
                    o = T if own else 0
                    return nc.tensor.matmul(bk[:, 0:nk], ZB[half(h), Z2["nq"] + h // 2, o + qt * P:o + (qt + 1) * P],
                                            ZB[half(h), Z2["nk"] + h // 2, o:TC], start=True, stop=True)

                def pv2(j, it, bk):
                    h, qt, nk, own = it
                    o, k0 = (T, 2) if own else (0, 0)
                    for kt in range(nk // P):
                        ins = nc.tensor.matmul(bk[half(h), o + qt * P:o + (qt + 1) * P],
                                               V2[:, k0 + kt, VW + h * 64:VW + (h + 1) * 64],
                                               PT2[:, j % 2, kt * P:(kt + 1) * P], start=(kt == 0), stop=(kt == nk // P - 1))
                    return ins

                attention(items2(uc), score2, P2, pv2, uc)
                pe.wait_ge(S("y_split"), me.nth("y_split", 5))
                for m in range(KS):
                    fm(KS, n, rhs, "wo_freed", "y_split" if m == 0 else None, 5)
                    stats_behind(m, n, SQ2)
                if uc:
                    rows(5)
                    rows(6)
                    columns(5)
                for m in range(2 * FT):
                    fm(KS, n, rhs, "up_freed", "x_split" if m == 0 else None)
                    if uc and m == 1:
                        columns(6)
                for m in range(KS):
                    fm(FT, n, lambda s: (HHI[:, s, 0:n], HLO[:, s, 0:n]), "wo_freed", "hid_split" if m == 0 else None)
                    stats_behind(m, n, SQF)

        @block.scalar
        def _(act):
            me = Side(act, "act")
            split = 0

            def A(out, in_, func=ACT.Copy, **kw):
                return nc.scalar.activation(out, in_, func, **kw)

            def split_to(n):
                nonlocal split
                while split < min(n, NU):
                    u, k = split, SPLIT_NO[split]
                    split += 1
                    if PLAIN[u]:
                        continue
                    act.wait_ge(S(f"raw{u % RAW}"), 16 * (u // RAW + 1))
                    if k >= SPL:
                        act.wait_ge(S("unit_done"), SPLIT_UNITS[k - SPL] + 1)
                    w = WIDTHS[u]
                    A(WHI[:, k % SPL, 0:w], RAWB[:, u % RAW, 0:w]).then_inc(S("hi_ready"), 1)

            def rest(n=1):
                for _ in range(n):
                    me.u += 1
                    split_to(me.u + AHEAD)

            def plain(n):
                me.u += n

            def ahead():
                split_to(me.u + AHEAD)

            def unit(n=1):
                rest(n)
                act.wait_ge(S("unit_done"), me.u)

            def shift_hi(l, n, shift):
                for s in range(KS):
                    act.wait_ge(S("t_ready"), me.nth("t_ready"))
                    for c in range(n // T):
                        w = slice(c * T, (c + 1) * T)
                        ins = A(NHI[:, s, w], TB2[:, s, w], ACT.Identity, bias=MOD[:, l, shift + s, c:c + 1])
                    ins.then_inc(S("xh_ready"), 1)

            def copy_rows(b, u):
                act.wait_ge(S("unit_done"), u)
                if made_rows[0] > 0:
                    act.wait_ge(S("cols_ready"), me.nth("cols_ready"))
                made_rows[0] += 1
                A(ROWS[:], bank[b][0:2, :]).then_inc(S("rows_copied"), 1)

            made_rows = [0]

            def guess(m, g, given):
                act.wait_ge(S(given), me.nth(given))
                A(g, m, ACT.Abs_reciprocal_sqrt).then_inc(S("rs_guess"), 1)

            def squares(n, sq, s, k):
                if s == KS - 2:
                    norms[0] += 1
                A(sq[:, k:k + 2, 0:n], X[:, s:s + 2, 0:n], ACT.Square).then_inc(S("sq_ready"), 1)

            norms = [0]

            def stats(n, sq):
                for s in range(0, KS, 2):
                    squares(n, sq, s, s)

            def residual(n, units, sq):
                ring = sq.shape[1]
                for m in range(KS + 2):
                    if m < KS:
                        rest(units)
                    if m >= 3 and m % 2 == 1:
                        act.wait_ge(S("wo_freed"), me.nth("wo_freed", 2))
                        if m - 3 >= ring:
                            act.wait_ge(S("sq_used"), 3 * norms[0] + (m - 5) // 2)
                        squares(n, sq, m - 3, (m - 3) % ring)
                me.tile += KS

            def split_hi(n, src, o, given, slabs=range(KS)):
                for s in slabs:
                    act.wait_ge(S(given), me.nth(given))
                    A(NHI[:, s, o:o + n], src[:, s, 0:n]).then_inc(S("xh_ready"), 1)

            def softmax(items, lbuf, pbuf, ptbuf, stb, scale, done, between=None):
                n = len(items)
                for i in range(n + 2):
                    if i < n:
                        k, nk = i % 3, items[i][2]
                        act.wait_ge(S("l_ready"), me.nth("l_ready"))
                        A(pbuf[:, k, 0:nk], lbuf[:, k, 0:nk], ACT.Exp, bias=stb[:, k, 1:2], scale=scale,
                          accum_out=stb[:, k, 2:3]).then_inc(S("e_ready"), 1)
                    if between is not None:
                        between(i)
                    if i >= 2:
                        j = i - 2
                        act.wait_ge(S("pt_ready"), me.nth("pt_ready"))
                        if j >= 2:
                            act.wait_ge(S("pv_done"), me.nth("pv_done"))
                            done(items[j - 2])
                        A(ptbuf[:, j % 2, 0:items[j][2]], bank[2 + j % 2][:, 0:items[j][2]]).then_inc(S("pt_freed"), 1)
                for j in (n - 2, n - 1):
                    act.wait_ge(S("pv_done"), me.nth("pv_done"))
                    done(items[j])

            act.dma_start(PRM[:], prm).then_inc(S("ld_prm"), 16)
            act.dma_start(X[:, :, 0:T], xt[:, :, 0:T]).then_inc(S("ld_x"), 16)
            act.wait_ge(S("ld_prm"), 16)
            A(CV2[:], prm_col("cvec", 0, 2 * KS).rearrange("p (s c) -> p s c", c=2), ACT.Silu).then_inc(S("c_ready"), 1)

            act.wait_ge(S("ld_x"), 16)
            for l in range(DEPTH):
                if l == 0:
                    stats(T, Y1)
                guess(MS1[:, 0, :], MS1[:, 2, :], "ms_eps")
                plain(2 * ROW_U)
                first_u = me.u
                copy_rows(5, first_u - ROW_U)
                ahead()
                split_hi(T, Y1, 0, "t_ready")
                copy_rows(6, first_u)
                rest(4)
                for t in range(NZ1):
                    unit()
                    A(Z[:, t, :], bank[me.next_tile()][:, 0:T], ACT.Identity, bias=prm_col(f"bin{l}", t)).then_inc(S("z_freed"), 1)
                    if t == 4:
                        act.wait_ge(S("z_freed"), me.nth("z_freed", 5))
                        A(SG[:], Z[:, Z1["glu"]:Z1["glu"] + 2, :], ACT.Sigmoid).then_inc(S("glu_ready"), 1)
                    if t == 16:
                        for qt in range(TT):
                            act.wait_ge(S("wi_ready"), me.nth("wi_ready"))
                            A(WI[:, qt, :], bank[6 + qt][:, 0:IDXH]).then_inc(S("wi_freed"), 1)
                    if 17 <= t < 21:
                        for i in (2 * (t - 17), 2 * (t - 17) + 1):
                            nk = P * (i // IDXH + 1)
                            act.wait_ge(S("idx_ready"), me.nth("idx_ready"))
                            if i >= 2:
                                act.wait_ge(S("rl_used"), me.nth("rl_used"))
                            A(RL[:, i % 2, 0:nk], bank[6 + i % 2][:, 0:nk], ACT.Relu, scale=HD ** -0.5).then_inc(S("idx_freed"), 1)
                    if t == 22:
                        act.wait_ge(S("rl_used"), me.nth("rl_used", 2))
                    if t == 24:
                        act.wait_ge(S("z_freed"), me.nth("z_freed", 20))
                        A(GT1[:, 0:2, :], Z[:, Z1["cgate"]:Z1["cgate"] + 2, :], ACT.Silu)
                        A(GT1[:, 2:4, :], Z[:, Z1["pgate"]:Z1["pgate"] + 2, :], ACT.Silu)
                        A(GT1[:, 4:6, :], Z[:, Z1["agate"]:Z1["agate"] + 2, :], ACT.Silu)
                act.wait_ge(S("z_freed"), me.nth("z_freed", NZ1 - 25))
                A(GT1[:, 6:8, :], Z[:, Z1["agate"] + 2:Z1["agate"] + 4, :], ACT.Silu).then_inc(S("silu_ready"), 1)

                def done1(it):
                    if ends_pair(it):
                        A(OB[:, it[0] // 2, :], bank[6 + (it[0] // 2) % 2][:, 0:T]).then_inc(S("o_freed"), 1)

                def beside(i):
                    if i == 9:
                        copy_rows(5, me.u + ROW_U)
                    if i == 13:
                        act.wait_ge(S("xc_ready"), me.nth("xc_ready"))
                        A(CT[:], CV[:], ACT.Square).then_inc(S("conv_sq"), 1)

                softmax(ITEMS1, L1, P1, PT1, ST1, HD ** -0.5, done1, beside)
                guess(MS1[:, 0, :], MS1[:, 2, :], "cvar_eps")
                for m in range(2):
                    act.wait_ge(S("pw_ready"), me.nth("pw_ready"))
                    A(Y1[:, 2 + m, :], bank[2 + m][:, 0:T], ACT.Identity, bias=PB[:, m:m + 1],
                      scale=prm_col(f"pools{l}", m)).then_inc(S("pw_freed"), 1)
                act.wait_ge(S("cn_ready"), me.nth("cn_ready"))
                for k in range(2):
                    ins = A(CV[:, k, :], CV[:, k, :], ACT.Silu, bias=prm_col(f"lnb{l}", k), scale=prm_col(f"lng{l}", k))
                ins.then_inc(S("conv_silu"), 1)
                plain(3 * ROW_U)
                copy_rows(4, me.u - ROW_U)
                split_hi(T, Y1, 0, "y_ready", range(2, KS))
                for m in range(2):
                    act.wait_ge(S("pw_ready"), me.nth("pw_ready"))
                    A(Y1[:, m, :], bank[m][:, 0:T], ACT.Identity, bias=prm_col(f"pwb{l}", m)).then_inc(S("pw_freed"), 1)
                ahead()
                split_hi(T, Y1, 0, "y_ready", range(2))
                copy_rows(5, me.u)
                act.wait_ge(S("ld_p1"), 16 * 3 * (l + 1))
                A(PLEH[:, 0, :, :], PIN[:]).then_inc(S("ple_hi"), 1)
                rest(KS)
                me.tile += KS
                split_hi(T, X, T, "wo_freed")
                for u in range(2):
                    for j in range(4):
                        if j == 3:
                            unit()
                        else:
                            act.wait_ge(S("ple_ready"), me.nth("ple_ready"))
                        A(Y1[:, 4 * u + j, :], bank[me.next_tile()][:, 0:T]).then_inc(S("ple_freed"), 1)
                plain(ROW_U)
                copy_rows(5, me.u)
                ahead()
                for m in range(KS + 2):
                    if m < KS:
                        unit()
                    if m >= 2:
                        act.wait_ge(S("x_new"), me.nth("x_new"))
                    if m < KS:
                        A(SG[:, m % 2, :], bank[me.next_tile()][:, 0:T], ACT.Sigmoid).then_inc(S("gate_freed"), 1)
                    if m >= 3 and m % 2 == 1:
                        squares(T, Y1, m - 3, m - 3)
            guess(MS1[:, 0, :], MS1[:, 2, :], "ms_eps")
            plain(ROW_U)
            copy_rows(5, me.u)
            act.wait_ge(S("x_new"), me.nth("x_new", KS))

            act.wait_ge(S("x_split"), me.nth("x_split", KS * DEPTH))
            act.wait_ge(S("y_split"), me.nth("y_split", KS * DEPTH))
            act.wait_ge(S("pw_freed"), me.nth("pw_freed", 4 * DEPTH))
            for l in range(DEPTH):
                uc = l < DEPTH - 1
                n = TC if uc else T
                if l == 0:
                    act.wait_ge(S("ld_ctx"), 16)
                if l == 0:
                    stats(TC, SQ2)
                guess(MS2[:, 0, :], MS2[:, 2, :], "ms_eps")
                if uc:
                    plain(2 * ROW_U)
                    first_u = me.u
                    copy_rows(6, first_u - ROW_U)
                ahead()
                shift_hi(l, TC, SH1)
                if uc:
                    copy_rows(7, first_u)
                act.wait_ge(S("x_split"), me.nth("x_split", KS))
                for v in range(2):
                    unit(4)
                    for t in range(4):
                        A(V2[:, t, v * VW:(v + 1) * VW], bank[t][:, 0:VW]).then_inc(S("v_freed"), 1)

                def gate_abs(i):
                    act.wait_ge(S("gate_ready"), me.nth("gate_ready"))
                    A(gate_part(GTA, i), bank[(6, 7, 4, 5)[i]][:, 0:VW].rearrange("p (t k) -> p t k", t=2),
                      ACT.Abs).then_inc(S("act_chain"), 1)

                def copy_sums(h):
                    for d in range(2):
                        act.wait_ge(S("b_ready"), me.nth("b_ready"))
                        A(BC[:, d, :], bank[(6 if h == 0 else 2) + d][:]).then_inc(S("b_copied"), 1)

                def copy_keys(h):
                    for w in range(2):
                        act.wait_ge(S("kq_ready"), me.nth("kq_ready"))
                        A(KQ[:, w, :], bank[(4 if h == 0 else 0) + w][:], scale=1.0 if w == 0 else GDK ** -0.5).then_inc(S("kq_freed"), 1)

                def output_hi(k):
                    act.wait_ge(S("yo_ready"), me.nth("yo_ready"))
                    A(NHI[:, k, 0:n], ZB[:, Z2["r"] + k, 0:n]).then_inc(S("xh_ready"), 1)

                for i, name in enumerate(TILES2):
                    unit()
                    w = T if name in LAT_ONLY and not uc else TC
                    z, g = ZB[:, i, 0:w], bank[me.next_tile()][:, 0:w]
                    if name == "glr":
                        ins = A(z, g, ACT.Identity, bias=cst("glrone"))
                    elif name == "nq":
                        ins = A(z, g, scale=64 ** -0.5)
                    else:
                        ins = A(z, g)
                    ins.then_inc(S("z_freed"), 1)
                    if i in (8, 9):
                        gate_abs(2 * i - 16)
                        gate_abs(2 * i - 15)
                    if i == 10:
                        act.wait_ge(S("act_chain"), me.nth("act_chain", 4))
                        for k in range(4):
                            A(gate_part(GTA, k), gate_part(GTA, k), ACT.Exp, scale=-1.0).then_inc(S("act_chain"), 1)
                    if i == 11:
                        act.wait_ge(S("act_chain"), me.nth("act_chain", 4))
                        for k in range(4):
                            A(gate_part(GTA, k), gate_part(GTA, k), ACT.Ln, bias=1.0).then_inc(S("gln_ready"), 1)
                    if i == 14:
                        act.wait_ge(S("z_freed"), me.nth("z_freed", 14))
                        A(ZB[:, Z2["r"]:Z2["r"] + 3, 0:n], ZB[:, Z2["r"]:Z2["r"] + 3, 0:n], ACT.Silu).then_inc(S("rsilu_ready"), 1)
                    if i == 15:
                        copy_sums(0)
                        copy_keys(0)
                act.wait_ge(S("z_freed"), me.nth("z_freed", NZ2 - 14))
                for h in range(GH):
                    if h % 2 == 0 and h > 0:
                        act.wait_ge(S("gpv_done"), me.nth("gpv_done"))
                        A(OM[:, 0, 0:n], bank[6 + (h // 2 - 1) % 2][:, 0:n], ACT.Square).then_inc(S("osq_ready"), 1)
                    for d in range(2):
                        act.wait_ge(S("bm_ready"), me.nth("bm_ready"))
                        r = slice(32 * d, 32 * d + 32)
                        A(E0[r, 0:T], BC[r, d, 0:T], ACT.Exp)
                        A(E0[r, T:TC], BC[r, d, T:TC], ACT.Exp, scale=-1.0, bias=BM[r, d, 4:5]).then_inc(S("e0_ready"), 1)
                        act.wait_ge(S("e0_ready"), me.nth("e0_ready"))
                        act.wait_ge(S("ex_ready"), me.nth("ex_ready"))
                        A(EY[:, d, :], exps(d), ACT.Exp).then_inc(S("ey_ready"), 1)
                    if uc and h == 0:
                        plain(ROW_U)
                        copy_rows(5, me.u)
                    if h < GH - 1:
                        copy_sums(h + 1)
                    if h % 2 == 1 and h > 1:
                        guess(OM[:, 1, 0:n], OM[:, 2, 0:n], "oms_eps")
                    if uc:
                        plain(ROW_U)
                        copy_rows(6 + (h // 2 + 1) % 2, me.u)
                    if h % 2 == 1:
                        act.wait_ge(S("gpv_done"), me.nth("gpv_done"))
                    act.wait_ge(S("ax_ready"), me.nth("ax_ready"))
                    for q in range(2 if uc else 1):
                        ins = A(AF[:, q, :, :].rearrange("p a t -> p (a t)")[:, P:3 * P], bank[0][:, 2 * q * P:(2 * q + 2) * P])
                    ins.then_inc(S("ax_freed"), 1)
                    act.wait_ge(S("ax_ready"), me.nth("ax_ready"))
                    A(A0[:].rearrange("p a t -> p (a t)"), bank[1][:]).then_inc(S("ax_freed"), 1)
                    act.wait_ge(S("dec_ready"), me.nth("dec_ready", 2))
                    if h < GH - 1:
                        copy_keys(h + 1)
                    if h % 2 == 0 and h > 2:
                        output_hi(h // 2 - 2)
                act.wait_ge(S("gpv_done"), me.nth("gpv_done"))
                A(OM[:, 0, 0:n], bank[6 + (GH // 2 - 1) % 2][:, 0:n], ACT.Square).then_inc(S("osq_ready"), 1)

                output_hi(GH // 2 - 2)

                def end_of_gated(i):
                    if i == 2:
                        guess(OM[:, 1, 0:n], OM[:, 2, 0:n], "oms_eps")
                        act.wait_ge(S("sc_ready"), me.nth("sc_ready", 2))
                        for k in range(2):
                            A(NHI[:, 3 + k, 0:n], ZB[:, Z2["scx"] + k, 0:n]).then_inc(S("xh_ready"), 1)
                    if i == 5:
                        output_hi(GH // 2 - 1)

                def done2(it):
                    if ends_pair(it, uc):
                        k = it[0] // 2
                        A(OY[:, k, 0:n], bank[6 + k % 2][:, 0:n]).then_inc(S("o_freed"), 1)
                        act.wait_ge(S("o_freed"), me.nth("o_freed"))
                        A(NHI[:, 5 + k, 0:n], OY[:, k, 0:n]).then_inc(S("xh_ready"), 1)

                if l == 0:
                    act.wait_ge(S("o_freed"), me.nth("o_freed", 4 * DEPTH))
                softmax(items2(uc), L2, P2, PT2, ST2, 1.0, done2, end_of_gated)
                ahead()
                act.wait_ge(S("y_split"), me.nth("y_split", KS))
                residual(n, 1, SQ2)
                guess(MS2[:, 0, 0:n], MS2[:, 2, 0:n], "ms_eps")
                if uc:
                    plain(2 * ROW_U)
                    first_u = me.u
                    copy_rows(5, first_u - ROW_U)
                ahead()
                shift_hi(l, n, SH2)
                if uc:
                    copy_rows(6, first_u)
                act.wait_ge(S("x_split"), me.nth("x_split", KS))
                for p in range(FT + 2):
                    if p < FT:
                        for w in range(2):
                            unit()
                            j = w * FT + p
                            if w == 0 and p >= 3:
                                act.wait_ge(S("hid_split"), me.nth("hid_split"))
                            A(CF[:, w, p % 3, 0:n], bank[me.next_tile()][:, 0:n], ACT.Identity,
                              bias=prm_col(f"fb{l}", j), scale=prm_col(f"fw{l}", 2 * FT + j)).then_inc(S("centre_ready"), 1)
                    if 1 <= p < FT + 1:
                        act.wait_ge(S("up_freed"), me.nth("up_freed", 2))
                        A(CF[:, 0, (p - 1) % 3, 0:n], CF[:, 0, (p - 1) % 3, 0:n], ACT.Silu).then_inc(S("fsilu_ready"), 1)
                    if p >= 2:
                        act.wait_ge(S("hid_ready"), me.nth("hid_ready"))
                        A(HHI[:, p - 2, 0:n], CF[:, 1, (p - 2) % 3, 0:n]).then_inc(S("hh_ready"), 1)
                act.wait_ge(S("hid_split"), me.nth("hid_split", 3))
                residual(n, 3, SQF)
            guess(MS2[:, 0, 0:T], MS2[:, 2, 0:T], "ms_eps")

        @block.vector
        def _(dve):
            me = Side(dve, "dve")
            V = nc.vector
            split = 0

            def split_to(n):
                nonlocal split
                while split < min(n, NU):
                    u, k = split, SPLIT_NO[split]
                    split += 1
                    if PLAIN[u]:
                        continue
                    dve.wait_ge(S("hi_ready"), k + 1)
                    w = WIDTHS[u]
                    V.tensor_tensor(WLO[:, k % SPL, 0:w], RAWB[:, u % RAW, 0:w], WHI[:, k % SPL, 0:w].bitcast(F32),
                                    ALU.subtract).then_inc(S("lo_ready"), 1)

            def rest(n=1):
                for _ in range(n):
                    me.u += 1
                    split_to(me.u + AHEAD)

            def plain(n):
                me.u += n

            def ahead():
                split_to(me.u + AHEAD)

            def unit(n=1):
                rest(n)
                dve.wait_ge(S("unit_done"), me.u)

            def rsqrt(m, g, t, out):
                dve.wait_ge(S("rs_guess"), me.nth("rs_guess"))
                for o in (g, out):
                    V.scalar_tensor_tensor(t, m, -0.5, g, ALU.mult, ALU.mult).then_inc(S("dve_chain"), 1)
                    dve.wait_ge(S("dve_chain"), me.nth("dve_chain"))
                    V.tensor_tensor(t, t, g, ALU.mult).then_inc(S("dve_chain"), 1)
                    dve.wait_ge(S("dve_chain"), me.nth("dve_chain"))
                    V.scalar_tensor_tensor(o, t, 1.5, g, ALU.add, ALU.mult).then_inc(S("dve_chain"), 1)
                    dve.wait_ge(S("dve_chain"), me.nth("dve_chain"))

            def stats(n, ms):
                dve.wait_ge(S("ms_ready"), me.nth("ms_ready"))
                V.tensor_scalar(ms[:, 0, 0:n], bank[4][:, 0:n], EPS, None, ALU.add).then_inc(S("ms_eps"), 1)
                rsqrt(ms[:, 0, 0:n], ms[:, 2, 0:n], ms[:, 1, 0:n], ms[:, 3, 0:n])

            def split_lo(n, src, o, done, slabs=range(KS)):
                for s in slabs:
                    dve.wait_ge(S("xh_ready"), me.nth("xh_ready"))
                    V.tensor_tensor(NLO[:, s, o:o + n], src[:, s, 0:n], NHI[:, s, o:o + n].bitcast(F32), ALU.subtract).then_inc(S(done), 1)

            def modulation(b):
                l, first = taken[0] // ROW_TILES, 4 * (taken[0] % ROW_TILES)
                taken[0] += 1
                dve.wait_ge(S("cols_ready"), me.nth("cols_ready"))
                V.tensor_tensor(MOD[:, l, first:first + 4, :], bank[b][:, 0:8].rearrange("p (j c) -> p j c", c=2),
                                bl(prm_col(f"bada{l}", first, 4), 2), ALU.add).then_inc(S("mod_done"), 1)

            taken = [0]

            def softmax(items, bias, lbuf, pbuf, stb, scale, between=None):
                n = len(items)
                for i in range(n + 1):
                    if i < n:
                        k, nk = i % 3, items[i][2]
                        b = bias(items[i])
                        dve.wait_ge(S("s_ready"), me.nth("s_ready"))
                        if b is None:
                            V.tensor_copy(lbuf[:, k, 0:nk], bank[i % 2][:, 0:nk])
                            V.reduce_max(stb[:, k, 0:1], bank[i % 2][:, 0:nk], AX_X).then_inc(S("s_freed"), 1)
                        else:
                            V.tensor_tensor_reduce(out=lbuf[:, k, 0:nk], in0=bank[i % 2][:, 0:nk], in1=b, scale=1.0,
                                                   scalar=-3.0e38, op0=ALU.add, op1=ALU.max,
                                                   accum_out=stb[:, k, 0:1]).then_inc(S("s_freed"), 1)
                        dve.wait_ge(S("s_freed"), me.nth("s_freed"))
                        V.tensor_scalar(stb[:, k, 1:2], stb[:, k, 0:1], -scale, None, ALU.mult).then_inc(S("l_ready"), 1)
                        if between is not None:
                            between(i)
                    if i >= 1:
                        k, nk = (i - 1) % 3, items[i - 1][2]
                        dve.wait_ge(S("e_ready"), me.nth("e_ready"))
                        V.reciprocal(stb[:, k, 3:4], stb[:, k, 2:3]).then_inc(S("dve_chain"), 1)
                        dve.wait_ge(S("dve_chain"), me.nth("dve_chain"))
                        V.tensor_scalar(pbuf[:, k, 0:nk], pbuf[:, k, 0:nk], stb[:, k, 3:4], None, ALU.mult).then_inc(S("p_ready"), 1)

            dve.wait_ge(S("ld_prm"), 16)

            dve.wait_ge(S("ld_x"), 16)
            V.memset(UP[:, :, 0:CONV_K - 1], 0.0).then_inc(S("dve_chain"), 1)
            dve.wait_ge(S("dve_chain"), me.nth("dve_chain"))
            dve.wait_ge(S("ld_c1"), 16)
            for l in range(DEPTH):
                dve.wait_ge(S("ld_p1"), 16 * 3 * (l + 1))
                stats(T, MS1)
                for s in range(KS):
                    V.scalar_tensor_tensor(Y1[:, s, :], X[:, s, 0:T], prm_col(f"norm{l}", s), MS1[:, 3, :],
                                           ALU.mult, ALU.mult).then_inc(S("t_ready"), 1)
                plain(2 * ROW_U)
                ahead()
                split_lo(T, Y1, 0, "x_split")
                modulation(5)
                unit(4)
                for t in range(TT):
                    V.tensor_tensor(V1[:, t, :], bank[t][:], BV[:], ALU.add).then_inc(S("v_freed"), 1)
                modulation(6)

                def rope(g, done):
                    k = 2 if g < 5 else 1
                    z = Z[:, Z1["q"] + 2 * g:Z1["q"] + 2 * g + k, :]
                    rt = RT[:, 0:k * T].rearrange("p (a t) -> p a t", a=k)
                    dve.wait_ge(S("rot_ready"), me.nth("rot_ready"))
                    V.tensor_tensor(rt, bank[4 + g % 2][:, 0:k * T].rearrange("p (a t) -> p a t", a=k),
                                    bc(c1v("sin"), k), ALU.mult).then_inc(S("rot_freed"), 1)
                    V.tensor_tensor(z, z, bc(c1v("cos"), k), ALU.mult).then_inc(S("dve_chain"), 1)
                    dve.wait_ge(S("rot_freed"), me.nth("rot_freed"))
                    dve.wait_ge(S("dve_chain"), me.nth("dve_chain"))
                    V.tensor_tensor(z, z, rt, ALU.add).then_inc(S(done), 1)
                    dve.wait_ge(S(done), me.nth(done))

                def index(i):
                    qt, h = i // IDXH, i % IDXH
                    nk = P * (qt + 1)
                    dve.wait_ge(S("idx_freed"), me.nth("idx_freed"))
                    if h == 0:
                        ins = V.tensor_scalar(SC[:, qt, 0:nk], RL[:, i % 2, 0:nk], WI[:, qt, h:h + 1], None, ALU.mult)
                    else:
                        ins = V.scalar_tensor_tensor(SC[:, qt, 0:nk], RL[:, i % 2, 0:nk], WI[:, qt, h:h + 1],
                                                     SC[:, qt, 0:nk], ALU.mult, ALU.add)
                    ins.then_inc(S("rl_used"), 1)
                    dve.wait_ge(S("rl_used"), me.nth("rl_used"))

                def topk(qt, r0, r1):
                    nk = P * (qt + 1)
                    sc, causal = SC[:, qt, 0:nk], c1v("causal")[:, qt * T:qt * T + nk]
                    if r0 == 0:
                        V.tensor_tensor(sc, sc, causal, ALU.add).then_inc(S("dve_chain"), 1)
                        dve.wait_ge(S("dve_chain"), me.nth("dve_chain"))
                    for _ in range(r0, r1):
                        V.max(M8[:], sc).then_inc(S("dve_chain"), 1)
                        dve.wait_ge(S("dve_chain"), me.nth("dve_chain"))
                        V.match_replace(out=sc, in_to_replace=M8[:], in_values=sc, imm_value=-3.0e38).then_inc(S("dve_chain"), 1)
                        dve.wait_ge(S("dve_chain"), me.nth("dve_chain"))
                    if r1 == TOPK // 8:
                        V.tensor_scalar(MB[:, qt, 0:nk], sc, -2.0e38, -1.0e30, ALU.is_gt, ALU.mult).then_inc(S("dve_chain"), 1)
                        dve.wait_ge(S("dve_chain"), me.nth("dve_chain"))
                        V.tensor_tensor(MB[:, qt, 0:nk], MB[:, qt, 0:nk], causal, ALU.add).then_inc(S("dve_chain"), 1)
                        dve.wait_ge(S("dve_chain"), me.nth("dve_chain"))

                def taps(k0, k1):
                    for k in range(k0, k1):
                        for m in range(2):
                            w, src = prm_col(f"dww{l}", m * CONV_K + k), UP[:, m, k:k + T]
                            if k == 0:
                                ins = V.tensor_scalar(CV[:, m, :], src, w, prm_col(f"dwb{l}", m), ALU.mult, ALU.add)
                            else:
                                ins = V.scalar_tensor_tensor(CV[:, m, :], src, w, CV[:, m, :], ALU.mult, ALU.add)
                        if k < CONV_K - 1:
                            ins.then_inc(S("dve_chain"), 1)
                            dve.wait_ge(S("dve_chain"), me.nth("dve_chain"))
                        else:
                            ins.then_inc(S("conv_ready"), 1)
                            dve.wait_ge(S("conv_ready"), me.nth("conv_ready"))

                for t in range(NZ1):
                    rest()
                    if t == 5:
                        dve.wait_ge(S("glu_ready"), me.nth("glu_ready"))
                        dve.wait_ge(S("z_freed"), me.nth("z_freed", 4))
                        V.tensor_tensor(UP[:, :, CONV_K - 1:], Z[:, Z1["val"]:Z1["val"] + 2, :], SG[:], ALU.mult).then_inc(S("dve_chain"), 1)
                        dve.wait_ge(S("dve_chain"), me.nth("dve_chain"))
                    if t in TAPS_AT:
                        taps(*TAPS_AT[t])
                    if t - 1 in ROPE_AT:
                        dve.wait_ge(S("z_freed"), me.nth("z_freed", 4 if t - 1 == 7 else 2))
                        rope(ROPE_AT[t - 1], "rope_done" if ROPE_AT[t - 1] == 3 else "dve_chain")
                    if t == 16:
                        dve.wait_ge(S("z_freed"), me.nth("z_freed", 4))
                        rope(4, "dve_chain")
                        rope(5, "qi_roped")
                    if t == 17:
                        dve.wait_ge(S("wi_freed"), me.nth("wi_freed", TT))
                    if 17 <= t < 21:
                        index(2 * (t - 17))
                        index(2 * (t - 17) + 1)
                    if t == 19:
                        topk(0, 0, 4)
                    if t == 20:
                        topk(0, 4, 8)
                    if t == 21:
                        topk(1, 0, 3)
                    if t == 22:
                        topk(1, 3, 6)
                    if t == 23:
                        topk(1, 6, 8)
                    if t == 24:
                        dve.wait_ge(S("z_freed"), me.nth("z_freed", 4))
                me.tile += NZ1
                plain(3 * ROW_U)
                def beside(i):
                    if i < 7:
                        taps(min(CONV_K, TAPS_LEFT + 2 * i), min(CONV_K, TAPS_LEFT + 2 * i + 2))
                    if i == 11:
                        modulation(5)
                    if i == 13:
                        dve.wait_ge(S("cstat_ready"), me.nth("cstat_ready"))
                        V.tensor_tensor(CV[:], CV[:], bc(bank[5][:, 0:T], 2), ALU.subtract).then_inc(S("xc_ready"), 1)
                        dve.wait_ge(S("xc_ready"), me.nth("xc_ready"))
                    if i == 15:
                        dve.wait_ge(S("cstat_ready"), me.nth("cstat_ready"))
                        V.tensor_scalar(MS1[:, 0, :], bank[5][:, 0:T], EPS, None, ALU.add).then_inc(S("cvar_eps"), 1)

                softmax(ITEMS1, lambda it: MB[:, it[1], 0:it[2]], L1, P1, ST1, HD ** -0.5, beside)
                rsqrt(MS1[:, 0, :], MS1[:, 2, :], MS1[:, 1, :], MS1[:, 3, :])
                V.tensor_tensor(CV[:], CV[:], bc(MS1[:, 3, :], 2), ALU.mult).then_inc(S("cn_ready"), 1)
                dve.wait_ge(S("silu_ready"), me.nth("silu_ready"))
                dve.wait_ge(S("o_freed"), me.nth("o_freed", 4))
                dve.wait_ge(S("pw_freed"), me.nth("pw_freed", 2))
                for m in range(2, KS):
                    V.tensor_tensor(Y1[:, m, :], Y1[:, m, :] if m < 4 else OB[:, m - 4, :], GT1[:, m, :], ALU.mult).then_inc(S("y_ready"), 1)
                split_lo(T, Y1, 0, "y_split", range(2, KS))
                for m in range(2):
                    dve.wait_ge(S("pw_freed"), me.nth("pw_freed"))
                    V.tensor_tensor(Y1[:, m, :], Y1[:, m, :], GT1[:, m, :], ALU.mult).then_inc(S("y_ready"), 1)
                ahead()
                split_lo(T, Y1, 0, "y_split", range(2))
                modulation(4)
                dve.wait_ge(S("ple_hi"), me.nth("ple_hi"))
                V.tensor_tensor(PLEH[:, 1, :, :], PIN[:], PLEH[:, 0, :, :].bitcast(F32), ALU.subtract).then_inc(S("ple_split"), 1)
                for m in range(KS):
                    unit()
                    V.tensor_tensor(X[:, m, 0:T], X[:, m, 0:T], bank[me.next_tile()][:, 0:T], ALU.add).then_inc(S("wo_freed"), 1)
                    if m == 1:
                        modulation(5)
                split_lo(T, X, T, "h_split")
                rest(2)
                dve.wait_ge(S("ple_freed"), me.nth("ple_freed", KS))
                me.tile += 2 * KS
                plain(ROW_U)
                ahead()
                for m in range(KS):
                    rest()
                    dve.wait_ge(S("gate_freed"), me.nth("gate_freed"))
                    V.tensor_tensor(Y1[:, m, :], Y1[:, m, :], SG[:, m % 2, :], ALU.mult).then_inc(S("dve_chain"), 1)
                    dve.wait_ge(S("dve_chain"), me.nth("dve_chain"))
                    V.tensor_tensor(X[:, m, 0:T], X[:, m, 0:T], Y1[:, m, :], ALU.add).then_inc(S("x_new"), 1)
                    if m == 0:
                        modulation(5)
            stats(T, MS1)
            for s in range(KS):
                V.scalar_tensor_tensor(X[:, s, 0:T], X[:, s, 0:T], prm_col("fin1", s), MS1[:, 3, :],
                                       ALU.mult, ALU.mult).then_inc(S("x_new"), 1)

            plain(ROW_U)

            def modulate(l, n, gain, shift, scale):
                V.scalar_tensor_tensor(GM[:], MOD[:, l, scale:scale + KS, :], 1.0, bl(prm_col(gain, 0, KS), 2),
                                       ALU.add, ALU.mult).then_inc(S("dve_chain"), 1)
                dve.wait_ge(S("dve_chain"), me.nth("dve_chain"))
                ahead()
                for s in range(KS + 1):
                    for c in range(n // T):
                        w = slice(c * T, (c + 1) * T)
                        if s < KS:
                            ins = V.scalar_tensor_tensor(TB2[:, s, w], X[:, s, w], GM[:, s, c:c + 1], MS2[:, 3, w], ALU.mult, ALU.mult)
                    if s < KS:
                        ins.then_inc(S("t_ready"), 1)
                    if s >= 1:
                        dve.wait_ge(S("xh_ready"), me.nth("xh_ready"))
                        dve.wait_ge(S("t_ready"), me.nth("t_ready"))
                        for c in range(n // T):
                            w = slice(c * T, (c + 1) * T)
                            ins = V.scalar_tensor_tensor(NLO[:, s - 1, w], TB2[:, s - 1, w], MOD[:, l, shift + s - 1, c:c + 1],
                                                         NHI[:, s - 1, w].bitcast(F32), ALU.add, ALU.subtract)
                        ins.then_inc(S("x_split"), 1)

            def residual(l, n, gate, units):
                for m in range(KS):
                    unit(units)
                    b = bank[me.next_tile()]
                    for c in range(n // T):
                        w = slice(c * T, (c + 1) * T)
                        ins = V.scalar_tensor_tensor(X[:, m, w], b[:, w], MOD[:, l, gate + m, c:c + 1], X[:, m, w],
                                                     ALU.mult, ALU.add)
                    ins.then_inc(S("wo_freed"), 1)

            def seq(ap, n):
                return ap.rearrange("p (s t) -> p s t", t=T)

            dve.wait_ge(S("x_new"), me.nth("x_new", KS * (DEPTH + 1)))
            for l in range(DEPTH):
                uc = l < DEPTH - 1
                n = TC if uc else T
                if uc:
                    plain(2 * ROW_U)
                    modulation(5)
                stats(TC, MS2)
                modulate(l, TC, f"nmix{l}", SH1, SC1)
                if uc:
                    modulation(6)
                rest(4)
                if uc:
                    modulation(7)
                rest(4)

                def rope(t):
                    z = ZB[:, t, 0:T]
                    dve.wait_ge(S("rot_ready"), me.nth("rot_ready"))
                    V.tensor_tensor(AM[:, 0:T], bank[4 + t % 2][:, 0:T], c2v("sin"), ALU.mult).then_inc(S("rot_freed"), 1)
                    V.tensor_tensor(z, z, c2v("cos"), ALU.mult).then_inc(S("dve_chain"), 1)
                    dve.wait_ge(S("rot_freed"), me.nth("rot_freed"))
                    dve.wait_ge(S("dve_chain"), me.nth("dve_chain"))
                    V.tensor_tensor(z, z, AM[:, 0:T], ALU.add).then_inc(S("rope_done"), 1)
                    dve.wait_ge(S("rope_done"), me.nth("rope_done"))

                def short_conv(k):
                    a, x = ZB[:, Z2["scc"] + k, 0:n], ZB[:, Z2["scx"] + k, 0:n]
                    V.tensor_tensor(a, a, x, ALU.mult).then_inc(S("dve_chain"), 1)
                    dve.wait_ge(S("dve_chain"), me.nth("dve_chain"))
                    w = [prm_col(f"scw{l}", 2 * tap + k) for tap in range(3)]
                    V.tensor_scalar(x, a, w[1], prm_col(f"scbias{l}", k), ALU.mult, ALU.add).then_inc(S("dve_chain"), 1)
                    dve.wait_ge(S("dve_chain"), me.nth("dve_chain"))
                    a, y = seq(a, n), seq(x, n)
                    V.scalar_tensor_tensor(y[:, :, 1:], a[:, :, :-1], w[0], y[:, :, 1:], ALU.mult, ALU.add).then_inc(S("dve_chain"), 1)
                    dve.wait_ge(S("dve_chain"), me.nth("dve_chain"))
                    V.scalar_tensor_tensor(y[:, :, :-1], a[:, :, 1:], w[2], y[:, :, :-1], ALU.mult, ALU.add).then_inc(S("dve_chain"), 1)
                    dve.wait_ge(S("dve_chain"), me.nth("dve_chain"))
                    V.tensor_tensor(x, x, ZB[:, Z2["scb"] + k, 0:n], ALU.mult).then_inc(S("sc_ready"), 1)

                def middles(d):
                    dve.wait_ge(S("b_copied"), me.nth("b_copied"))
                    b = BC[:, d, :]
                    for c in range(NCH):
                        r = slice(CH * c, CH * (c + 1))
                        V.tensor_copy(BM[r, d, 0:4], BC[r, d, :].rearrange("p (i t) -> p i t", t=P)[
                            :, :, CH * c + CH // 2 - 1 + d])
                    e = TC - 1 if d == 0 else T
                    V.tensor_copy(BM[:, d, 4:5], b[:, e:e + 1]).then_inc(S("bm_ready"), 1)
                    dve.wait_ge(S("bm_ready"), me.nth("bm_ready"))
                    V.tensor_tensor(AM[:].rearrange("p (i t) -> p i t", t=P),
                                    b.rearrange("p (i t) -> p i t", t=P),
                                    bl(BM[:, d, 0:4], P), ALU.subtract).then_inc(S("dve_chain"), 1)
                    dve.wait_ge(S("dve_chain"), me.nth("dve_chain"))

                def exponents(d):
                    am = AM[:].rearrange("p (i t) -> p i t", t=P)
                    cap = c2v("capkf") if d == 0 else c2v("capkb")
                    ex = exps(d)
                    V.tensor_tensor(ex[:, 0:512].rearrange("p (i t) -> p i t", t=P), am, bc(c2v("capq"), 4), ALU.min)
                    V.scalar_tensor_tensor(ex[:, 512:1024].rearrange("p (i t) -> p i t", t=P), am, -1.0,
                                           bc(cap, 4), ALU.mult, ALU.min)
                    V.tensor_tensor(ex[:, 1024:].rearrange("p (s t) -> p s t", t=P),
                                    bl(BM[:, d, 1 - d:4:2], P),
                                    BC[:, d, :].rearrange("p (s i t) -> p s i t", i=2, t=P)[:, :, d, :],
                                    ALU.subtract).then_inc(S("ex_ready"), 1)
                    dve.wait_ge(S("ex_ready"), me.nth("ex_ready"))

                def decay(d):
                    V.tensor_tensor(EY[:, d, 0:512], EY[:, d, 0:512], KQ[:, 1, :], ALU.mult)
                    V.tensor_tensor(EY[:, d, 512:1024], EY[:, d, 512:1024], KQ[:, 0, :], ALU.mult)
                    dve.wait_ge(S("e0_ready"), me.nth("e0_ready"))
                    if d == 1:
                        V.tensor_tensor(E0[:, 0:T], E0[:, 0:T], KQ[0:64, 1, 0:T], ALU.mult)
                        V.tensor_tensor(E0[:, T:], E0[:, T:], KQ[0:64, 0, T:], ALU.mult)
                    ey = EY[:, d, 1024:].rearrange("p (s t) -> p s t", t=P)
                    V.tensor_tensor(ey, ey, KQ[:, 0, :].rearrange("p (s i t) -> p s i t", i=2, t=P)[:, :, d, :],
                                    ALU.mult).then_inc(S("dec_ready"), 1)

                def output(k):
                    z = ZB[:, Z2["r"] + k, 0:n]
                    dve.wait_ge(S("osq_ready"), me.nth("osq_ready"))
                    V.scalar_tensor_tensor(z, bank[6 + k % 2][:, 0:n], prm_col(f"glag{l}"), z,
                                           ALU.mult, ALU.mult).then_inc(S("og_read"), 1)
                    dve.wait_ge(S("og_read"), me.nth("og_read"))

                def output_eps():
                    dve.wait_ge(S("oms_ready"), me.nth("oms_ready"))
                    V.tensor_scalar(OM[:, 1, 0:n], bank[5][:, 0:n], EPS, None, ALU.add).then_inc(S("oms_eps"), 1)

                def output_norm(k):
                    z = ZB[:, Z2["r"] + k, 0:n]
                    rsqrt(OM[:, 1, 0:n], OM[:, 2, 0:n], AM[:, 0:n], OM[:, 2, 0:n])
                    V.tensor_tensor(z, z, OM[:, 2, 0:n], ALU.mult).then_inc(S("yo_ready"), 1)
                    dve.wait_ge(S("yo_ready"), me.nth("yo_ready"))

                def output_lo(k):
                    dve.wait_ge(S("xh_ready"), me.nth("xh_ready"))
                    V.tensor_tensor(NLO[:, k, 0:n], ZB[:, Z2["r"] + k, 0:n], NHI[:, k, 0:n].bitcast(F32),
                                    ALU.subtract).then_inc(S("y_split"), 1)

                for i in range(NZ2):
                    rest()
                    if i == 5:
                        dve.wait_ge(S("ld_c2"), 16 * 2 * (l + 1))
                        dve.wait_ge(S("z_freed"), me.nth("z_freed", 4))
                    if i in (5, 6, 7):
                        rope(i - 5)
                    if i == 11:
                        for k in range(4):
                            dve.wait_ge(S("gln_ready"), me.nth("gln_ready"))
                            V.scalar_tensor_tensor(gate_part(GT, k), bank[(6, 7, 4, 5)[k]][:, 0:VW].rearrange("p (t k) -> p t k", t=2),
                                                   0.0, gate_part(GTA, k), ALU.min, ALU.subtract).then_inc(S("g_ready"), 1)
                    if i == 12:
                        dve.wait_ge(S("z_freed"), me.nth("z_freed", 6))
                    if i in (12, 13):
                        short_conv(i - 12)
                    if i in (16, 17):
                        middles(i - 16)
                        exponents(i - 16)
                me.tile += NZ2
                dve.wait_ge(S("z_freed"), me.nth("z_freed", NZ2 - 10))
                dve.wait_ge(S("rsilu_ready"), me.nth("rsilu_ready"))
                if uc:
                    plain(ROW_U)
                for h in range(GH):
                    if h % 2 == 0 and h > 0:
                        output(h // 2 - 1)
                    if h % 2 == 1 and h > 1:
                        output_eps()
                    dve.wait_ge(S("kq_freed"), me.nth("kq_freed", 2))
                    dve.wait_ge(S("ey_ready"), me.nth("ey_ready"))
                    decay(0)
                    dve.wait_ge(S("ey_ready"), me.nth("ey_ready"))
                    decay(1)
                    if uc and h == 0:
                        modulation(5)
                    if h < GH - 1:
                        middles(0)
                        exponents(0)
                    if h > 0:
                        dve.wait_ge(S("gpv_done"), me.nth("gpv_done"))
                    for q in range(2 if uc else 1):
                        dve.wait_ge(S("a_ready"), me.nth("a_ready"))
                        V.tensor_tensor(AM[:], bank[4 + q][:], c2v("mask"), ALU.mult).then_inc(S("am_read"), 1)
                        dve.wait_ge(S("am_read"), me.nth("am_read"))
                        o = AF[:, q, :, :].rearrange("p a (b t) -> p (a b) t", t=P)[:, 0:4:3, :]
                        V.tensor_tensor(o, AM[:, 0:T].rearrange("p (a t) -> p a t", t=P),
                                        AM[:, T:].rearrange("p (a t) -> p a t", t=P), ALU.add).then_inc(S("af_ready"), 1)
                        dve.wait_ge(S("af_ready"), me.nth("af_ready"))
                    if h < GH - 1:
                        middles(1)
                        exponents(1)
                    if uc:
                        plain(ROW_U)
                        modulation(6 + (h // 2 + 1) % 2)
                    if h % 2 == 1 and h > 1:
                        output_norm(h // 2 - 1)
                    if h % 2 == 0 and h > 2:
                        output_lo(h // 2 - 2)
                dve.wait_ge(S("gpv_done"), me.nth("gpv_done"))
                output(GH // 2 - 1)
                output_lo(GH // 2 - 2)

                def end_of_gated(i):
                    if i == 1:
                        output_eps()
                    if i == 3:
                        for k in range(2):
                            dve.wait_ge(S("xh_ready"), me.nth("xh_ready"))
                            V.tensor_tensor(NLO[:, 3 + k, 0:n], ZB[:, Z2["scx"] + k, 0:n], NHI[:, 3 + k, 0:n].bitcast(F32),
                                            ALU.subtract).then_inc(S("y_split"), 1)
                    if i == 4:
                        output_norm(GH // 2 - 1)
                    if i == 6:
                        output_lo(GH // 2 - 1)

                V.memset(NB[:, :, :, T:], 0.0).then_inc(S("dve_chain"), 1)
                dve.wait_ge(S("dve_chain"), me.nth("dve_chain"))
                half_loads = [0, 0]

                def bias2(it):
                    h, qt, nk, own = it
                    if own:
                        return None
                    if qt == 0:
                        half_loads[h % 2] += 1
                        dve.wait_ge(S(f"ld_nb{h % 2}"), 16 * (NAH // 2 * l + half_loads[h % 2]))
                    return NB[:, h % 2, qt, :]

                if l == 0:
                    me.seen["s_freed"] = len(ITEMS1) * DEPTH
                softmax(items2(uc), bias2, L2, P2, ST2, 1.0, end_of_gated)
                for k in range(3):
                    dve.wait_ge(S("xh_ready"), me.nth("xh_ready"))
                    V.tensor_tensor(NLO[:, 5 + k, 0:n], OY[:, k, 0:n], NHI[:, 5 + k, 0:n].bitcast(F32),
                                    ALU.subtract).then_inc(S("y_split"), 1)
                ahead()
                residual(l, n, G1, 1)
                dve.wait_ge(S("wo_freed"), me.nth("wo_freed", KS))
                stats(n, MS2)
                if uc:
                    plain(2 * ROW_U)
                modulate(l, n, f"nffn{l}", SH2, SC2)
                if uc:
                    modulation(5)
                for p in range(FT + 2):
                    if uc and p == 2:
                        modulation(6)
                    if p < FT:
                        for w in range(2):
                            unit()
                            dve.wait_ge(S("centre_ready"), me.nth("centre_ready"))
                            b = seq(bank[me.next_tile()][:, 0:n], n)
                            y = seq(CF[:, w, p % 3, 0:n], n)
                            j = w * FT + p
                            V.scalar_tensor_tensor(y[:, :, 1:], b[:, :, :-1], prm_col(f"fw{l}", j),
                                                   y[:, :, 1:], ALU.mult, ALU.add).then_inc(S("dve_chain"), 1)
                            dve.wait_ge(S("dve_chain"), me.nth("dve_chain"))
                            V.scalar_tensor_tensor(y[:, :, :-1], b[:, :, 1:], prm_col(f"fw{l}", 4 * FT + j),
                                                   y[:, :, :-1], ALU.mult, ALU.add).then_inc(S("up_freed"), 1)
                    if 1 <= p < FT + 1:
                        k = (p - 1) % 3
                        dve.wait_ge(S("fsilu_ready"), me.nth("fsilu_ready"))
                        V.tensor_tensor(CF[:, 1, k, 0:n], CF[:, 1, k, 0:n], CF[:, 0, k, 0:n], ALU.mult).then_inc(S("hid_ready"), 1)
                    if p >= 2:
                        dve.wait_ge(S("hh_ready"), me.nth("hh_ready"))
                        V.tensor_tensor(HLO[:, p - 2, 0:n], CF[:, 1, (p - 2) % 3, 0:n],
                                        HHI[:, p - 2, 0:n].bitcast(F32), ALU.subtract).then_inc(S("hid_split"), 1)
                dve.wait_ge(S("up_freed"), me.nth("up_freed", 2 * FT))
                dve.wait_ge(S("hid_ready"), me.nth("hid_ready", FT))
                residual(l, n, G2, 3)
                dve.wait_ge(S("wo_freed"), me.nth("wo_freed", KS))
            stats(T, MS2)
            for s in range(KS):
                V.scalar_tensor_tensor(X[:, s, 0:T], X[:, s, 0:T], prm_col("fin2", s), MS2[:, 3, 0:T],
                                       ALU.mult, ALU.mult).then_inc(S("x_new"), 1)


def fm_units(w, cols):
    cols = np.asarray(cols)
    t = np.zeros((w.shape[0], P), np.float32)
    ok = cols >= 0
    t[:, :len(cols)][:, ok] = w[:, cols[ok]]
    t = t.reshape(-1, P, P).transpose(1, 0, 2)
    return [t[:, s:s + 8].reshape(P, -1) for s in range(0, t.shape[1], 8)]


def tm_units(w):
    t = w.reshape(KS, P, -1).transpose(1, 0, 2)
    return [t[:, s:s + 2].reshape(P, -1) for s in range(0, KS, 2)]


def columns1():
    o = np.cumsum([0, 256, 256, 256, 256, 256, 512, 512, 512, 512, 256, 64, 4])
    val, glu, cg, pin, pg, q, k, v, ag, qi, ki, wi = o[:12]
    base = {"q": q, "k": k, "qi": qi, "val": val, "glu": glu, "cgate": cg, "pin": pin, "pgate": pg, "agate": ag}
    out = []
    for t, name in enumerate(TILES1):
        if name == "ki":
            out.append(np.concatenate([ki + np.arange(64)] * 2))
        elif name == "wi":
            out.append(np.concatenate([wi + np.arange(4), np.full(124, -1)]))
        else:
            out.append(base[name] + (t - Z1[name]) * P + np.arange(P))
    return out, v


def columns2():
    o = np.cumsum([0, 192, 192, 384, 16, 16, 384, 256, 256, 256, 384, 384, 384])
    q, k, v, lf, lb, r, sb_, sc_, sx, nq, nk, nv = o[:12]
    base = {"nk": nk, "nq": nq, "r": r, "scb": sb_, "scc": sc_, "scx": sx}
    pad = np.full(16, -1)
    out = []
    for t, name in enumerate(TILES2):
        if name == "gqa":
            out.append(q + np.arange(P))
        elif name == "gka":
            out.append(k + np.arange(P))
        elif name == "gqk":
            out.append(np.concatenate([q + P + np.arange(64), k + P + np.arange(64)]))
        elif name == "glr":
            out.append(np.concatenate([lf + np.arange(16), pad, lb + np.arange(16), np.full(80, -1)]))
        else:
            out.append(base[name] + (t - Z2[name]) * P + np.arange(P))
    return out, v, nv


def constants():
    f = np.float32
    cc, c1, c2 = np.zeros((P, NCC), f), np.zeros((P, NC1), f), np.zeros((P, NC2), f)

    def put(arr, table, name, value):
        a, n = table[name]
        arr[:, a:a + n] = value

    i = np.arange(P)
    put(cc, CC, "ident", np.eye(P))
    put(cc, CC, "ones", 1.0 / D)
    put(cc, CC, "ones256", 1.0 / CONV_W)
    put(cc, CC, "blk", (i[:, None] // 64 == i[None, :] // 64) / 64.0)
    put(cc, CC, "glrone", ((i == 16) | (i == 48))[:, None])

    perm = np.zeros((P, P))
    for d in range(P):
        if d % 64 < 32:
            perm[d + 32, d] = -1.0
        else:
            perm[d - 32, d] = 1.0
    put(c1, C1, "perm", perm)
    t = np.arange(T)
    inv = (f(10000.0) ** (-np.arange(32, dtype=f) / f(32))).astype(f)
    ang = (inv[i % 32][:, None] * t.astype(f)[None, :]).astype(f)
    put(c1, C1, "cos", np.cos(ang))
    put(c1, C1, "sin", np.sin(ang))
    put(c1, C1, "causal", np.concatenate([np.where(t[None, :] <= qt * P + i[:, None], 0.0, -1.0e30) for qt in range(TT)], 1))
    put(c1, C1, "icnt", np.concatenate([1.0 / np.minimum(t[None, :] + 1, np.array(POOL_WINDOWS)[2 * m + i // 64][:, None])
                                        for m in range(2)], 1))

    perm = np.zeros((P, P))
    perm[i[1::2], i[0::2]] = -1.0
    perm[i[0::2], i[1::2]] = 1.0
    put(c2, C2, "perm", perm)
    inv = (f(10000.0) ** (-np.arange(8, dtype=f) / f(8))).astype(f)
    ang = np.concatenate([(t // 64).astype(f)[:, None] * inv, (t % 64).astype(f)[:, None] * inv], 1).astype(f)
    ang = ang.T[(i % 32) // 2]
    put(c2, C2, "cos", np.cos(ang))
    put(c2, C2, "sin", np.sin(ang))
    put(c2, C2, "rep", i[:, None] % 32 == i[None, :] % 32)
    tri = (i[:, None] <= i[None, :]) / 16.0
    put(c2, C2, "uf", np.concatenate([tri, np.full((P, P), 1 / 16.0)], 1))
    put(c2, C2, "ub", np.concatenate([np.full((P, P), 1 / 16.0), tri.T], 1))
    c = i[:, None] // CH
    put(c2, C2, "capkf", np.where(i[None, :] < CH * (c + 1), CAP, -200.0))
    put(c2, C2, "capkb", np.where(i[None, :] >= CH * c, CAP, -200.0))
    put(c2, C2, "capq", np.where(i[None, :] // CH == c, CAP, -200.0))
    mf = (i[:, None] <= i[None, :]) * 1.0
    put(c2, C2, "mask", np.concatenate([mf, mf, mf.T, mf.T], 1))
    return cc, c1, c2


def bias_index():
    t = np.arange(T)
    r, c = t // 64, t % 64
    start = np.clip(c - 8, 0, 64 - 16)
    inside = (c[None, :] >= start[:, None]) & (c[None, :] < start[:, None] + 16)
    dr = r[None, :] - r[:, None] + 7
    dc = np.clip(c[None, :] - c[:, None] + 15, 0, 30)
    return dr, dc, inside


def kernel(**inp):
    import concourse.bacc as bacc
    from concourse.bass_utils import run_bass_kernel_spmd

    a = {k: np.ascontiguousarray(v) for k, v in inp.items()}
    f = np.float32
    ws = np.zeros((NU, P, UNIT), f)
    at = 0

    def put(units):
        nonlocal at
        for u in units:
            assert u.shape[1] == WIDTHS[at]
            ws[at, :, 0:u.shape[1]] = u
            at += 1

    def tiles(w, n=None):
        for m in range((w.shape[1] if n is None else n) // P):
            put(fm_units(w, m * P + np.arange(P)))

    taken = 0

    def rows(n):
        nonlocal taken
        for _ in range(n):
            l, c = taken // ROW_TILES, taken % ROW_TILES * 512
            put(tm_units(a["w_ada_2"][l][:, c:c + 512]))
            taken += 1

    cols, v = columns1()
    for l in range(DEPTH):
        w = a["w_in"][l]
        rows(2)
        put(tm_units(w[:, v:v + 512]))
        for c in cols:
            put(fm_units(w, c))
        rows(3)
        tiles(a["w_out"][l])
        pw = a["ple_w"][l].reshape(2, P, KS, P).transpose(1, 2, 0, 3)
        put([pw[:, 4 * u:4 * u + 4].reshape(P, -1) for u in range(2)])
        rows(1)
        tiles(a["ple_gate_w"][l])
    rows(1)
    cols2, v, nv = columns2()
    for l in range(DEPTH):
        w = a["w_in_2"][l]
        rows(2 if l == 0 else 0)
        put(tm_units(w[:, v:v + VW]))
        put(tm_units(w[:, nv:nv + VW]))
        for c in cols2:
            put(fm_units(w, c))
        rows(1 + GH if l == 0 else 0)
        tiles(a["w_out_2"][l])
        rows(2 if l == 0 else 0)
        for m in range(FT):
            for o in (0, FFN):
                put(fm_units(a["ffn_w_up_2"][l], o + m * P + np.arange(P)))
        tiles(a["ffn_w_down_2"][l])
    assert at == NU

    prm = np.zeros((P, NPC), f)

    def par(name, vec):
        vec = vec.reshape(-1, P).T
        prm[:, PC[name]:PC[name] + vec.shape[1]] = vec

    for l in range(DEPTH):
        par(f"norm{l}", a["norm_g"][l])
        b = a["b_in"][l]
        par(f"bin{l}", np.concatenate([np.where(c >= 0, b[c], f(0)) for c in cols]))
        prm[:, PC[f"dww{l}"]:PC[f"dww{l}"] + 62] = a["conv_dw_w"][l].reshape(CONV_K, 2, P).transpose(2, 1, 0).reshape(P, 62)
        for name, src in (("dwb", "conv_dw_b"), ("lng", "conv_ln_g"), ("lnb", "conv_ln_b"), ("pwb", "conv_pw_b"),
                          ("poolb", "pool_b"), ("pools", "pool_scale"), ("nmix", "norm_mix_g_2"), ("nffn", "norm_ffn_g_2"),
                          ("bada", "b_ada_2"), ("scbias", "sc_conv_b_2"), ("fb", "ffn_conv_b_2"), ("scw", "sc_conv_w_2"),
                          ("fw", "ffn_conv_w_2")):
            par(f"{name}{l}", a[src][l])
        par(f"glag{l}", np.concatenate([a["gla_norm_g_2"][l]] * 2))
    par("fin1", a["final_norm_g"])
    par("fin2", a["final_norm_g_2"])
    cv = np.stack([a["c_2"][0], a["c_ctx_2"]], 1)
    prm[:, PC["cvec"]:] = cv.reshape(KS, P, 2).transpose(1, 0, 2).reshape(P, 2 * KS)

    mat1 = np.zeros((DEPTH, P, 768), f)
    mat1[:, :, 0:512] = a["conv_pw_w"].reshape(DEPTH, 2, P, 256).transpose(0, 2, 1, 3).reshape(DEPTH, P, 512)
    for g in range(4):
        r, o = 64 * (g % 2), 512 + P * (g // 2) + 64 * (g % 2)
        mat1[:, r:r + 64, o:o + 64] = a["pool_w"][:, g]
    wgp = np.zeros((DEPTH, 64, 192), f)
    wgp[:, 0:16], wgp[:, 16] = a["gla_wg2_fw_2"], a["gla_bg_fw_2"]
    wgp[:, 32:48], wgp[:, 48] = a["gla_wg2_bw_2"], a["gla_bg_bw_2"]
    dr, dc, inside = bias_index()
    nab = np.where(inside, a["na_rpb_2"][:, :, dr, dc], f(-1.0e30)).astype(f)
    nab = np.ascontiguousarray(nab.reshape(DEPTH, NAH, TT, P, T).transpose(0, 1, 3, 2, 4))

    def slabs(x):
        return x.T.reshape(-1, P, x.shape[0]).transpose(1, 0, 2)

    xt = np.ascontiguousarray(np.concatenate([slabs(a["x"][0]), slabs(a["ctx_2"][0])], 2))
    ptin = np.ascontiguousarray(np.stack([slabs(a["p"][l, 0]) for l in range(DEPTH)]))
    bv1 = np.ascontiguousarray(a["b_in"][:, columns1()[1]:columns1()[1] + 512])
    cc, c1, c2 = constants()

    nc = bacc.Bacc("TRN2", target_bir_lowering=False, num_devices=1)
    arrays = dict(ws=ws, prm=prm, cc=cc, c1=c1, c2=c2, xt=xt, ptin=ptin, mat1=mat1, bv1=bv1, wgp=wgp, nab=nab)
    aps = {k: nc.dram_tensor(f"in_{k}", v.shape, F32, kind="ExternalInput").ap() for k, v in arrays.items()}
    out = nc.dram_tensor("out_x", (P, KS, T), F32, kind="ExternalOutput").ap()
    build(nc, out=out, **aps)
    r = run_bass_kernel_spmd(nc, [{f"in_{k}": v for k, v in arrays.items()}], core_ids=[0])
    y = r.results[0]["out_x"]
    return np.ascontiguousarray(y.transpose(2, 1, 0).reshape(1, T, D))
```
